# Optimizing a Trainium2 kernel written in Bass

```python
import jax, jax.numpy as jnp
from jax import lax
import numpy as np

D_MODEL = 1024
BATCH = 1
SEQ = 512
DEPTH = 2

N_MIXERS = 2
N_MLA_LAYERS = (DEPTH + N_MIXERS - 1) // N_MIXERS
N_RWKV_LAYERS = DEPTH // N_MIXERS
NORM_EPS = 1e-6

MLA_HEADS = 8
QK_NOPE_DIM = 128
QK_ROPE_DIM = 64
QK_DIM = QK_NOPE_DIM + QK_ROPE_DIM
V_HEAD_DIM = 128
Q_LORA_RANK = 384
KV_LORA_RANK = 256
MLA_IN_DIM = Q_LORA_RANK + KV_LORA_RANK + QK_ROPE_DIM
ROPE_THETA = 10000.0
Q_BLOCK = 128

RWKV_HEAD = 64
RWKV_HEADS = D_MODEL // RWKV_HEAD
DECAY_LORA = 64
AAA_LORA = 64
MV_LORA = 32
GATE_LORA = 160
GN_EPS = 64e-5

D_FF = 2816
CONV_WIDTH = 3

kernel_name = "hybrid_mla_rwkv7_convglu"

def _rms_norm(x, g):
    xf = x.astype(jnp.float32)
    y = xf * lax.rsqrt(jnp.mean(xf * xf, axis=-1, keepdims=True) + NORM_EPS)
    return (y * g.astype(jnp.float32)).astype(x.dtype)

def _rope(t, positions):
    half = QK_ROPE_DIM // 2
    inv_freq = ROPE_THETA ** (-jnp.arange(half, dtype=jnp.float32) / half)
    ang = positions.astype(jnp.float32)[..., None] * inv_freq
    ang = ang.reshape(ang.shape[:2] + (1,) * (t.ndim - 3) + (half,))
    cos, sin = jnp.cos(ang), jnp.sin(ang)
    tf = t.astype(jnp.float32)
    t1, t2 = tf[..., :half], tf[..., half:]
    return jnp.concatenate([t1 * cos - t2 * sin, t2 * cos + t1 * sin], axis=-1).astype(t.dtype)

def _mla(h, positions, w_in, q_norm, w_uq, kv_norm, w_ukv, w_o):
    B, S, _ = h.shape
    lat = h @ w_in
    q_lat = lat[..., :Q_LORA_RANK]
    c_kv = lat[..., Q_LORA_RANK:Q_LORA_RANK + KV_LORA_RANK]
    k_rope = _rope(lat[..., Q_LORA_RANK + KV_LORA_RANK:], positions)
    q = (_rms_norm(q_lat, q_norm) @ w_uq).reshape(B, S, MLA_HEADS, QK_DIM)
    q_nope = q[..., :QK_NOPE_DIM]
    q_rope = _rope(q[..., QK_NOPE_DIM:], positions)
    kv = (_rms_norm(c_kv, kv_norm) @ w_ukv).reshape(B, S, MLA_HEADS, QK_NOPE_DIM + V_HEAD_DIM)
    k_nope = kv[..., :QK_NOPE_DIM]
    v = kv[..., QK_NOPE_DIM:]
    scale = QK_DIM ** -0.5
    n_blk = S // Q_BLOCK
    key_pos = jnp.arange(S)

    def to_blocks(t):
        return t.reshape((B, n_blk, Q_BLOCK) + t.shape[2:]).swapaxes(0, 1)

    def attend(args):
        qn, qr, blk = args
        s = (jnp.einsum('bqhd,bkhd->bhqk', qn, k_nope)
             + jnp.einsum('bqhr,bkr->bhqk', qr, k_rope)).astype(jnp.float32) * scale
        q_pos = blk * Q_BLOCK + jnp.arange(Q_BLOCK)
        causal = key_pos[None, :] <= q_pos[:, None]
        s = jnp.where(causal, s, jnp.finfo(jnp.float32).min)
        p = jax.nn.softmax(s, axis=-1).astype(v.dtype)
        return jnp.einsum('bhqk,bkhd->bqhd', p, v)

    o = lax.map(attend, (to_blocks(q_nope), to_blocks(q_rope), jnp.arange(n_blk)))
    o = o.swapaxes(0, 1).reshape(B, S, MLA_HEADS * V_HEAD_DIM)
    return o @ w_o

def _token_shift(x):
    return jnp.pad(x, ((0, 0), (1, 0), (0, 0)))[:, :-1]

def _wkv7_scan(r, w, k, v, a, b):
    B, S, H, N = r.shape

    def step(state, inp):
        r_t, w_t, k_t, v_t, a_t, b_t = inp
        sa = jnp.einsum('bhij,bhj->bhi', state, a_t)
        state = (state * w_t[:, :, None, :] + sa[..., None] * b_t[:, :, None, :]
                 + v_t[..., None] * k_t[:, :, None, :])
        return state, jnp.einsum('bhij,bhj->bhi', state, r_t)

    xs = tuple(jnp.moveaxis(t, 1, 0) for t in (r, w, k, v, a, b))
    _, y = lax.scan(step, jnp.zeros((B, H, N, N), jnp.float32), xs)
    return jnp.moveaxis(y, 0, 1)

def _rwkv7(h, v_first, v_lora, mix, w_rkv, w0, w1, w2, a0, a1, a2, g1, g2,
           k_k, k_a, r_k, ln_w, ln_b, w_o):
    B, S, D = h.shape
    H, N = RWKV_HEADS, RWKV_HEAD
    xx = _token_shift(h) - h
    xm = h[None] + xx[None] * mix[:, None, None, :]
    rkv = jnp.einsum('nbsd,nde->nbse', xm[:3], w_rkv)
    r, k, v = rkv[0], rkv[1], rkv[2]
    xw, xa, xg = xm[3], xm[4], xm[5]
    log_w = -jax.nn.softplus(-(w0 + jnp.tanh(xw @ w1) @ w2)) - 0.5
    decay = jnp.exp(-jnp.exp(log_w.astype(jnp.float32)))
    a = jax.nn.sigmoid(a0 + (xa @ a1) @ a2)
    g = jax.nn.sigmoid(xg @ g1) @ g2
    if v_lora is None:
        v_first = v
    else:
        v0, v1, v2 = v_lora
        v = v + (v_first - v) * jax.nn.sigmoid(v0 + (xv_lora_in := xm[2]) @ v1 @ v2)
    kk = (k * k_k).astype(jnp.float32).reshape(B, S, H, N)
    kk = kk / jnp.maximum(jnp.sqrt(jnp.sum(kk * kk, axis=-1, keepdims=True)), 1e-12)
    k = k * (1 + (a - 1) * k_a)
    heads = lambda t: t.astype(jnp.float32).reshape(B, S, H, N)
    rf, kf, vf, af = heads(r), heads(k), heads(v), heads(a)
    y = _wkv7_scan(rf, heads(decay), kf, vf, -kk, kk * af)
    mu = jnp.mean(y, axis=-1, keepdims=True)
    var = jnp.mean(jnp.square(y - mu), axis=-1, keepdims=True)
    yn = ((y - mu) * lax.rsqrt(var + GN_EPS)).reshape(B, S, D) * ln_w.astype(jnp.float32) + ln_b.astype(jnp.float32)
    bonus = (jnp.sum(rf * kf * r_k.astype(jnp.float32), axis=-1, keepdims=True) * vf).reshape(B, S, D)
    out = ((yn + bonus).astype(h.dtype) * g) @ w_o
    return out, v_first

def _conv_glu(h, w_in, conv_w, conv_b, w_out):
    hu = h @ w_in
    gate, up = hu[..., :D_FF], hu[..., D_FF:]
    gate = lax.conv_general_dilated(
        gate, conv_w[:, None, :], window_strides=(1,), padding=[(CONV_WIDTH - 1, 0)],
        dimension_numbers=('NWC', 'WIO', 'NWC'), feature_group_count=D_FF) + conv_b
    return (jax.nn.silu(gate) * up) @ w_out

def setup_inputs(seed: int = 0) -> dict:
    key = jax.random.key(seed)
    ks = iter(jax.random.split(key, 48))
    nrm = lambda shape, scale: jax.random.normal(next(ks), shape, jnp.float32) * scale
    uni = lambda shape, lo, hi: jax.random.uniform(next(ks), shape, jnp.float32, lo, hi)
    Lm, Lr, D = N_MLA_LAYERS, N_RWKV_LAYERS, D_MODEL
    return {
        "x": nrm((BATCH, SEQ, D), 1.0),
        "positions": jnp.broadcast_to(jnp.arange(SEQ, dtype=jnp.int32), (BATCH, SEQ)),
        "norm_mix": 1.0 + nrm((DEPTH, D), 0.05),
        "norm_ffn": 1.0 + nrm((DEPTH, D), 0.05),
        "norm_final": 1.0 + nrm((D,), 0.05),
        "mla_w_in": nrm((Lm, D, MLA_IN_DIM), D ** -0.5),
        "mla_q_norm": 1.0 + nrm((Lm, Q_LORA_RANK), 0.05),
        "mla_w_uq": nrm((Lm, Q_LORA_RANK, MLA_HEADS * QK_DIM), Q_LORA_RANK ** -0.5),
        "mla_kv_norm": 1.0 + nrm((Lm, KV_LORA_RANK), 0.05),
        "mla_w_ukv": nrm((Lm, KV_LORA_RANK, MLA_HEADS * (QK_NOPE_DIM + V_HEAD_DIM)), KV_LORA_RANK ** -0.5),
        "mla_w_o": nrm((Lm, MLA_HEADS * V_HEAD_DIM, D), (MLA_HEADS * V_HEAD_DIM) ** -0.5),
        "rwkv_mix": uni((Lr, 6, D), 0.0, 1.0),
        "rwkv_w_rkv": nrm((Lr, 3, D, D), D ** -0.5),
        "rwkv_w0": uni((Lr, D), -5.0, -0.5),
        "rwkv_w1": nrm((Lr, D, DECAY_LORA), D ** -0.5),
        "rwkv_w2": nrm((Lr, DECAY_LORA, D), 0.1 * DECAY_LORA ** -0.5),
        "rwkv_a0": nrm((Lr, D), 0.1),
        "rwkv_a1": nrm((Lr, D, AAA_LORA), D ** -0.5),
        "rwkv_a2": nrm((Lr, AAA_LORA, D), 0.1 * AAA_LORA ** -0.5),
        "rwkv_v0": 1.0 + nrm((Lr - 1, D), 0.1),
        "rwkv_v1": nrm((Lr - 1, D, MV_LORA), D ** -0.5),
        "rwkv_v2": nrm((Lr - 1, MV_LORA, D), 0.1 * MV_LORA ** -0.5),
        "rwkv_g1": nrm((Lr, D, GATE_LORA), D ** -0.5),
        "rwkv_g2": nrm((Lr, GATE_LORA, D), GATE_LORA ** -0.5),
        "rwkv_k_k": 0.85 + nrm((Lr, D), 0.05),
        "rwkv_k_a": 1.0 + nrm((Lr, D), 0.05),
        "rwkv_r_k": nrm((Lr, RWKV_HEADS, RWKV_HEAD), 0.1),
        "rwkv_ln_w": 1.0 + nrm((Lr, D), 0.05),
        "rwkv_ln_b": nrm((Lr, D), 0.01),
        "rwkv_w_o": nrm((Lr, D, D), D ** -0.5),
        "ffn_w_in": nrm((DEPTH, D, 2 * D_FF), D ** -0.5),
        "ffn_conv_w": nrm((DEPTH, CONV_WIDTH, D_FF), CONV_WIDTH ** -0.5),
        "ffn_conv_b": nrm((DEPTH, D_FF), 0.01),
        "ffn_w_out": nrm((DEPTH, D_FF, D), D_FF ** -0.5),
    }

def reference(x, positions, norm_mix, norm_ffn, norm_final,
              mla_w_in, mla_q_norm, mla_w_uq, mla_kv_norm, mla_w_ukv, mla_w_o,
              rwkv_mix, rwkv_w_rkv, rwkv_w0, rwkv_w1, rwkv_w2, rwkv_a0, rwkv_a1, rwkv_a2,
              rwkv_v0, rwkv_v1, rwkv_v2, rwkv_g1, rwkv_g2, rwkv_k_k, rwkv_k_a, rwkv_r_k,
              rwkv_ln_w, rwkv_ln_b, rwkv_w_o,
              ffn_w_in, ffn_conv_w, ffn_conv_b, ffn_w_out):
    v_first = None
    for i in range(DEPTH):
        h = _rms_norm(x, norm_mix[i])
        j = i // N_MIXERS
        if i % N_MIXERS == 0:
            y = _mla(h, positions, mla_w_in[j], mla_q_norm[j], mla_w_uq[j],
                     mla_kv_norm[j], mla_w_ukv[j], mla_w_o[j])
        else:
            v_lora = None if j == 0 else (rwkv_v0[j - 1], rwkv_v1[j - 1], rwkv_v2[j - 1])
            y, v_first = _rwkv7(h, v_first, v_lora, rwkv_mix[j], rwkv_w_rkv[j],
                                rwkv_w0[j], rwkv_w1[j], rwkv_w2[j],
                                rwkv_a0[j], rwkv_a1[j], rwkv_a2[j],
                                rwkv_g1[j], rwkv_g2[j], rwkv_k_k[j], rwkv_k_a[j], rwkv_r_k[j],
                                rwkv_ln_w[j], rwkv_ln_b[j], rwkv_w_o[j])
        x = x + y
        x = x + _conv_glu(_rms_norm(x, norm_ffn[i]), ffn_w_in[i], ffn_conv_w[i],
                          ffn_conv_b[i], ffn_w_out[i])
    return _rms_norm(x, norm_final)


_drawn_inputs = setup_inputs


def setup_inputs(seed=0):
    import zlib

    import numpy as np

    out = dict(_drawn_inputs(seed))
    spreads = {}
    factors = {'mla_q_norm': 4.93,
     'mla_kv_norm': 3.482,
     'rwkv_w1': 31.785,
     'rwkv_w2': 31.579,
     'rwkv_a0': 9.088,
     'rwkv_a1': 3.048,
     'rwkv_a2': 3.067,
     'rwkv_k_k': 28.624,
     'rwkv_ln_b': 38.551,
     'ffn_conv_b': 22.078,
     'norm_ffn': 2.902,
     'rwkv_k_a': 6.109,
     'rwkv_ln_w': 6.833}
    for name, (base, spread) in spreads.items():
        noise = np.random.default_rng([zlib.crc32(name.encode()), seed]).standard_normal(out[name].shape)
        drawn = base * np.exp(spread * noise) if base else spread * noise
        out[name] = __import__('jax').numpy.asarray(drawn.astype(out[name].dtype))
    for name, factor in factors.items():
        out[name] = (out[name] * factor).astype(out[name].dtype)
    return out
```

```python
from contextlib import ExitStack, contextmanager

import numpy as np

import concourse.bass as bass
from concourse import mybir

F32 = mybir.dt.float32
F32R = mybir.dt.float32r
I32 = mybir.dt.int32
ALU = mybir.AluOpType
ACT = mybir.ActivationFunctionType
AX_X = mybir.AxisListType.X

P = 128
T = 512
D = 1024
KD = D // P
NORM_EPS = 1e-6
HEADS, NOPE, ROPE, VDIM = 8, 128, 64, 128
QL, KVL = 384, 256
KQ, KKV = QL // P, KVL // P
QB = T // P
SCALE = float(NOPE + ROPE) ** -0.5
NEG = -1.0e30
RH, RN = 16, 64
GN_EPS = 64e-5
CH = 64
NC = T // CH
LW, LG = 64, 160
DFF = 2816
HALF = DFF // P // 2
KAPPA = float(np.exp(-0.5))
SLOT = 3 * 2 * P + 3 * P + 2 * 2 * P + 2 * 2 * P

VEC = {}
_at = 0
for _name, _n in (("norm_mix", 2 * KD), ("norm_ffn", 2 * KD), ("norm_final", KD), ("q_norm", KQ), ("kv_norm", KKV),
                  ("mix", 6 * KD), ("w0", KD), ("a0", KD), ("k_k", KD), ("k_a", KD), ("r_k", KD), ("ln_w", KD),
                  ("ln_b", KD), ("conv_w", 2 * 3 * 2 * HALF), ("conv_b", 2 * 2 * HALF), ("inv_freq", 1)):
    VEC[_name] = _at
    _at += _n
NVEC = _at
CON = {}
_at = 0
for _name, _n in (("ones", P), ("rot", P), ("ident", P), ("causal", P), ("headsum", P), ("headmean", P),
                  ("incl", CH), ("strict", CH), ("ident64", CH), ("levels", 6 * CH), ("reset", T)):
    CON[_name] = _at
    _at += _n
NCON = _at


class Item:

    def __init__(self, t, tpar, j0, thalf):
        self.t, self.j = t, j0 + t
        self.slot = (j0 + tpar) % 2
        self.turn = thalf + (j0 + tpar) // 2
        self.args = (t, tpar, j0, thalf)

    @property
    def prev(self):
        t, tpar, j0, thalf = self.args
        return Item(t - 1, tpar - 1, j0, thalf)


def items(eng, n, j0):
    lead = 2 + n % 2
    for t in range(lead):
        yield Item(t, t, j0, 0)
    if n > lead:
        with eng.Fori(0, (n - lead) // 2) as i:
            for b in range(2):
                yield Item(lead + b + 2 * i, lead + b, j0, i)


def wait(eng, sem, value):
    if isinstance(value, int) and value <= 0:
        return
    eng.wait_ge(sem, value)


class Chain:

    def __init__(self, eng, sem, base=0):
        self.eng, self.sem, self.base, self.n = eng, sem, base, 0

    def __call__(self, ins):
        ins.then_inc(self.sem, 1)
        self.n += 1
        self.eng.wait_ge(self.sem, self.base + self.n)


def trunk(nc, a, stop="all"):
    with ExitStack() as outer:
        scopes = [[]]

        @contextmanager
        def phase():
            scopes.append([])
            with ExitStack() as stack:
                yield stack
            used = scopes.pop()
            if used:
                nc.clear_and_free_semaphores(used)
                nc.all_engine_barrier()

        def sem(name):
            s = nc.alloc_semaphore(name=name)
            scopes[-1].append(s)
            return s

        def sbuf(stack, name, shape, dt=F32):
            return stack.enter_context(nc.sbuf_tensor(name, shape, dt))

        def psum(stack, name, shape=(P, 512)):
            return stack.enter_context(nc.psum_tensor(name, list(shape), F32))

        x = sbuf(outer, "x_resid", [P, KD, T])
        vec = sbuf(outer, "vec", [P, NVEC])
        con = sbuf(outer, "con", [P, NCON])
        raw = [sbuf(outer, f"w_raw{b}", [P, SLOT]) for b in range(2)]
        whi, wlo = [None, None], [None, None]

        def ring(stack, tag):
            for b in range(2):
                whi[b] = sbuf(stack, f"{tag}_w_hi{b}", [P, SLOT], F32R)
                wlo[b] = sbuf(stack, f"{tag}_w_lo{b}", [P, SLOT], F32R)

        w_loaded = [sem("w_loaded0"), sem("w_loaded1")]
        w_hi_ready, w_lo_ready, w_used = sem("w_hi_ready"), sem("w_lo_ready"), sem("w_used")
        x_loaded, con_loaded = sem("x_loaded"), sem("con_loaded")

        def C(name, n=P, rows=slice(0, P)):
            return con[rows, CON[name]:CON[name] + n]

        def V(name, k):
            if isinstance(k, int):
                return vec[:, VEC[name] + k:VEC[name] + k + 1]
            return vec[:, bass.ds(k + VEC[name], 1)]

        def load(sp, it, src, n):
            wait(sp, w_lo_ready, it.j - 1)
            sp.dma_start(raw[it.slot][:, 0:n], src).then_inc(w_loaded[it.slot], 16)

        def split_hi(act, it, n):
            act.wait_ge(w_loaded[it.slot], 16 * it.turn + 16)
            wait(act, w_used, it.j - 1)
            nc.scalar.copy(whi[it.slot][:, 0:n], raw[it.slot][:, 0:n]).then_inc(w_hi_ready, 1)

        def split_lo(pool, it, n):
            pool.wait_ge(w_loaded[it.slot], 16 * it.turn + 16)
            pool.wait_ge(w_hi_ready, it.j + 1)
            nc.gpsimd.tensor_tensor(wlo[it.slot][:, 0:n], raw[it.slot][:, 0:n],
                                    whi[it.slot][:, 0:n].bitcast(F32), ALU.subtract).then_inc(w_lo_ready, 1)

        def three(out, w_at, m, rhs_hi, rhs_lo, slot, start, stop):
            wh, wl = whi[slot][:, w_at:w_at + m], wlo[slot][:, w_at:w_at + m]
            nc.tensor.matmul(out, wh, rhs_hi, start=start, stop=False)
            nc.tensor.matmul(out, wh, rhs_lo, start=False, stop=False)
            return nc.tensor.matmul(out, wl, rhs_hi, start=False, stop=stop)

        def norm_sems(tag):
            return {n: sem(f"{tag}_{n}") for n in ("sq", "ss_used", "ss", "mean", "recip", "rstd", "hn", "hi", "lo")}

        def norm_act(act, s, n, src, sq):
            for k in range(n):
                wait(act, s["ss_used"], k - 1)
                nc.scalar.activation(sq[:, k % 2, :], src(k), ACT.Square).then_inc(s["sq"], 1)

        def norm_act_sqrt(act, s, rstd):
            act.wait_ge(s["recip"], 1)
            nc.scalar.activation(rstd[:, :], rstd[:, :], ACT.Sqrt).then_inc(s["rstd"], 1)

        def norm_pe(pe, s, n, sq, ps):
            for k in range(n):
                pe.wait_ge(s["sq"], k + 1)
                last = nc.tensor.matmul(ps[:, :], C("ones"), sq[:, k % 2, :], start=k == 0, stop=k == n - 1)
                last.then_inc(s["ss_used"], 1)

        def norm_dve(dve, s, n, ps, rstd):
            dve.wait_ge(s["ss_used"], n)
            nc.vector.tensor_scalar(rstd[:, :], ps[:, :], 1.0 / (n * P), NORM_EPS, ALU.mult, ALU.add).then_inc(s["mean"], 1)
            dve.wait_ge(s["mean"], 1)
            nc.vector.reciprocal(rstd[:, :], rstd[:, :]).then_inc(s["recip"], 1)

        def normed_split_dve(dve, s, n, src, gain, rstd, hn):
            dve.wait_ge(s["rstd"], 1)
            for k in range(n):
                wait(dve, s["lo"], k - 1)
                nc.vector.scalar_tensor_tensor(out=hn[:, k % 2, :], in0=src(k), scalar=gain(k), in1=rstd[:, :],
                                               op0=ALU.mult, op1=ALU.mult).then_inc(s["hn"], 1)

        def normed_split_act(act, s, n, hn, hi):
            for k in range(n):
                act.wait_ge(s["hn"], k + 1)
                nc.scalar.copy(hi(k), hn[:, k % 2, :]).then_inc(s["hi"], 1)

        def normed_split_pool(pool, s, n, hn, hi, lo):
            for k in range(n):
                pool.wait_ge(s["hi"], k + 1)
                pool.wait_ge(s["hn"], k + 1)
                nc.gpsimd.tensor_tensor(lo(k), hn[:, k % 2, :], hi(k).bitcast(F32), ALU.subtract).then_inc(s["lo"], 1)

        def xk(k):
            return x[:, k, :] if isinstance(k, int) else x[:, bass.ds(k, 1), :].rearrange("p a t -> p (a t)")

        def dyn(t3, k):
            return t3[:, k, :] if isinstance(k, int) else t3[:, bass.ds(k, 1), :].rearrange("p a t -> p (a t)")

        j_used = [0]

        def project_residual(tag, w, ohi, olo):
            j0 = j_used[0]
            n = KD * P
            with phase() as st:
                ring(st, tag)
                ps = [psum(st, f"{tag}_ps{b}") for b in range(2)]
                free = sem(f"{tag}_added")
                block = st.enter_context(nc.Block(no_gpsimd_drain=True))

                @block.sync
                def _(sp):
                    for it in items(sp, KD, j0):
                        load(sp, it, w[bass.ds(it.t, 1), :, :].rearrange("a p n -> p (a n)"), n)

                @block.scalar
                def _(act):
                    for it in items(act, KD, j0):
                        split_hi(act, it, n)

                @block.gpsimd
                def _(pool):
                    for it in items(pool, KD, j0):
                        split_lo(pool, it, n)

                @block.tensor
                def _(pe):
                    for it in items(pe, KD, j0):
                        pe.wait_ge(w_lo_ready, it.j + 1)
                        wait(pe, free, it.t - 1)
                        for k in range(KD):
                            last = three(ps[it.slot][:, :], k * P, P, ohi[:, k, :], olo[:, k, :], it.slot, k == 0, k == KD - 1)
                        last.then_inc(w_used, 1)

                @block.vector
                def _(dve):
                    for it in items(dve, KD, j0):
                        dve.wait_ge(w_used, it.j + 1)
                        nc.vector.tensor_tensor(xk(it.t), ps[it.slot][:, :], xk(it.t), ALU.add).then_inc(free, 1)
            j_used[0] += KD

        def conv_glu(tag, layer, w_in, w_out):
            jb = j_used[0]
            n_in, n_out = 2 * KD * P, HALF * P
            with phase() as st:
                ring(st, tag)
                sq, rstd = sbuf(st, f"{tag}_sq", [P, 2, T]), sbuf(st, f"{tag}_rstd", [P, T])
                hn = sbuf(st, f"{tag}_hn", [P, 2, T])
                hhi, hlo = sbuf(st, f"{tag}_hhi", [P, KD, T], F32R), sbuf(st, f"{tag}_hlo", [P, KD, T], F32R)
                ahi, alo = sbuf(st, f"{tag}_ahi", [P, HALF, T], F32R), sbuf(st, f"{tag}_alo", [P, HALF, T], F32R)
                cv, sl = sbuf(st, f"{tag}_conv", [P, 2, T]), sbuf(st, f"{tag}_silu", [P, 2, T])
                ga = sbuf(st, f"{tag}_act", [P, 2, T])
                ps_g = [psum(st, f"{tag}_gate{b}") for b in range(2)]
                ps_u = [psum(st, f"{tag}_up{b}") for b in range(2)]
                ps_y = [psum(st, f"{tag}_y{b}") for b in range(2)]
                ps_n = psum(st, f"{tag}_ss")
                s = norm_sems(tag)
                tap2, tap1, conv_done, silu_done, gated, act_hi, act_lo, added = (
                    sem(f"{tag}_{n}") for n in ("tap2", "tap1", "conv_done", "silu_done", "gated", "act_hi", "act_lo", "added"))
                block = st.enter_context(nc.Block(no_gpsimd_drain=True))
                per_half = HALF + KD

                def halves():
                    for hf in range(2):
                        j0 = jb + hf * per_half
                        yield hf, j0, j0 + HALF, hf * HALF, hf * KD

                @block.sync
                def _(sp):
                    for hf, ji, jo, tb, ob in halves():
                        for it in items(sp, HALF, ji):
                            load(sp, it, w_in[bass.ds(it.t + tb, 1), :, :].rearrange("a p n -> p (a n)"), n_in)
                        for it in items(sp, KD, jo):
                            load(sp, it, w_out[bass.ds(it.t + ob, 1), :, :].rearrange("a p n -> p (a n)"), n_out)

                @block.gpsimd
                def _(pool):
                    normed_split_pool(pool, s, KD, hn, lambda k: hhi[:, k, :], lambda k: hlo[:, k, :])
                    for hf, ji, jo, tb, ob in halves():
                        for it in items(pool, HALF, ji):
                            split_lo(pool, it, n_in)
                        for it in items(pool, KD, jo):
                            split_lo(pool, it, n_out)

                def conv_act(act, it, tb):
                    u = it.t + tb
                    act.wait_ge(w_used, it.j + 1)
                    wait(act, silu_done, u - 1)
                    nc.scalar.activation(cv[:, it.slot, :], ps_g[it.slot][:, :], ACT.Identity,
                                         scale=V("conv_w", u + (layer * 3 + 2) * 2 * HALF),
                                         bias=V("conv_b", u + layer * 2 * HALF)).then_inc(tap2, 1)
                    act.wait_ge(conv_done, u + 1)
                    wait(act, gated, u - 1)
                    nc.scalar.activation(sl[:, it.slot, :], cv[:, it.slot, :], ACT.Silu).then_inc(silu_done, 1)

                @block.scalar
                def _(act):
                    norm_act(act, s, KD, xk, sq)
                    norm_act_sqrt(act, s, rstd)
                    normed_split_act(act, s, KD, hn, lambda k: hhi[:, k, :])
                    for hf, ji, jo, tb, ob in halves():
                        for it in items(act, HALF, ji):
                            split_hi(act, it, n_in)
                            if not (isinstance(it.t, int) and it.t == 0):
                                conv_act(act, it.prev, tb)
                        conv_act(act, Item(HALF - 1, HALF - 1, ji, 0), tb)
                        for it in items(act, KD, jo):
                            split_hi(act, it, n_out)

                @block.vector
                def _(dve):
                    norm_dve(dve, s, KD, ps_n, rstd)
                    normed_split_dve(dve, s, KD, xk, lambda k: V("norm_ffn", layer * KD + k), rstd, hn)
                    for hf, ji, jo, tb, ob in halves():
                        for it in items(dve, HALF, ji):
                            u, b = it.t + tb, it.slot
                            dve.wait_ge(tap2, u + 1)
                            nc.vector.scalar_tensor_tensor(
                                out=cv[:, b, 1:T], in0=ps_g[b][:, 0:T - 1], scalar=V("conv_w", u + (layer * 3 + 1) * 2 * HALF),
                                in1=cv[:, b, 1:T], op0=ALU.mult, op1=ALU.add).then_inc(tap1, 1)
                            dve.wait_ge(tap1, u + 1)
                            nc.vector.scalar_tensor_tensor(
                                out=cv[:, b, 2:T], in0=ps_g[b][:, 0:T - 2], scalar=V("conv_w", u + (layer * 3) * 2 * HALF),
                                in1=cv[:, b, 2:T], op0=ALU.mult, op1=ALU.add).then_inc(conv_done, 1)
                            dve.wait_ge(silu_done, u + 1)
                            wait(dve, act_lo, u - 1)
                            nc.vector.tensor_tensor(ga[:, b, :], ps_u[b][:, :], sl[:, b, :], ALU.mult).then_inc(gated, 1)
                            dve.wait_ge(gated, u + 1)
                            nc.vector.tensor_copy(dyn(ahi, it.t), ga[:, b, :]).then_inc(act_hi, 1)
                            dve.wait_ge(act_hi, u + 1)
                            nc.vector.tensor_tensor(dyn(alo, it.t), ga[:, b, :], dyn(ahi, it.t).bitcast(F32),
                                                    ALU.subtract).then_inc(act_lo, 1)
                        for it in items(dve, KD, jo):
                            dve.wait_ge(w_used, it.j + 1)
                            nc.vector.tensor_tensor(xk(it.t), ps_y[it.slot][:, :], xk(it.t), ALU.add).then_inc(added, 1)

                @block.tensor
                def _(pe):
                    norm_pe(pe, s, KD, sq, ps_n)
                    for hf, ji, jo, tb, ob in halves():
                        for it in items(pe, HALF, ji):
                            b = it.slot
                            pe.wait_ge(w_lo_ready, it.j + 1)
                            wait(pe, gated, it.t + tb - 1)
                            for k in range(KD):
                                if hf == 0 and isinstance(it.t, int) and it.t == 0:
                                    pe.wait_ge(s["lo"], k + 1)
                                three(ps_g[b][:, :], k * P, P, hhi[:, k, :], hlo[:, k, :], b, k == 0, k == KD - 1)
                            for k in range(KD):
                                last = three(ps_u[b][:, :], (KD + k) * P, P, hhi[:, k, :], hlo[:, k, :], b, k == 0, k == KD - 1)
                            last.then_inc(w_used, 1)
                        pe.wait_ge(act_lo, tb + HALF)
                        for it in items(pe, KD, jo):
                            b = it.slot
                            pe.wait_ge(w_lo_ready, it.j + 1)
                            wait(pe, added, it.t + ob - 1)
                            for f in range(HALF):
                                last = three(ps_y[b][:, :], f * P, P, ahi[:, f, :], alo[:, f, :], b, f == 0, f == HALF - 1)
                            last.then_inc(w_used, 1)
            j_used[0] += 2 * per_half

        def attention():
            j0 = j_used[0]
            n_lat = KQ + KKV + 1
            NP = HEADS // 2
            with phase() as st:
                cos, sin = sbuf(st, "cos", [P, T]), sbuf(st, "sin", [P, T])
                qhi, qlo = sbuf(st, "qlat_hi", [P, KQ, T], F32R), sbuf(st, "qlat_lo", [P, KQ, T], F32R)
                chi, clo = sbuf(st, "clat_hi", [P, KKV, T], F32R), sbuf(st, "clat_lo", [P, KKV, T], F32R)
                krope = sbuf(st, "krope", [P, T])
                ohi, olo = sbuf(st, "attn_ohi", [P, HEADS, T], F32R), sbuf(st, "attn_olo", [P, HEADS, T], F32R)

                with phase() as s1:
                    ring(s1, "m")
                    sq, rstd = sbuf(s1, "m_sq", [P, 2, T]), sbuf(s1, "m_rstd", [P, T])
                    hn = sbuf(s1, "m_hn", [P, 2, T])
                    hhi, hlo = sbuf(s1, "m_hhi", [P, KD, T], F32R), sbuf(s1, "m_hlo", [P, KD, T], F32R)
                    lat = sbuf(s1, "lat", [P, n_lat, T])
                    pos_i, ang, turns, red = sbuf(s1, "pos_i", [P, T], I32), sbuf(s1, "ang", [P, T]), sbuf(s1, "turns", [P, T]), sbuf(s1, "red", [P, T])
                    rq, rc = sbuf(s1, "rstd_q", [P, T]), sbuf(s1, "rstd_c", [P, T])
                    ktmp = sbuf(s1, "ktmp", [P, 2, T])
                    ps = [psum(s1, f"lat_ps{b}") for b in range(2)]
                    ps_n, ps_q, ps_c, ps_r = (psum(s1, f"m_{n}") for n in ("ss", "ssq", "ssc", "krot"))
                    s, sq_s, sc_s = norm_sems("m"), norm_sems("mq"), norm_sems("mc")
                    lat_out, angles, tables, krot, kmul = (sem(n) for n in ("lat_out", "angles", "tables", "krot", "kmul"))
                    pos_loaded = sem("pos_loaded")
                    n = KD * P
                    block = s1.enter_context(nc.Block(no_gpsimd_drain=True))

                    @block.sync
                    def _(sp):
                        sp.dma_start(x[:, :, :], a["x"]).then_inc(x_loaded, 16)
                        sp.dma_start(vec[:, :], a["vec"]).then_inc(con_loaded, 16)
                        sp.dma_start(con[:, :], a["con"]).then_inc(con_loaded, 16)
                        sp.dma_start(pos_i[:, :], a["positions"]).then_inc(pos_loaded, 16)
                        for it in items(sp, n_lat, j0):
                            load(sp, it, a["w_lat"][bass.ds(it.t, 1), :, :].rearrange("a p n -> p (a n)"), n)

                    @block.scalar
                    def _(act):
                        act.wait_ge(x_loaded, 16)
                        norm_act(act, s, KD, xk, sq)
                        norm_act_sqrt(act, s, rstd)
                        normed_split_act(act, s, KD, hn, lambda k: hhi[:, k, :])

                        def out(it):
                            act.wait_ge(w_used, it.j + 1)
                            nc.scalar.copy(dyn(lat, it.t), ps[it.slot][:, :]).then_inc(lat_out, 1)
                        for it in items(act, n_lat, j0):
                            split_hi(act, it, n)
                            if not (isinstance(it.t, int) and it.t == 0):
                                out(it.prev)
                        out(Item(n_lat - 1, n_lat - 1, j0, 0))
                        act.wait_ge(lat_out, n_lat)
                        norm_act(act, sq_s, KQ, lambda k: lat[:, k, :], sq)
                        act.wait_ge(sq_s["ss_used"], KQ)
                        norm_act(act, sc_s, KKV, lambda k: lat[:, KQ + k, :], sq)
                        norm_act_sqrt(act, sq_s, rq)
                        norm_act_sqrt(act, sc_s, rc)
                        normed_split_act(act, sq_s, KQ, hn, lambda k: qhi[:, k, :])
                        normed_split_act(act, sc_s, KKV, hn, lambda k: chi[:, k, :])
                        act.wait_ge(angles, 1)
                        nc.scalar.activation(sin[:, :], turns[:, :], ACT.Sin).then_inc(tables, 1)
                        act.wait_ge(angles, 2)
                        nc.scalar.activation(cos[:, :], red[:, :], ACT.Sin).then_inc(tables, 1)

                    @block.gpsimd
                    def _(pool):
                        normed_split_pool(pool, s, KD, hn, lambda k: hhi[:, k, :], lambda k: hlo[:, k, :])
                        for it in items(pool, n_lat, j0):
                            split_lo(pool, it, n)
                        normed_split_pool(pool, sq_s, KQ, hn, lambda k: qhi[:, k, :], lambda k: qlo[:, k, :])
                        normed_split_pool(pool, sc_s, KKV, hn, lambda k: chi[:, k, :], lambda k: clo[:, k, :])

                    @block.vector
                    def _(dve):
                        dve.wait_ge(con_loaded, 32)
                        dve.wait_ge(x_loaded, 16)
                        norm_dve(dve, s, KD, ps_n, rstd)
                        normed_split_dve(dve, s, KD, xk, lambda k: V("norm_mix", k), rstd, hn)
                        chain = Chain(dve, sem("angle_chain"))
                        dve.wait_ge(pos_loaded, 16)
                        chain(nc.vector.tensor_copy(ang[:, :], pos_i[:, :]))
                        chain(nc.vector.tensor_scalar(ang[:, :], ang[:, :], V("inv_freq", 0), None, ALU.mult))
                        magic = float(3 << 22)
                        step1 = 6.28125
                        step2 = float(np.float32(round((2 * np.pi - step1) * 2 ** 20) / 2 ** 20))
                        step3 = float(np.float32(2 * np.pi - step1 - step2))
                        pi_in = float(np.nextafter(np.float32(np.pi), np.float32(0)))
                        for dst, shift, quarter in ((turns, 0.0, 0.0), (red, 0.25, float(np.pi / 2))):
                            chain(nc.vector.tensor_scalar(dst[:, :], ang[:, :], float(1 / (2 * np.pi)), shift, ALU.mult, ALU.add))
                            chain(nc.vector.tensor_scalar(dst[:, :], dst[:, :], magic, None, ALU.add))
                            chain(nc.vector.tensor_scalar(ktmp[:, 0, :], dst[:, :], magic, None, ALU.subtract))
                            chain(nc.vector.scalar_tensor_tensor(out=dst[:, :], in0=ktmp[:, 0, :], scalar=-step1, in1=ang[:, :], op0=ALU.mult, op1=ALU.add))
                            chain(nc.vector.scalar_tensor_tensor(out=dst[:, :], in0=ktmp[:, 0, :], scalar=-step2, in1=dst[:, :], op0=ALU.mult, op1=ALU.add))
                            chain(nc.vector.scalar_tensor_tensor(out=dst[:, :], in0=ktmp[:, 0, :], scalar=-step3, in1=dst[:, :], op0=ALU.mult, op1=ALU.add))
                            chain(nc.vector.tensor_scalar(dst[:, :], dst[:, :], quarter, pi_in, ALU.add, ALU.min))
                            nc.vector.tensor_scalar(dst[:, :], dst[:, :], -pi_in, None, ALU.max).then_inc(angles, 1)
                        norm_dve(dve, sq_s, KQ, ps_q, rq)
                        norm_dve(dve, sc_s, KKV, ps_c, rc)
                        normed_split_dve(dve, sq_s, KQ, lambda k: lat[:, k, :], lambda k: V("q_norm", k), rq, hn)
                        dve.wait_ge(sq_s["lo"], KQ)
                        normed_split_dve(dve, sc_s, KKV, lambda k: lat[:, KQ + k, :], lambda k: V("kv_norm", k), rc, hn)
                        dve.wait_ge(tables, 2)
                        dve.wait_ge(krot, 1)
                        nc.vector.tensor_tensor(ktmp[:, 0, :], lat[:, n_lat - 1, :], cos[:, :], ALU.mult).then_inc(kmul, 1)
                        nc.vector.tensor_tensor(ktmp[:, 1, :], ps_r[:, :], sin[:, :], ALU.mult).then_inc(kmul, 1)
                        dve.wait_ge(kmul, 2)
                        nc.vector.tensor_tensor(krope[:, :], ktmp[:, 0, :], ktmp[:, 1, :], ALU.add).then_inc(kmul, 1)

                    @block.tensor
                    def _(pe):
                        pe.wait_ge(con_loaded, 32)
                        norm_pe(pe, s, KD, sq, ps_n)
                        for it in items(pe, n_lat, j0):
                            pe.wait_ge(w_lo_ready, it.j + 1)
                            wait(pe, lat_out, it.t - 1)
                            for k in range(KD):
                                if isinstance(it.t, int) and it.t == 0:
                                    pe.wait_ge(s["lo"], k + 1)
                                last = three(ps[it.slot][:, :], k * P, P, hhi[:, k, :], hlo[:, k, :], it.slot, k == 0, k == KD - 1)
                            last.then_inc(w_used, 1)
                        pe.wait_ge(lat_out, n_lat)
                        nc.tensor.matmul(ps_r[:, :], C("rot"), lat[:, n_lat - 1, :], start=True, stop=True).then_inc(krot, 1)
                        norm_pe(pe, sq_s, KQ, sq, ps_q)
                        norm_pe(pe, sc_s, KKV, sq, ps_c)

                with phase() as s2:
                    jp = j0 + n_lat
                    ring(s2, "p")
                    qn, kn = sbuf(s2, "q_nope", [P, 2, T]), sbuf(s2, "k_nope", [P, 2, T])
                    qraw, qr = sbuf(s2, "q_rope_raw", [P, T]), sbuf(s2, "q_rope", [P, T])
                    qcos, qsin = sbuf(s2, "q_cos", [P, T]), sbuf(s2, "q_sin", [P, T])
                    v = sbuf(s2, "v", [P, QB, 2 * VDIM])
                    pexp = sbuf(s2, "p_exp", [P, 2, T])
                    pT = sbuf(s2, "p_T", [P, 2, QB, T])
                    mx, nmx, rs, ri = (sbuf(s2, n, [P, 2 * QB]) for n in ("mx", "nmx", "rowsum", "rinv"))
                    pp = [psum(s2, f"proj_ps{b}") for b in range(2)]
                    sc = [psum(s2, f"score_ps{b}") for b in range(2)]
                    tp = [psum(s2, f"pT_ps{b}") for b in range(2)]
                    op = [psum(s2, f"o_ps{b}") for b in range(2)]
                    S = {n: sem(n) for n in ("proj_done", "proj_out", "rot_done", "qrope_mul", "qrope_done", "score_done", "masked",
                                             "max_done", "nmax_done", "exp_done", "rinv_done", "p_norm", "pT_done", "pT_out",
                                             "o_done", "o_hi", "o_lo")}
                    NPR = 7
                    NB = 2 * QB
                    at_qn, at_qr = 0, KQ * 2 * P
                    at_kn = at_qr + KQ * P
                    at_v = at_kn + KKV * 2 * P
                    block = s2.enter_context(nc.Block(no_gpsimd_drain=True))

                    @block.sync
                    def _(sp):
                        for it in items(sp, NP, jp):
                            load(sp, it, a["w_pair"][bass.ds(it.t, 1), :, :].rearrange("a p n -> p (a n)"), SLOT)

                    @block.gpsimd
                    def _(pool):
                        for it in items(pool, NP, jp):
                            split_lo(pool, it, SLOT)

                    @block.tensor
                    def _(pe):
                        def lat_product(it, step, w_at, kk, hi, lo, stride):
                            for k in range(kk):
                                last = three(pp[step % 2][:, :], w_at + k * stride, P, hi[:, k, :], lo[:, k, :], it.slot,
                                             k == 0, k == kk - 1)
                            last.then_inc(S["proj_done"], 1)

                        def value_product(it, g):
                            for tt in range(2):
                                tok = slice((2 * g + tt) * P, (2 * g + tt + 1) * P)
                                out = pp[(5 + g) % 2][:, tt * 2 * VDIM:(tt + 1) * 2 * VDIM]
                                for k in range(KKV):
                                    wv = slice(at_v + k * 2 * VDIM, at_v + (k + 1) * 2 * VDIM)
                                    nc.tensor.matmul(out, chi[:, k, tok], whi[it.slot][:, wv], start=k == 0, stop=False)
                                    nc.tensor.matmul(out, chi[:, k, tok], wlo[it.slot][:, wv], start=False, stop=False)
                                    last = nc.tensor.matmul(out, clo[:, k, tok], whi[it.slot][:, wv], start=False, stop=k == KKV - 1)
                            return last

                        def scores(t, n):
                            h, i = n // QB, n % QB
                            nk, qs, rows = (i + 1) * P, slice(i * P, (i + 1) * P), slice(h * ROPE, (h + 1) * ROPE)
                            wait(pe, S["exp_done"], NB * t + n - 1)
                            nc.tensor.matmul(sc[n % 2][:, 0:nk], qn[:, h, qs], kn[:, h, 0:nk], start=True, stop=False)
                            nc.tensor.matmul(sc[n % 2][:, 0:nk], qr[rows, qs], krope[rows, 0:nk], start=False,
                                             stop=True).then_inc(S["score_done"], 1)

                        def turn_p(t, n):
                            wait(pe, S["pT_out"], NB * t + n - 1)
                            pe.wait_ge(S["p_norm"], NB * t + n + 1)
                            for kb in range(n % QB + 1):
                                ks = slice(kb * P, (kb + 1) * P)
                                last = nc.tensor.transpose(tp[n % 2][:, ks], pexp[:, n % 2, ks], C("ident"))
                            last.then_inc(S["pT_done"], 1)

                        def value_sum(t, h):
                            pe.wait_ge(S["pT_out"], NB * t + QB * (h + 1))
                            wait(pe, S["o_lo"], 2 * t + h - 1)
                            for kb in range(QB):
                                last = nc.tensor.matmul(op[h][:, kb * P:T], v[:, kb, h * VDIM:(h + 1) * VDIM],
                                                        pT[:, h, kb, kb * P:T], start=kb == 0, stop=kb == QB - 1)
                            last.then_inc(S["o_done"], 1)

                        for it in items(pe, NP, jp):
                            t = it.t
                            pe.wait_ge(w_lo_ready, it.j + 1)
                            wait(pe, S["proj_out"], NPR * t)
                            lat_product(it, 0, at_qn, KQ, qhi, qlo, 2 * P)
                            wait(pe, S["qrope_done"], t)
                            lat_product(it, 1, at_qn + P, KQ, qhi, qlo, 2 * P)
                            pe.wait_ge(S["proj_out"], NPR * t + 1)
                            lat_product(it, 2, at_qr, KQ, qhi, qlo, P)
                            pe.wait_ge(S["proj_out"], NPR * t + 2)
                            lat_product(it, 3, at_kn, KKV, chi, clo, 2 * P)
                            pe.wait_ge(S["proj_out"], NPR * t + 3)
                            lat_product(it, 4, at_kn + P, KKV, chi, clo, 2 * P)
                            pe.wait_ge(S["proj_out"], NPR * t + 4)
                            value_product(it, 0).then_inc(S["proj_done"], 1)
                            pe.wait_ge(S["proj_out"], NPR * t + 5)
                            value_product(it, 1).then_inc(w_used, 1)
                            pe.wait_ge(S["proj_out"], NPR * t + 6)
                            nc.tensor.matmul(pp[1][:, :], C("rot"), qraw[:, :], start=True, stop=True).then_inc(S["rot_done"], 1)
                            pe.wait_ge(S["proj_out"], NPR * t + 7)
                            pe.wait_ge(S["qrope_done"], t + 1)
                            for n in range(NB + 1):
                                if n < NB:
                                    scores(t, n)
                                if n > 0:
                                    turn_p(t, n - 1)
                                if n == QB + 2:
                                    value_sum(t, 0)
                            value_sum(t, 1)

                    @block.scalar
                    def _(act):
                        def exps(t, n):
                            act.wait_ge(S["nmax_done"], NB * t + n + 1)
                            wait(act, S["pT_done"], NB * t + n - 1)
                            nk = (n % QB + 1) * P
                            nc.scalar.activation(pexp[:, n % 2, 0:nk], sc[n % 2][:, 0:nk], ACT.Exp, scale=SCALE,
                                                 bias=nmx[:, n:n + 1], accum_out=rs[:, n:n + 1]).then_inc(S["exp_done"], 1)

                        def turned_out(t, n):
                            act.wait_ge(S["pT_done"], NB * t + n + 1)
                            h, i = n // QB, n % QB
                            wait(act, S["o_done"], 2 * t + h - 1)
                            nc.scalar.copy(pT[:, h, 0:i + 1, i * P:(i + 1) * P],
                                           tp[n % 2][:, 0:(i + 1) * P].rearrange("p (k q) -> p k q", q=P)).then_inc(S["pT_out"], 1)

                        def out_hi(t, h):
                            act.wait_ge(S["o_done"], 2 * t + h + 1)
                            nc.scalar.copy(dyn(ohi, 2 * t + h), op[h][:, :]).then_inc(S["o_hi"], 1)

                        for it in items(act, NP, jp):
                            t = it.t
                            split_hi(act, it, SLOT)
                            for step, dst in enumerate((qn[:, 0, :], qn[:, 1, :], qraw[:, :], kn[:, 0, :], kn[:, 1, :])):
                                act.wait_ge(S["proj_done"], (NPR - 1) * t + step + 1)
                                nc.scalar.copy(dst, pp[step % 2][:, :]).then_inc(S["proj_out"], 1)
                            for g in range(2):
                                if g == 0:
                                    act.wait_ge(S["proj_done"], (NPR - 1) * t + 6)
                                else:
                                    act.wait_ge(w_used, it.j + 1)
                                nc.scalar.copy(v[:, 2 * g:2 * g + 2, :], pp[(5 + g) % 2][:, :].rearrange("p (a n) -> p a n", a=2)).then_inc(S["proj_out"], 1)
                            for n in range(NB):
                                exps(t, n)
                                if n >= 2:
                                    turned_out(t, n - 2)
                            turned_out(t, NB - 2)
                            out_hi(t, 0)
                            turned_out(t, NB - 1)
                            out_hi(t, 1)

                    @block.vector
                    def _(dve):
                        def row_max(t, n):
                            i = n % QB
                            nk, diag = (i + 1) * P, slice(i * P, (i + 1) * P)
                            dve.wait_ge(S["score_done"], NB * t + n + 1)
                            nc.vector.tensor_tensor(sc[n % 2][:, diag], sc[n % 2][:, diag], C("causal"), ALU.add).then_inc(S["masked"], 1)
                            dve.wait_ge(S["masked"], NB * t + n + 1)
                            nc.vector.reduce_max(mx[:, n:n + 1], sc[n % 2][:, 0:nk], AX_X).then_inc(S["max_done"], 1)
                            dve.wait_ge(S["max_done"], NB * t + n + 1)
                            nc.vector.tensor_scalar(nmx[:, n:n + 1], mx[:, n:n + 1], -SCALE, None, ALU.mult).then_inc(S["nmax_done"], 1)

                        def normalize(t, n):
                            nk = (n % QB + 1) * P
                            dve.wait_ge(S["exp_done"], NB * t + n + 1)
                            nc.vector.reciprocal(ri[:, n:n + 1], rs[:, n:n + 1]).then_inc(S["rinv_done"], 1)
                            dve.wait_ge(S["rinv_done"], NB * t + n + 1)
                            nc.vector.tensor_scalar(pexp[:, n % 2, 0:nk], pexp[:, n % 2, 0:nk], ri[:, n:n + 1], None,
                                                    ALU.mult).then_inc(S["p_norm"], 1)

                        def out_lo(t, h):
                            dve.wait_ge(S["o_hi"], 2 * t + h + 1)
                            nc.vector.tensor_tensor(dyn(olo, 2 * t + h), op[h][:, :], dyn(ohi, 2 * t + h).bitcast(F32),
                                                    ALU.subtract).then_inc(S["o_lo"], 1)

                        for it in items(dve, NP, jp):
                            t = it.t
                            dve.wait_ge(S["proj_out"], NPR * t + 3)
                            nc.vector.tensor_tensor(qcos[:, :], qraw[:, :], cos[:, :], ALU.mult).then_inc(S["qrope_mul"], 1)
                            dve.wait_ge(S["rot_done"], t + 1)
                            nc.vector.tensor_tensor(qsin[:, :], pp[1][:, :], sin[:, :], ALU.mult).then_inc(S["qrope_mul"], 1)
                            dve.wait_ge(S["qrope_mul"], 2 * t + 2)
                            nc.vector.tensor_tensor(qr[:, :], qcos[:, :], qsin[:, :], ALU.add).then_inc(S["qrope_done"], 1)
                            for n in range(NB):
                                row_max(t, n)
                                if n > 0:
                                    normalize(t, n - 1)
                            normalize(t, NB - 1)
                            out_lo(t, 0)
                            out_lo(t, 1)
                j_used[0] = jp + NP
                project_residual("mo", a["w_attn_out"], ohi, olo)

        def rwkv():
            j0 = j_used[0]
            with phase() as st:
                h = sbuf(st, "h", [P, KD, T])
                kT, rT = sbuf(st, "kT", [P, KD, T]), sbuf(st, "rT", [P, KD, T])
                vT = h
                th, la = sbuf(st, "w_lora", [LW, T]), sbuf(st, "a_lora", [LW, T])
                lga, lgb = sbuf(st, "g_lora_a", [P, T]), sbuf(st, "g_lora_b", [LG - P, T])

                with phase() as s1:
                    ring(s1, "r")
                    xx = sbuf(s1, "shift_diff", [P, KD, T])
                    xm = sbuf(s1, "mixed", [P, 4, T])
                    xhi, xlo = sbuf(s1, "mixed_hi", [P, KD, T], F32R), sbuf(s1, "mixed_lo", [P, KD, T], F32R)
                    l1 = sbuf(s1, "lora_in", [P, KD, 2 * LW + LG])
                    rstd = sbuf(s1, "r_rstd", [P, T])
                    ps = [psum(s1, f"rkv_ps{b}") for b in range(2)]
                    ps_n, ps_w, ps_a, ps_ga, ps_gb = (psum(s1, f"r_{n}") for n in ("ss", "lw", "la", "lga", "lgb"))
                    s = norm_sems("r")
                    lora_loaded, normed, shifted, mixed, m_hi, m_lo, lora_used, rkv_out, lora_out = (
                        sem(f"r_{n}") for n in ("lora_loaded", "normed", "shifted", "mixed", "mix_hi", "mix_lo", "lora_used", "rkv_out", "lora_out"))
                    n = KD * P
                    NL = 3
                    MIXES = (3, 4, 5, 1, 0, 2)
                    DST = (kT, rT, vT)
                    block = s1.enter_context(nc.Block(no_gpsimd_drain=True))

                    @block.sync
                    def _(sp):
                        sp.dma_start(l1[:, :, :], a["lora_in"].rearrange("p (k n) -> p k n", k=KD)).then_inc(lora_loaded, 16)
                        for q in range(3):
                            for it in items(sp, KD, j0 + q * KD):
                                load(sp, it, a["w_rkv"][bass.ds(it.t + q * KD, 1), :, :].rearrange("a p n -> p (a n)"), n)

                    @block.vector
                    def _(dve):
                        norm_dve(dve, s, KD, ps_n, rstd)
                        dve.wait_ge(s["rstd"], 1)
                        for k in range(KD):
                            nc.vector.scalar_tensor_tensor(out=h[:, k, :], in0=xk(k), scalar=V("norm_mix", KD + k), in1=rstd[:, :],
                                                           op0=ALU.mult, op1=ALU.mult).then_inc(normed, 1)
                            dve.wait_ge(normed, k + 1)
                            nc.vector.tensor_tensor(xx[:, k, 1:T], h[:, k, 0:T - 1], h[:, k, 1:T], ALU.subtract).then_inc(shifted, 1)
                            nc.vector.tensor_scalar(xx[:, k, 0:1], h[:, k, 0:1], -1.0, None, ALU.mult).then_inc(shifted, 1)
                        for q, mi in enumerate(MIXES):
                            for k in range(KD):
                                u = q * KD + k
                                dve.wait_ge(shifted, 2 * k + 2)
                                if u - 4 >= NL * KD:
                                    dve.wait_ge(m_lo, u - 4 - NL * KD + 1)
                                elif u >= 4:
                                    dve.wait_ge(lora_used, u - 3)
                                nc.vector.scalar_tensor_tensor(out=xm[:, u % 4, :], in0=xx[:, k, :], scalar=V("mix", mi * KD + k),
                                                               in1=h[:, k, :], op0=ALU.mult, op1=ALU.add).then_inc(mixed, 1)

                    @block.scalar
                    def _(act):
                        norm_act(act, s, KD, xk, xm)
                        norm_act_sqrt(act, s, rstd)
                        act.wait_ge(lora_used, KD)
                        nc.scalar.activation(th[:, :], ps_w[0:LW, :], ACT.Tanh).then_inc(lora_out, 1)
                        act.wait_ge(lora_used, 2 * KD)
                        nc.scalar.copy(la[:, :], ps_a[0:LW, :]).then_inc(lora_out, 1)
                        act.wait_ge(lora_used, 3 * KD)
                        nc.scalar.activation(lga[:, :], ps_ga[:, :], ACT.Sigmoid).then_inc(lora_out, 1)
                        nc.scalar.activation(lgb[:, :], ps_gb[0:LG - P, :], ACT.Sigmoid).then_inc(lora_out, 1)
                        for q in range(3):
                            for k in range(KD):
                                u = (NL + q) * KD + k
                                act.wait_ge(mixed, u + 1)
                                wait(act, w_used, j0 + q * KD if q else 0)
                                nc.scalar.copy(xhi[:, k, :], xm[:, u % 4, :]).then_inc(m_hi, 1)

                            def out(it):
                                act.wait_ge(w_used, it.j + 1)
                                nc.scalar.copy(dyn(DST[q], it.t), ps[it.slot][:, :]).then_inc(rkv_out, 1)
                            for it in items(act, KD, j0 + q * KD):
                                split_hi(act, it, n)
                                if not (isinstance(it.t, int) and it.t == 0):
                                    out(it.prev)
                            out(Item(KD - 1, KD - 1, j0 + q * KD, 0))

                    @block.gpsimd
                    def _(pool):
                        for q in range(3):
                            for k in range(KD):
                                u = (NL + q) * KD + k
                                pool.wait_ge(m_hi, q * KD + k + 1)
                                nc.gpsimd.tensor_tensor(xlo[:, k, :], xm[:, u % 4, :], xhi[:, k, :].bitcast(F32), ALU.subtract).then_inc(m_lo, 1)
                            for it in items(pool, KD, j0 + q * KD):
                                split_lo(pool, it, n)

                    @block.tensor
                    def _(pe):
                        norm_pe(pe, s, KD, xm, ps_n)
                        pe.wait_ge(lora_loaded, 16)
                        for q, (at, m, out) in enumerate(((0, LW, ps_w), (LW, LW, ps_a), (2 * LW, LG, ps_ga))):
                            for k in range(KD):
                                u = q * KD + k
                                pe.wait_ge(mixed, u + 1)
                                last = nc.tensor.matmul(out[0:min(m, P), :], l1[:, k, at:at + min(m, P)], xm[:, u % 4, :],
                                                        start=k == 0, stop=k == KD - 1)
                                if m > P:
                                    last = nc.tensor.matmul(ps_gb[0:m - P, :], l1[:, k, at + P:at + m], xm[:, u % 4, :],
                                                            start=k == 0, stop=k == KD - 1)
                                last.then_inc(lora_used, 1)
                        for q in range(3):
                            for it in items(pe, KD, j0 + q * KD):
                                pe.wait_ge(w_lo_ready, it.j + 1)
                                wait(pe, rkv_out, it.t + q * KD - 1)
                                for k in range(KD):
                                    if isinstance(it.t, int) and it.t == 0:
                                        pe.wait_ge(m_lo, q * KD + k + 1)
                                    last = three(ps[it.slot][:, :], k * P, P, xhi[:, k, :], xlo[:, k, :], it.slot, k == 0, k == KD - 1)
                                last.then_inc(w_used, 1)
                j_used[0] += 3 * KD
                ohi, olo = sbuf(st, "wkv_ohi", [P, KD, T], F32R), sbuf(st, "wkv_olo", [P, KD, T], F32R)
                wkv(kT, rT, vT, th, la, lga, lgb, ohi, olo)
                project_residual("ro", a["w_rwkv_out"], ohi, olo)

        def wkv(kT, rT, vT, th, la, lga, lgb, ohi, olo):
            with phase() as st:
                work = sbuf(st, "work", [P, 11, T])

                def tile(i):
                    return raw[i // 4][:, (i % 4) * T:(i % 4 + 1) * T] if i < 8 else work[:, i - 8, :]
                (d, rate, gate, D, Dc, Dp, eR, eK, eA, kk, kk2, rn, kp, rk, b1, bonus, prob, inv, tt) = (tile(i) for i in range(19))
                y, yc, yc2, out_t = eR, eK, eA, kk

                def ch(t2):
                    return t2.rearrange("p (c s) -> p c s", s=CH)
                lw = sbuf(st, "lora_out", [P, 4 * P])
                AR = sbuf(st, "AR", [P, NC, 2, CH])
                KB = sbuf(st, "KB", [P, NC, 2, CH])
                KBT = sbuf(st, "KBT", [P, NC, P])
                VU = sbuf(st, "VU", [P, NC, 2, CH])
                Vs = sbuf(st, "V_stacked", [P, NC, CH])
                AB = sbuf(st, "a_B", [P, NC, 2, CH])
                MB = sbuf(st, "M_B", [P, NC, 2, CH])
                LT = sbuf(st, "LT", [P, NC, CH])
                LB = sbuf(st, "LT_B", [P, 2, NC, 2, CH])
                RKB = sbuf(st, "RKB", [P, NC, 2, CH])
                PB = sbuf(st, "P_B", [P, NC, 2, CH])
                TB = sbuf(st, "T_B", [P, NC, 2, CH])
                R = sbuf(st, "R", [P, CH])
                Sp, Sg = sbuf(st, "S", [P, 2, CH]), sbuf(st, "S_decayed", [P, CH])
                SB = sbuf(st, "S_B", [P, 2, 2, CH])
                gs = sbuf(st, "chunk_decay", [P, NC])
                B = [psum(st, f"wkv_ps{b}") for b in range(8)]
                names = ("lw_loaded", "zeroed", "lora_done", "lora_ev", "vb_done", "v_done", "v_out", "dc_done", "dp_done", "gs_done", "exps",
                         "gs_exp", "kk2_done", "ss_done", "rn_recip", "rn_done", "rk_done", "bonus_done", "bonus_out", "ar_done",
                         "kb_done", "kbt_done", "kbt_out", "gram_done", "lt_done", "gram_out", "p_ready", "pb_done", "lb_done", "x0_done",
                         "x_out", "tt_done", "tt_out", "tb_done", "xl_done", "pl_done", "p_new", "x_new", "rhs_done", "rhs_out",
                         "u_done", "u_out0", "u_out1", "s_done", "s_new", "sb_done", "y_done", "y_out", "mu_done", "yc_done", "yc2_done",
                         "var_done", "var_recip", "rstd_done", "out_hi", "out_lo")
                S = {n: sem(f"k_{n}") for n in names}
                chain_sem = {e: sem(f"k_chain_{e}") for e in ("dve", "act", "pool")}
                per = {}
                HR = (slice(0, CH), slice(CH, P))
                VR = HR
                UR = (HR[1], HR[0])
                LEVELS = 5

                def turns(eng, name, body):
                    chain = Chain(eng, chain_sem.get(name))
                    body(0, chain)
                    each = chain.n
                    with eng.Fori(1, KD) as c:
                        body(c, Chain(eng, chain_sem.get(name), c * each))

                block = st.enter_context(nc.Block(no_gpsimd_drain=True))

                @block.sync
                def _(sp):
                    def body(c, _):
                        wait(sp, S["lora_done"], c)
                        sp.dma_start(lw[:, :], a["lora_out"][bass.ds(c, 1), :, :].rearrange("a p n -> p (a n)")).then_inc(S["lw_loaded"], 16)
                    turns(sp, "sp", body)

                @block.tensor
                def _(pe):
                    def flat(t4):
                        return t4.rearrange("p a s -> p (a s)")

                    def body(c, _):
                        pe.wait_ge(S["lw_loaded"], 16 * c + 16)
                        wait(pe, S["out_lo"], c)
                        nc.tensor.matmul(B[0][:, :], lw[0:LW, 0:P], th[:, :], start=True, stop=True)
                        nc.tensor.matmul(B[1][:, :], lw[0:LW, P:2 * P], la[:, :], start=True, stop=True)
                        nc.tensor.matmul(B[2][:, :], lw[:, 2 * P:3 * P], lga[:, :], start=True, stop=False)
                        nc.tensor.matmul(B[2][:, :], lw[0:LG - P, 3 * P:4 * P], lgb[:, :], start=False, stop=True).then_inc(S["lora_done"], 1)
                        pe.wait_ge(S["vb_done"], 2 * c + 2)
                        for q in range(NC):
                            last = nc.tensor.matmul(B[5][:, q * CH:(q + 1) * CH], flat(PB[:, q, :, :]), C("ident64", CH), start=True, stop=True)
                        last.then_inc(S["v_done"], 1)
                        pe.wait_ge(S["kk2_done"], c + 1)
                        nc.tensor.matmul(B[3][:, :], C("headsum"), kk2, start=True, stop=True).then_inc(S["ss_done"], 1)
                        pe.wait_ge(S["rk_done"], c + 1)
                        nc.tensor.matmul(B[4][:, :], C("headsum"), rk, start=True, stop=True).then_inc(S["bonus_done"], 1)
                        pe.wait_ge(S["kb_done"], 4 * c + 4)
                        for q in range(NC):
                            last = nc.tensor.transpose(B[6 + q // 4][:, (q % 4) * P:(q % 4 + 1) * P], flat(KB[:, q, :, :]), C("ident"))
                        last.then_inc(S["kbt_done"], 1)
                        pe.wait_ge(S["ar_done"], 2 * c + 2)
                        pe.wait_ge(S["lora_ev"], 3 * c + 3)
                        pe.wait_ge(S["rn_recip"], 2 * c + 1)
                        for hh in range(2):
                            for q in range(NC):
                                last = nc.tensor.matmul(B[2 * hh + q // 4][:, (q % 4) * P:(q % 4 + 1) * P],
                                                        flat(KB[HR[hh], q, :, :]), flat(AR[HR[hh], q, :, :]), start=True, stop=True)
                        last.then_inc(S["gram_done"], 1)
                        pe.wait_ge(S["pb_done"], 2 * (LEVELS + 1) * c + 2)
                        pe.wait_ge(S["kbt_out"], 2 * c + 2)
                        for q in range(NC):
                            last = nc.tensor.matmul(B[6][:, q * CH:(q + 1) * CH], flat(PB[:, q, :, :]), C("ident64", CH), start=True, stop=True)
                        last.then_inc(S["x0_done"], 1)
                        pe.wait_ge(S["bonus_out"], c + 1)
                        pe.wait_ge(S["v_out"], 3 * c + 3)
                        for l in range(LEVELS):
                            pe.wait_ge(S["lb_done"], 2 * (LEVELS * c + l + 1))
                            if l == 0:
                                pe.wait_ge(S["x_out"], c + 1)
                            else:
                                pe.wait_ge(S["x_new"], (LEVELS - 1) * c + l)
                            for q in range(NC):
                                last = nc.tensor.matmul(B[4][:, q * CH:(q + 1) * CH], flat(LB[:, l % 2, q, :, :]), ch(inv)[:, q, :], start=True, stop=True)
                            last.then_inc(S["tt_done"], 1)
                            if l < LEVELS - 1:
                                pe.wait_ge(S["tt_out"], LEVELS * c + l + 1)
                                pe.wait_ge(S["pb_done"], 2 * ((LEVELS + 1) * c + l + 1))
                                for q in range(NC):
                                    last = nc.tensor.matmul(B[6][:, q * CH:(q + 1) * CH], flat(PB[:, q, :, :]), ch(tt)[:, q, :], start=True, stop=True)
                                last.then_inc(S["xl_done"], 1)
                            pe.wait_ge(S["tb_done"], 2 * (LEVELS * c + l + 1))
                            if l == 0:
                                pe.wait_ge(S["p_ready"], c + 1)
                            else:
                                pe.wait_ge(S["p_new"], LEVELS * c + l)
                            for q in range(NC):
                                last = nc.tensor.matmul(B[5][:, q * CH:(q + 1) * CH], flat(TB[:, q, :, :]), ch(prob)[:, q, :], start=True, stop=True)
                            last.then_inc(S["pl_done"], 1)
                        pe.wait_ge(S["pb_done"], 2 * (LEVELS + 1) * (c + 1))
                        pe.wait_ge(S["gram_out"], 8 * c + 8)
                        pe.wait_ge(S["x_new"], (LEVELS - 1) * (c + 1))

                        def outputs(q):
                            out = B[7][:, q * CH:(q + 1) * CH]
                            if q > 0:
                                pe.wait_ge(S["sb_done"], 2 * ((NC - 1) * c + q))
                                nc.tensor.matmul(out, flat(SB[:, q % 2, :, :]), AR[:, q, 1, :], start=True, stop=False)
                            for hh in range(2):
                                last = nc.tensor.matmul(B[7][HR[hh], q * CH:(q + 1) * CH], VU[:, q, hh, :], RKB[:, q, hh, :], start=q == 0, stop=True)
                            return last
                        for q in range(NC):
                            out = B[4][:, 0:CH]
                            if q > 0:
                                pe.wait_ge(S["s_new"], (NC - 1) * c + q)
                                nc.tensor.matmul(out, flat(AB[:, q, :, :]), Sp[:, q % 2, :], start=True, stop=False)
                            nc.tensor.matmul(out, flat(MB[:, q, :, :]), Vs[:, q, :], start=q == 0, stop=True).then_inc(S["rhs_done"], 1)
                            if q > 0:
                                outputs(q - 1)
                            pe.wait_ge(S["rhs_out"], NC * c + q + 1)
                            nc.tensor.matmul(B[5][:, 0:CH], flat(PB[:, q, :, :]), R[:, :], start=True, stop=True).then_inc(S["u_done"], 1)
                            pe.wait_ge(S["u_out0"], NC * c + q + 1)
                            pe.wait_ge(S["u_out1"], NC * c + q + 1)
                            if q < NC - 1:
                                for hh in range(2):
                                    last = nc.tensor.matmul(B[6][HR[hh], 0:CH], KBT[:, q, hh * CH:(hh + 1) * CH], VU[:, q, hh, :], start=True, stop=True)
                                last.then_inc(S["s_done"], 1)
                        outputs(NC - 1).then_inc(S["y_done"], 1)
                        pe.wait_ge(S["y_out"], c + 1)
                        nc.tensor.matmul(B[0][:, :], C("headmean"), y, start=True, stop=True).then_inc(S["mu_done"], 1)
                        pe.wait_ge(S["yc2_done"], c + 1)
                        nc.tensor.matmul(B[1][:, :], C("headmean"), yc2, start=True, stop=True).then_inc(S["var_done"], 1)
                    turns(pe, "pe", body)

                @block.scalar
                def _(act):
                    def body(c, chain):
                        A = nc.scalar
                        wait(act, S["out_lo"], c)
                        if isinstance(c, int):
                            act.wait_ge(S["zeroed"], 6)
                        for hh in range(2):
                            A.copy(PB[HR[hh], :, hh, :], ch(dyn(vT, c))[HR[hh], :, :]).then_inc(S["vb_done"], 1)
                        act.wait_ge(S["lora_done"], c + 1)
                        A.activation(d, B[0][:, :], ACT.Sigmoid, bias=V("w0", c)).then_inc(S["lora_ev"], 1)
                        A.activation(rate, B[1][:, :], ACT.Sigmoid, bias=V("a0", c)).then_inc(S["lora_ev"], 1)
                        A.copy(gate, B[2][:, :]).then_inc(S["lora_ev"], 1)
                        act.wait_ge(S["v_done"], c + 1)
                        A.copy(Vs[:, :, :], ch(B[5][:, :])).then_inc(S["v_out"], 1)
                        for hh in range(2):
                            A.copy(VU[VR[hh], :, hh, :], ch(B[5][VR[hh], :])).then_inc(S["v_out"], 1)
                        act.wait_ge(S["rn_recip"], 2 * c + 2)
                        A.activation(rn, rn, ACT.Sqrt).then_inc(S["rn_done"], 1)
                        act.wait_ge(S["dc_done"], c + 1)
                        A.activation(eR, Dc, ACT.Exp, scale=-KAPPA).then_inc(S["exps"], 1)
                        A.activation(eK, Dc, ACT.Exp, scale=KAPPA).then_inc(S["exps"], 1)
                        act.wait_ge(S["dp_done"], c + 1)
                        A.activation(eA, Dp, ACT.Exp, scale=-KAPPA).then_inc(S["exps"], 1)
                        act.wait_ge(S["gs_done"], c + 1)
                        A.activation(gs[:, 0:NC - 1], gs[:, 0:NC - 1], ACT.Exp, scale=-KAPPA).then_inc(S["gs_exp"], 1)
                        act.wait_ge(S["kbt_done"], c + 1)
                        for b in range(2):
                            A.copy(KBT[:, 4 * b:4 * b + 4, :], B[6 + b][:, :].rearrange("p (c s) -> p c s", s=P)).then_inc(S["kbt_out"], 1)

                        def p_blocks():
                            for hh in range(2):
                                A.copy(PB[HR[hh], :, hh, :], ch(prob)[HR[hh], :, :]).then_inc(S["pb_done"], 1)
                        act.wait_ge(S["p_ready"], c + 1)
                        p_blocks()
                        act.wait_ge(S["x0_done"], c + 1)
                        A.copy(inv, B[6][:, :]).then_inc(S["x_out"], 1)
                        for l in range(LEVELS):
                            act.wait_ge(S["tt_done"], LEVELS * c + l + 1)
                            A.copy(tt, B[4][:, :]).then_inc(S["tt_out"], 1)
                            act.wait_ge(S["p_new"], LEVELS * c + l + 1)
                            p_blocks()
                        for q in range(NC):
                            act.wait_ge(S["rhs_done"], NC * c + q + 1)
                            A.copy(R[:, :], B[4][:, 0:CH]).then_inc(S["rhs_out"], 1)
                            act.wait_ge(S["u_done"], NC * c + q + 1)
                            A.copy(VU[UR[0], q, 0, :], B[5][UR[0], 0:CH]).then_inc(S["u_out0"], 1)
                        act.wait_ge(S["y_done"], c + 1)
                        A.copy(y, B[7][:, :]).then_inc(S["y_out"], 1)
                        act.wait_ge(S["yc_done"], c + 1)
                        A.activation(yc2, yc, ACT.Square).then_inc(S["yc2_done"], 1)
                        act.wait_ge(S["var_recip"], c + 1)
                        A.activation(rn, rn, ACT.Sqrt).then_inc(S["rstd_done"], 1)
                    turns(act, "act", body)

                @block.gpsimd
                def _(pool):
                    for t4 in (PB, TB, AB, MB):
                        nc.gpsimd.memset(t4[:, :, :, :], 0.0).then_inc(S["zeroed"], 1)
                    nc.gpsimd.memset(SB[:, :, :, :], 0.0).then_inc(S["zeroed"], 1)
                    nc.gpsimd.memset(LB[:, :, :, :, :], 0.0).then_inc(S["zeroed"], 1)
                    pool.wait_ge(S["zeroed"], 6)

                    def body(c, chain):
                        G = nc.gpsimd
                        pool.wait_ge(S["dc_done"], c + 1)
                        G.tensor_tensor(Dp, Dc, d, ALU.subtract).then_inc(S["dp_done"], 1)
                        pool.wait_ge(S["lt_done"], 4 * c + 4)
                        for l in range(LEVELS):
                            wait(pool, S["tt_done"], LEVELS * c + l - 1)
                            for hh in range(2):
                                m = con[HR[hh], CON["levels"] + (l + 1) * CH:CON["levels"] + (l + 2) * CH].unsqueeze(1).to_broadcast([CH, NC, CH])
                                G.tensor_tensor(LB[HR[hh], l % 2, :, hh, :], LT[HR[hh], :, :], m, ALU.mult).then_inc(S["lb_done"], 1)
                    turns(pool, "pool", body)

                @block.vector
                def _(dve):
                    def body(c, chain):
                        X = nc.vector
                        if isinstance(c, int):
                            dve.wait_ge(S["zeroed"], 6)
                        dve.wait_ge(S["lora_ev"], 3 * c + 2)
                        chain(X.tensor_tensor_scan(D, C("reset", T), d, 0.0, ALU.mult, ALU.add))
                        mid = CH // 2 - 1
                        X.tensor_tensor(ch(Dc), ch(D), ch(D)[:, :, mid:mid + 1].to_broadcast([P, NC, CH]), ALU.subtract).then_inc(S["dc_done"], 1)
                        chain(X.tensor_scalar(kk, dyn(kT, c), V("k_k", c), None, ALU.mult))
                        X.tensor_tensor(kk2, kk, kk, ALU.mult).then_inc(S["kk2_done"], 1)
                        chain(X.tensor_scalar(kp, rate, -1.0, V("k_a", c), ALU.add, ALU.mult))
                        chain(X.scalar_tensor_tensor(out=kp, in0=kp, scalar=1.0, in1=dyn(kT, c), op0=ALU.add, op1=ALU.mult))
                        X.scalar_tensor_tensor(out=rk, in0=dyn(rT, c), scalar=V("r_k", c), in1=kp, op0=ALU.mult, op1=ALU.mult).then_inc(S["rk_done"], 1)
                        dve.wait_ge(S["dc_done"], c + 1)
                        X.tensor_tensor(gs[:, 0:NC - 1], ch(Dc)[:, 0:NC - 1, CH - 1], ch(D)[:, 1:NC, mid], ALU.add).then_inc(S["gs_done"], 1)
                        dve.wait_ge(S["ss_done"], c + 1)
                        X.tensor_scalar(rn, B[3][:, :], 1e-24, None, ALU.max).then_inc(S["rn_recip"], 1)
                        dve.wait_ge(S["rn_recip"], 2 * c + 1)
                        X.reciprocal(rn, rn).then_inc(S["rn_recip"], 1)
                        dve.wait_ge(S["bonus_done"], c + 1)
                        X.tensor_tensor(bonus, B[4][:, :], dyn(vT, c), ALU.mult).then_inc(S["bonus_out"], 1)
                        dve.wait_ge(S["rn_done"], c + 1)
                        chain(X.tensor_tensor(kk, kk, rn, ALU.mult))
                        chain(X.tensor_tensor(b1, kk, rate, ALU.mult))
                        dve.wait_ge(S["exps"], 3 * c + 3)
                        X.tensor_tensor(KB[HR[0], :, 0, :], ch(kp)[HR[0], :, :], ch(eK)[HR[0], :, :], ALU.mult).then_inc(S["kb_done"], 1)
                        X.tensor_tensor(KB[HR[0], :, 1, :], ch(b1)[HR[0], :, :], ch(eK)[HR[0], :, :], ALU.mult).then_inc(S["kb_done"], 1)
                        X.tensor_tensor(KB[HR[1], :, 0, :], ch(b1)[HR[1], :, :], ch(eK)[HR[1], :, :], ALU.mult).then_inc(S["kb_done"], 1)
                        X.tensor_tensor(KB[HR[1], :, 1, :], ch(kp)[HR[1], :, :], ch(eK)[HR[1], :, :], ALU.mult).then_inc(S["kb_done"], 1)
                        X.scalar_tensor_tensor(out=AR[:, :, 0, :], in0=ch(kk), scalar=-1.0, in1=ch(eA), op0=ALU.mult, op1=ALU.mult).then_inc(S["ar_done"], 1)
                        X.tensor_tensor(AR[:, :, 1, :], dyn(rT, c).rearrange("p (c s) -> p c s", s=CH), ch(eR), ALU.mult).then_inc(S["ar_done"], 1)
                        dve.wait_ge(S["ar_done"], 2 * c + 1)
                        for hh in range(2):
                            chain(X.tensor_copy(AB[HR[hh], :, 1 - hh, :], AR[HR[hh], :, 0, :]))
                        dve.wait_ge(S["gram_done"], c + 1)
                        bank = [B[i][:, :].rearrange("p (c n) -> p c n", n=P) for i in range(4)]

                        def mask(name, rows):
                            return C(name, CH, rows).unsqueeze(1).to_broadcast([rows.stop - rows.start, 4, CH])
                        for i in range(4):
                            hh, qs = i // 2, slice(4 * (i % 2), 4 * (i % 2) + 4)
                            X.tensor_tensor(LT[UR[hh], qs, :], bank[i][UR[hh], :, 0:CH], mask("strict", UR[hh]), ALU.mult).then_inc(S["lt_done"], 1)
                        dve.wait_ge(S["lt_done"], 4 * c + 4)
                        chain(X.tensor_tensor(ch(prob), LT[:, :, :], con[:, CON["levels"]:CON["levels"] + CH].unsqueeze(1).to_broadcast([P, NC, CH]), ALU.mult))
                        X.tensor_tensor(ch(prob), ch(prob), C("ident64", CH).unsqueeze(1).to_broadcast([P, NC, CH]), ALU.add).then_inc(S["p_ready"], 1)
                        for i in range(4):
                            hh, qs = i // 2, slice(4 * (i % 2), 4 * (i % 2) + 4)
                            X.tensor_tensor(MB[VR[hh], qs, 1 - hh, :], bank[i][VR[hh], :, 0:CH], mask("strict", VR[hh]), ALU.mult).then_inc(S["gram_out"], 1)
                            X.tensor_tensor(RKB[:, qs, hh, :], bank[i][:, :, CH:P], mask("incl", slice(0, P)), ALU.mult).then_inc(S["gram_out"], 1)
                        for l in range(LEVELS):
                            dve.wait_ge(S["tt_out"], LEVELS * c + l + 1)
                            for hh in range(2):
                                X.tensor_copy(TB[HR[hh], :, hh, :], ch(tt)[HR[hh], :, :]).then_inc(S["tb_done"], 1)
                            if l < LEVELS - 1:
                                dve.wait_ge(S["xl_done"], (LEVELS - 1) * c + l + 1)
                                X.tensor_tensor(inv, inv, B[6][:, :], ALU.add).then_inc(S["x_new"], 1)
                            dve.wait_ge(S["pl_done"], LEVELS * c + l + 1)
                            X.tensor_tensor(prob, prob, B[5][:, :], ALU.add).then_inc(S["p_new"], 1)
                        dve.wait_ge(S["gs_exp"], c + 1)
                        for q in range(NC):
                            dve.wait_ge(S["u_done"], NC * c + q + 1)
                            X.tensor_copy(VU[UR[1], q, 1, :], B[5][UR[1], 0:CH]).then_inc(S["u_out1"], 1)
                            if q < NC - 1:
                                if q > 0:
                                    dve.wait_ge(S["s_new"], (NC - 1) * c + q)
                                    chain(X.tensor_scalar(Sg[:, :], Sp[:, q % 2, :], gs[:, q:q + 1], None, ALU.mult))
                                dve.wait_ge(S["s_done"], (NC - 1) * c + q + 1)
                                if q == 0:
                                    X.tensor_scalar(Sp[:, 1, :], B[6][:, 0:CH], gs[:, 0:1], None, ALU.mult).then_inc(S["s_new"], 1)
                                else:
                                    X.scalar_tensor_tensor(out=Sp[:, (q + 1) % 2, :], in0=B[6][:, 0:CH], scalar=gs[:, q:q + 1],
                                                           in1=Sg[:, :], op0=ALU.mult, op1=ALU.add).then_inc(S["s_new"], 1)
                                dve.wait_ge(S["s_new"], (NC - 1) * c + q + 1)
                                for hh in range(2):
                                    X.tensor_copy(SB[HR[hh], (q + 1) % 2, hh, :], Sp[HR[hh], (q + 1) % 2, :]).then_inc(S["sb_done"], 1)
                        dve.wait_ge(S["mu_done"], c + 1)
                        X.tensor_tensor(yc, y, B[0][:, :], ALU.subtract).then_inc(S["yc_done"], 1)
                        dve.wait_ge(S["var_done"], c + 1)
                        chain(X.tensor_scalar(rn, B[1][:, :], GN_EPS, None, ALU.add))
                        X.reciprocal(rn, rn).then_inc(S["var_recip"], 1)
                        dve.wait_ge(S["rstd_done"], c + 1)
                        chain(X.tensor_tensor(out_t, yc, rn, ALU.mult))
                        chain(X.tensor_scalar(out_t, out_t, V("ln_w", c), V("ln_b", c), ALU.mult, ALU.add))
                        dve.wait_ge(S["bonus_out"], c + 1)
                        chain(X.tensor_tensor(out_t, out_t, bonus, ALU.add))
                        chain(X.tensor_tensor(out_t, out_t, gate, ALU.mult))
                        X.tensor_copy(dyn(ohi, c), out_t).then_inc(S["out_hi"], 1)
                        dve.wait_ge(S["out_hi"], c + 1)
                        X.tensor_tensor(dyn(olo, c), out_t, dyn(ohi, c).bitcast(F32), ALU.subtract).then_inc(S["out_lo"], 1)
                    turns(dve, "dve", body)

        def finish(norm=True):
            with phase() as st:
                sq, rstd = sbuf(st, "f_sq", [P, 2, T]), sbuf(st, "f_rstd", [P, T])
                out = sbuf(st, "f_out", [P, KD, T])
                ps_n = psum(st, "f_ss")
                s = norm_sems("f")
                stored = sem("stored")
                block = st.enter_context(nc.Block(no_gpsimd_drain=True))

                @block.scalar
                def _(act):
                    norm_act(act, s, KD, xk, sq)
                    norm_act_sqrt(act, s, rstd)

                @block.tensor
                def _(pe):
                    norm_pe(pe, s, KD, sq, ps_n)

                @block.vector
                def _(dve):
                    norm_dve(dve, s, KD, ps_n, rstd)
                    dve.wait_ge(s["rstd"], 1)
                    for k in range(KD):
                        if norm:
                            nc.vector.scalar_tensor_tensor(out=out[:, k, :], in0=xk(k), scalar=V("norm_final", k), in1=rstd[:, :],
                                                           op0=ALU.mult, op1=ALU.mult).then_inc(s["hn"], 1)
                        else:
                            nc.vector.tensor_copy(out[:, k, :], xk(k)).then_inc(s["hn"], 1)

                @block.sync
                def _(sp):
                    for k in range(KD):
                        sp.wait_ge(s["hn"], k + 1)
                        sp.dma_start(a["out"][:, k, :], out[:, k, :]).then_inc(stored, 16)
                    sp.wait_ge(stored, 16 * KD)

        attention()
        if stop != "attn":
            conv_glu("f0", 0, a["ffn_in0"], a["ffn_out0"])
            if stop != "ffn0":
                rwkv()
                if stop != "rwkv":
                    conv_glu("f1", 1, a["ffn_in1"], a["ffn_out1"])
        finish(stop == "all")


def constant_matrices():
    c = np.zeros((P, NCON), np.float32)

    def put(name, m):
        c[:, CON[name]:CON[name] + m.shape[1]] = m
    i, j = np.arange(P)[:, None], np.arange(P)[None, :]
    put("ones", np.ones((P, P)))
    half = ROPE // 2
    first = j % ROPE < half
    put("rot", np.where(first & (i == j + half), -1.0, 0.0) + np.where(~first & (i == j - half), 1.0, 0.0))
    put("ident", np.eye(P))
    put("causal", np.where(j > i, NEG, 0.0))
    put("headsum", (i // RN == j // RN) * 1.0)
    put("headmean", (i // RN == j // RN) / RN)
    s, t = np.arange(P)[:, None] % CH, np.arange(CH)[None, :]
    put("incl", (s <= t) * 1.0)
    put("strict", (s < t) * 1.0)
    put("ident64", (s == t) * 1.0)
    put("levels", np.concatenate([(s // (2 * m) == t // (2 * m)) & (s // m % 2 == 0) & (t // m % 2 == 1)
                                  for m in (1, 2, 4, 8, 16, 32)], axis=1) * 1.0)
    put("reset", np.broadcast_to(np.arange(T)[None, :] % CH != 0, (P, T)) * 1.0)
    return c


def kernel(**inputs):
    import numpy as _np
    import concourse.bacc as _bacc
    from concourse import mybir as _mybir
    from concourse.bass_utils import run_bass_kernel_spmd as _run

    g = {k: _np.asarray(v) for k, v in inputs.items()}

    def tiles(w, m=P):
        k, n = w.shape
        return w.reshape(k // P, P, n // m, m).transpose(2, 1, 0, 3).reshape(n // m, P, k // P * m)

    def chan(v):
        return v.reshape(-1, P).T

    half = ROPE // 2
    inv_freq = (_np.float32(10000.0) ** (-_np.arange(half, dtype=_np.float32) / _np.float32(half))).astype(_np.float32)
    vec = _np.concatenate([chan(g["norm_mix"]), chan(g["norm_ffn"]), chan(g["norm_final"]), chan(g["mla_q_norm"]), chan(g["mla_kv_norm"]),
                           chan(g["rwkv_mix"]), chan(g["rwkv_w0"]), chan(g["rwkv_a0"]), chan(g["rwkv_k_k"]), chan(g["rwkv_k_a"]),
                           chan(g["rwkv_r_k"]), chan(g["rwkv_ln_w"]), chan(g["rwkv_ln_b"]), chan(g["ffn_conv_w"]), chan(g["ffn_conv_b"]),
                           _np.tile(inv_freq, P // half)[:, None]], axis=1)
    w_in = g["mla_w_in"][0]
    rope_cols = w_in[:, QL + KVL:]
    w_lat = tiles(_np.concatenate([w_in[:, :QL + KVL], rope_cols, rope_cols], axis=1))
    uq = g["mla_w_uq"][0].reshape(QL, HEADS, NOPE + ROPE)
    ukv = g["mla_w_ukv"][0].reshape(KVL, HEADS, NOPE + VDIM)
    w_pair = _np.concatenate([tiles(uq[:, :, :NOPE].reshape(QL, -1), 2 * NOPE), tiles(uq[:, :, NOPE:].reshape(QL, -1), 2 * ROPE),
                              tiles(ukv[:, :, :NOPE].reshape(KVL, -1), 2 * NOPE), tiles(ukv[:, :, NOPE:].reshape(KVL, -1), 2 * VDIM)], axis=2)
    lora_out = _np.zeros((KD, P, 4 * P), _np.float32)
    lora_out[:, :LW, 0:P] = g["rwkv_w2"][0].reshape(LW, KD, P).transpose(1, 0, 2)
    lora_out[:, :LW, P:2 * P] = g["rwkv_a2"][0].reshape(LW, KD, P).transpose(1, 0, 2)
    g2 = g["rwkv_g2"][0].reshape(LG, KD, P).transpose(1, 0, 2)
    lora_out[:, :, 2 * P:3 * P] = g2[:, :P]
    lora_out[:, :LG - P, 3 * P:4 * P] = g2[:, P:]
    arrays = {
        "x": g["x"][0].T.reshape(KD, P, T).transpose(1, 0, 2),
        "positions": _np.broadcast_to(g["positions"][0][None, :], (P, T)),
        "vec": vec, "con": constant_matrices(),
        "w_lat": w_lat, "w_pair": w_pair, "w_attn_out": tiles(g["mla_w_o"][0]),
        "lora_in": tiles(_np.concatenate([g["rwkv_w1"][0], g["rwkv_a1"][0], g["rwkv_g1"][0]], axis=1), 2 * LW + LG)[0],
        "w_rkv": _np.concatenate([tiles(g["rwkv_w_rkv"][0, n]) for n in (1, 0, 2)]),
        "lora_out": lora_out, "w_rwkv_out": tiles(g["rwkv_w_o"][0]),
    }
    for layer in range(2):
        w = g["ffn_w_in"][layer]
        arrays[f"ffn_in{layer}"] = _np.concatenate([tiles(w[:, :DFF]), tiles(w[:, DFF:])], axis=2)
        wo = g["ffn_w_out"][layer]
        arrays[f"ffn_out{layer}"] = _np.concatenate([tiles(wo[:DFF // 2]), tiles(wo[DFF // 2:])])
    arrays = {k: _np.ascontiguousarray(v) for k, v in arrays.items()}
    nc = _bacc.Bacc("TRN2", target_bir_lowering=False, num_devices=1)
    aps = {k: nc.dram_tensor(f"in_{k}", v.shape, _mybir.dt.from_np(v.dtype), kind="ExternalInput").ap() for k, v in arrays.items()}
    aps["out"] = nc.dram_tensor("out", (P, KD, T), _mybir.dt.float32, kind="ExternalOutput").ap()
    trunk(nc, aps)
    r = _run(nc, [{f"in_{k}": v for k, v in arrays.items()}], core_ids=[0])
    out = r.results[0]["out"]
    return _np.ascontiguousarray(out.transpose(2, 1, 0).reshape(1, T, D))
```

```python
from contextlib import ExitStack, contextmanager

import numpy as np

import concourse.bass as bass
from concourse import mybir

F32 = mybir.dt.float32
F32R = mybir.dt.float32r
I32 = mybir.dt.int32
ALU = mybir.AluOpType
ACT = mybir.ActivationFunctionType
AX_X = mybir.AxisListType.X

P = 128
T = 512
D = 1024
KD = D // P
NORM_EPS = 1e-6
HEADS, NOPE, ROPE, VDIM = 8, 128, 64, 128
QL, KVL = 384, 256
KQ, KKV = QL // P, KVL // P
QB = T // P
SCALE = float(NOPE + ROPE) ** -0.5
NEG = -1.0e30
RH, RN = 16, 64
GN_EPS = 64e-5
CH = 64
NC = T // CH
LW, LG = 64, 160
DFF = 2816
HALF = DFF // P // 2
KAPPA = float(np.exp(-0.5))
SLOT = 3 * 2 * P + 3 * P + 2 * 2 * P + 2 * 2 * P

VEC = {}
_at = 0
for _name, _n in (("norm_mix", 2 * KD), ("norm_ffn", 2 * KD), ("norm_final", KD), ("q_norm", KQ), ("kv_norm", KKV),
                  ("mix", 6 * KD), ("w0", KD), ("a0", KD), ("k_k", KD), ("k_a", KD), ("r_k", KD), ("ln_w", KD),
                  ("ln_b", KD), ("conv_w", 2 * 3 * 2 * HALF), ("conv_b", 2 * 2 * HALF), ("inv_freq", 1)):
    VEC[_name] = _at
    _at += _n
NVEC = _at
CON = {}
_at = 0
for _name, _n in (("ones", P), ("rot", P), ("ident", P), ("causal", P), ("headsum", P), ("headmean", P),
                  ("incl", CH), ("strict", CH), ("ident64", CH), ("levels", 6 * CH), ("reset", T)):
    CON[_name] = _at
    _at += _n
NCON = _at


class Item:

    def __init__(self, t, tpar, j0, thalf):
        self.t, self.j = t, j0 + t
        self.slot = (j0 + tpar) % 2
        self.turn = thalf + (j0 + tpar) // 2
        self.args = (t, tpar, j0, thalf)

    @property
    def prev(self):
        t, tpar, j0, thalf = self.args
        return Item(t - 1, tpar - 1, j0, thalf)


def items(eng, n, j0):
    lead = 2 + n % 2
    for t in range(lead):
        yield Item(t, t, j0, 0)
    if n > lead:
        with eng.Fori(0, (n - lead) // 2) as i:
            for b in range(2):
                yield Item(lead + b + 2 * i, lead + b, j0, i)


def wait(eng, sem, value):
    if isinstance(value, int) and value <= 0:
        return
    eng.wait_ge(sem, value)


class Chain:

    def __init__(self, eng, sem, base=0):
        self.eng, self.sem, self.base, self.n = eng, sem, base, 0

    def __call__(self, ins):
        ins.then_inc(self.sem, 1)
        self.n += 1
        self.eng.wait_ge(self.sem, self.base + self.n)


def trunk(nc, a, stop="all"):
    with ExitStack() as outer:
        scopes = [[]]

        @contextmanager
        def phase():
            scopes.append([])
            with ExitStack() as stack:
                yield stack
            used = scopes.pop()
            if used:
                nc.clear_and_free_semaphores(used)
                nc.all_engine_barrier()

        def sem(name):
            s = nc.alloc_semaphore(name=name)
            scopes[-1].append(s)
            return s

        def sbuf(stack, name, shape, dt=F32):
            return stack.enter_context(nc.sbuf_tensor(name, shape, dt))

        def psum(stack, name, shape=(P, 512)):
            return stack.enter_context(nc.psum_tensor(name, list(shape), F32))

        x = sbuf(outer, "x_resid", [P, KD, T])
        vec = sbuf(outer, "vec", [P, NVEC])
        con = sbuf(outer, "con", [P, NCON])
        raw = [sbuf(outer, f"w_raw{b}", [P, SLOT]) for b in range(2)]
        whi, wlo = [None, None], [None, None]

        def ring(stack, tag):
            for b in range(2):
                whi[b] = sbuf(stack, f"{tag}_w_hi{b}", [P, SLOT], F32R)
                wlo[b] = sbuf(stack, f"{tag}_w_lo{b}", [P, SLOT], F32R)

        w_loaded = [sem("w_loaded0"), sem("w_loaded1")]
        w_hi_ready, w_lo_ready, w_used = sem("w_hi_ready"), sem("w_lo_ready"), sem("w_used")
        x_loaded, con_loaded = sem("x_loaded"), sem("con_loaded")

        def C(name, n=P, rows=slice(0, P)):
            return con[rows, CON[name]:CON[name] + n]

        def V(name, k):
            if isinstance(k, int):
                return vec[:, VEC[name] + k:VEC[name] + k + 1]
            return vec[:, bass.ds(k + VEC[name], 1)]

        def load(sp, it, src, n):
            wait(sp, w_lo_ready, it.j - 1)
            sp.dma_start(raw[it.slot][:, 0:n], src).then_inc(w_loaded[it.slot], 16)

        def split_hi(act, it, n):
            act.wait_ge(w_loaded[it.slot], 16 * it.turn + 16)
            wait(act, w_used, it.j - 1)
            nc.scalar.copy(whi[it.slot][:, 0:n], raw[it.slot][:, 0:n]).then_inc(w_hi_ready, 1)

        def split_lo(pool, it, n):
            pool.wait_ge(w_loaded[it.slot], 16 * it.turn + 16)
            pool.wait_ge(w_hi_ready, it.j + 1)
            nc.gpsimd.tensor_tensor(wlo[it.slot][:, 0:n], raw[it.slot][:, 0:n],
                                    whi[it.slot][:, 0:n].bitcast(F32), ALU.subtract).then_inc(w_lo_ready, 1)

        def three(out, w_at, m, rhs_hi, rhs_lo, slot, start, stop):
            wh, wl = whi[slot][:, w_at:w_at + m], wlo[slot][:, w_at:w_at + m]
            nc.tensor.matmul(out, wh, rhs_hi, start=start, stop=False)
            nc.tensor.matmul(out, wh, rhs_lo, start=False, stop=False)
            return nc.tensor.matmul(out, wl, rhs_hi, start=False, stop=stop)

        def norm_sems(tag):
            return {n: sem(f"{tag}_{n}") for n in ("sq", "ss_used", "ss", "mean", "recip", "rstd", "hn", "hi", "lo")}

        def norm_act(act, s, n, src, sq):
            for k in range(n):
                wait(act, s["ss_used"], k - 1)
                nc.scalar.activation(sq[:, k % 2, :], src(k), ACT.Square).then_inc(s["sq"], 1)

        def norm_act_sqrt(act, s, rstd):
            act.wait_ge(s["recip"], 1)
            nc.scalar.activation(rstd[:, :], rstd[:, :], ACT.Sqrt).then_inc(s["rstd"], 1)

        def norm_pe(pe, s, n, sq, ps):
            for k in range(n):
                pe.wait_ge(s["sq"], k + 1)
                last = nc.tensor.matmul(ps[:, :], C("ones"), sq[:, k % 2, :], start=k == 0, stop=k == n - 1)
                last.then_inc(s["ss_used"], 1)

        def norm_dve(dve, s, n, ps, rstd):
            dve.wait_ge(s["ss_used"], n)
            nc.vector.tensor_scalar(rstd[:, :], ps[:, :], 1.0 / (n * P), NORM_EPS, ALU.mult, ALU.add).then_inc(s["mean"], 1)
            dve.wait_ge(s["mean"], 1)
            nc.vector.reciprocal(rstd[:, :], rstd[:, :]).then_inc(s["recip"], 1)

        def normed_split_dve(dve, s, n, src, gain, rstd, hn):
            dve.wait_ge(s["rstd"], 1)
            for k in range(n):
                wait(dve, s["lo"], k - 1)
                nc.vector.scalar_tensor_tensor(out=hn[:, k % 2, :], in0=src(k), scalar=gain(k), in1=rstd[:, :],
                                               op0=ALU.mult, op1=ALU.mult).then_inc(s["hn"], 1)

        def normed_split_act(act, s, n, hn, hi):
            for k in range(n):
                act.wait_ge(s["hn"], k + 1)
                nc.scalar.copy(hi(k), hn[:, k % 2, :]).then_inc(s["hi"], 1)

        def normed_split_pool(pool, s, n, hn, hi, lo):
            for k in range(n):
                pool.wait_ge(s["hi"], k + 1)
                pool.wait_ge(s["hn"], k + 1)
                nc.gpsimd.tensor_tensor(lo(k), hn[:, k % 2, :], hi(k).bitcast(F32), ALU.subtract).then_inc(s["lo"], 1)

        def xk(k):
            return x[:, k, :] if isinstance(k, int) else x[:, bass.ds(k, 1), :].rearrange("p a t -> p (a t)")

        def dyn(t3, k):
            return t3[:, k, :] if isinstance(k, int) else t3[:, bass.ds(k, 1), :].rearrange("p a t -> p (a t)")

        j_used = [0]

        def project_residual(tag, w, ohi, olo, o=None):
            j0 = j_used[0]
            n = KD * P
            with phase() as st:
                ring(st, tag)
                ps = [psum(st, f"{tag}_ps{b}") for b in range(2)]
                free, o_hi, o_lo = sem(f"{tag}_added"), sem(f"{tag}_o_hi"), sem(f"{tag}_o_lo")
                block = st.enter_context(nc.Block(no_gpsimd_drain=True))

                @block.sync
                def _(sp):
                    for it in items(sp, KD, j0):
                        load(sp, it, w[bass.ds(it.t, 1), :, :].rearrange("a p n -> p (a n)"), n)

                @block.scalar
                def _(act):
                    if o is not None:
                        for k in range(KD):
                            nc.scalar.copy(ohi[:, k, :], o[:, k, :]).then_inc(o_hi, 1)
                    for it in items(act, KD, j0):
                        split_hi(act, it, n)

                @block.gpsimd
                def _(pool):
                    for it in items(pool, KD, j0):
                        split_lo(pool, it, n)

                @block.tensor
                def _(pe):
                    for it in items(pe, KD, j0):
                        pe.wait_ge(w_lo_ready, it.j + 1)
                        wait(pe, free, it.t - 1)
                        for k in range(KD):
                            if o is not None and isinstance(it.t, int) and it.t == 0:
                                pe.wait_ge(o_lo, k + 1)
                            last = three(ps[it.slot][:, :], k * P, P, ohi[:, k, :], olo[:, k, :], it.slot, k == 0, k == KD - 1)
                        last.then_inc(w_used, 1)

                @block.vector
                def _(dve):
                    if o is not None:
                        for k in range(KD):
                            dve.wait_ge(o_hi, k + 1)
                            nc.vector.tensor_tensor(olo[:, k, :], o[:, k, :], ohi[:, k, :].bitcast(F32), ALU.subtract).then_inc(o_lo, 1)
                    for it in items(dve, KD, j0):
                        dve.wait_ge(w_used, it.j + 1)
                        nc.vector.tensor_tensor(xk(it.t), ps[it.slot][:, :], xk(it.t), ALU.add).then_inc(free, 1)
            j_used[0] += KD

        def conv_glu(tag, layer, w_in, w_out):
            jb = j_used[0]
            n_in, n_out = 2 * KD * P, HALF * P
            with phase() as st:
                ring(st, tag)
                sq, rstd = sbuf(st, f"{tag}_sq", [P, 2, T]), sbuf(st, f"{tag}_rstd", [P, T])
                hn = sbuf(st, f"{tag}_hn", [P, 2, T])
                hhi, hlo = sbuf(st, f"{tag}_hhi", [P, KD, T], F32R), sbuf(st, f"{tag}_hlo", [P, KD, T], F32R)
                ahi, alo = sbuf(st, f"{tag}_ahi", [P, HALF, T], F32R), sbuf(st, f"{tag}_alo", [P, HALF, T], F32R)
                cv, sl = sbuf(st, f"{tag}_conv", [P, 2, T]), sbuf(st, f"{tag}_silu", [P, 2, T])
                ga = sbuf(st, f"{tag}_act", [P, 2, T])
                ps_g = [psum(st, f"{tag}_gate{b}") for b in range(2)]
                ps_u = [psum(st, f"{tag}_up{b}") for b in range(2)]
                ps_y = [psum(st, f"{tag}_y{b}") for b in range(2)]
                ps_n = psum(st, f"{tag}_ss")
                s = norm_sems(tag)
                tap2, tap1, conv_done, silu_done, gated, act_hi, act_lo, added = (
                    sem(f"{tag}_{n}") for n in ("tap2", "tap1", "conv_done", "silu_done", "gated", "act_hi", "act_lo", "added"))
                block = st.enter_context(nc.Block(no_gpsimd_drain=True))
                per_half = HALF + KD

                def halves():
                    for hf in range(2):
                        j0 = jb + hf * per_half
                        yield hf, j0, j0 + HALF, hf * HALF, hf * KD

                @block.sync
                def _(sp):
                    for hf, ji, jo, tb, ob in halves():
                        for it in items(sp, HALF, ji):
                            load(sp, it, w_in[bass.ds(it.t + tb, 1), :, :].rearrange("a p n -> p (a n)"), n_in)
                        for it in items(sp, KD, jo):
                            load(sp, it, w_out[bass.ds(it.t + ob, 1), :, :].rearrange("a p n -> p (a n)"), n_out)

                @block.gpsimd
                def _(pool):
                    normed_split_pool(pool, s, KD, hn, lambda k: hhi[:, k, :], lambda k: hlo[:, k, :])
                    for hf, ji, jo, tb, ob in halves():
                        for it in items(pool, HALF, ji):
                            split_lo(pool, it, n_in)
                        for it in items(pool, KD, jo):
                            split_lo(pool, it, n_out)

                def conv_act(act, it, tb):
                    u = it.t + tb
                    act.wait_ge(w_used, it.j + 1)
                    wait(act, silu_done, u - 1)
                    nc.scalar.activation(cv[:, it.slot, :], ps_g[it.slot][:, :], ACT.Identity,
                                         scale=V("conv_w", u + (layer * 3 + 2) * 2 * HALF),
                                         bias=V("conv_b", u + layer * 2 * HALF)).then_inc(tap2, 1)
                    act.wait_ge(conv_done, u + 1)
                    wait(act, gated, u - 1)
                    nc.scalar.activation(sl[:, it.slot, :], cv[:, it.slot, :], ACT.Silu).then_inc(silu_done, 1)

                @block.scalar
                def _(act):
                    norm_act(act, s, KD, xk, sq)
                    norm_act_sqrt(act, s, rstd)
                    normed_split_act(act, s, KD, hn, lambda k: hhi[:, k, :])
                    for hf, ji, jo, tb, ob in halves():
                        for it in items(act, HALF, ji):
                            split_hi(act, it, n_in)
                            if not (isinstance(it.t, int) and it.t == 0):
                                conv_act(act, it.prev, tb)
                        conv_act(act, Item(HALF - 1, HALF - 1, ji, 0), tb)
                        for it in items(act, KD, jo):
                            split_hi(act, it, n_out)

                @block.vector
                def _(dve):
                    norm_dve(dve, s, KD, ps_n, rstd)
                    normed_split_dve(dve, s, KD, xk, lambda k: V("norm_ffn", layer * KD + k), rstd, hn)
                    for hf, ji, jo, tb, ob in halves():
                        for it in items(dve, HALF, ji):
                            u, b = it.t + tb, it.slot
                            dve.wait_ge(tap2, u + 1)
                            nc.vector.scalar_tensor_tensor(
                                out=cv[:, b, 1:T], in0=ps_g[b][:, 0:T - 1], scalar=V("conv_w", u + (layer * 3 + 1) * 2 * HALF),
                                in1=cv[:, b, 1:T], op0=ALU.mult, op1=ALU.add).then_inc(tap1, 1)
                            dve.wait_ge(tap1, u + 1)
                            nc.vector.scalar_tensor_tensor(
                                out=cv[:, b, 2:T], in0=ps_g[b][:, 0:T - 2], scalar=V("conv_w", u + (layer * 3) * 2 * HALF),
                                in1=cv[:, b, 2:T], op0=ALU.mult, op1=ALU.add).then_inc(conv_done, 1)
                            dve.wait_ge(silu_done, u + 1)
                            wait(dve, act_lo, u - 1)
                            nc.vector.tensor_tensor(ga[:, b, :], ps_u[b][:, :], sl[:, b, :], ALU.mult).then_inc(gated, 1)
                            dve.wait_ge(gated, u + 1)
                            nc.vector.tensor_copy(dyn(ahi, it.t), ga[:, b, :]).then_inc(act_hi, 1)
                            dve.wait_ge(act_hi, u + 1)
                            nc.vector.tensor_tensor(dyn(alo, it.t), ga[:, b, :], dyn(ahi, it.t).bitcast(F32),
                                                    ALU.subtract).then_inc(act_lo, 1)
                        for it in items(dve, KD, jo):
                            dve.wait_ge(w_used, it.j + 1)
                            nc.vector.tensor_tensor(xk(it.t), ps_y[it.slot][:, :], xk(it.t), ALU.add).then_inc(added, 1)

                @block.tensor
                def _(pe):
                    norm_pe(pe, s, KD, sq, ps_n)
                    for hf, ji, jo, tb, ob in halves():
                        for it in items(pe, HALF, ji):
                            b = it.slot
                            pe.wait_ge(w_lo_ready, it.j + 1)
                            wait(pe, gated, it.t + tb - 1)
                            for k in range(KD):
                                if hf == 0 and isinstance(it.t, int) and it.t == 0:
                                    pe.wait_ge(s["lo"], k + 1)
                                three(ps_g[b][:, :], k * P, P, hhi[:, k, :], hlo[:, k, :], b, k == 0, k == KD - 1)
                            for k in range(KD):
                                last = three(ps_u[b][:, :], (KD + k) * P, P, hhi[:, k, :], hlo[:, k, :], b, k == 0, k == KD - 1)
                            last.then_inc(w_used, 1)
                        pe.wait_ge(act_lo, tb + HALF)
                        for it in items(pe, KD, jo):
                            b = it.slot
                            pe.wait_ge(w_lo_ready, it.j + 1)
                            wait(pe, added, it.t + ob - 1)
                            for f in range(HALF):
                                last = three(ps_y[b][:, :], f * P, P, ahi[:, f, :], alo[:, f, :], b, f == 0, f == HALF - 1)
                            last.then_inc(w_used, 1)
            j_used[0] += 2 * per_half

        def attention():
            j0 = j_used[0]
            n_lat = KQ + KKV + 1
            NP = HEADS // 2
            with phase() as st:
                cos, sin = sbuf(st, "cos", [P, T]), sbuf(st, "sin", [P, T])
                qhi, qlo = sbuf(st, "qlat_hi", [P, KQ, T], F32R), sbuf(st, "qlat_lo", [P, KQ, T], F32R)
                chi, clo = sbuf(st, "clat_hi", [P, KKV, T], F32R), sbuf(st, "clat_lo", [P, KKV, T], F32R)
                krope = sbuf(st, "krope", [P, T])
                ohi, olo = sbuf(st, "attn_ohi", [P, HEADS, T], F32R), sbuf(st, "attn_olo", [P, HEADS, T], F32R)

                with phase() as s1:
                    ring(s1, "m")
                    sq, rstd = sbuf(s1, "m_sq", [P, 2, T]), sbuf(s1, "m_rstd", [P, T])
                    hn = sbuf(s1, "m_hn", [P, 2, T])
                    hhi, hlo = sbuf(s1, "m_hhi", [P, KD, T], F32R), sbuf(s1, "m_hlo", [P, KD, T], F32R)
                    lat = sbuf(s1, "lat", [P, n_lat, T])
                    pos_i, ang, turns, red = sbuf(s1, "pos_i", [P, T], I32), sbuf(s1, "ang", [P, T]), sbuf(s1, "turns", [P, T]), sbuf(s1, "red", [P, T])
                    rq, rc = sbuf(s1, "rstd_q", [P, T]), sbuf(s1, "rstd_c", [P, T])
                    ktmp = sbuf(s1, "ktmp", [P, 2, T])
                    ps = [psum(s1, f"lat_ps{b}") for b in range(2)]
                    ps_n, ps_q, ps_c, ps_r = (psum(s1, f"m_{n}") for n in ("ss", "ssq", "ssc", "krot"))
                    s, sq_s, sc_s = norm_sems("m"), norm_sems("mq"), norm_sems("mc")
                    lat_out, angles, tables, krot, kmul = (sem(n) for n in ("lat_out", "angles", "tables", "krot", "kmul"))
                    pos_loaded = sem("pos_loaded")
                    n = KD * P
                    block = s1.enter_context(nc.Block(no_gpsimd_drain=True))

                    @block.sync
                    def _(sp):
                        sp.dma_start(x[:, :, :], a["x"]).then_inc(x_loaded, 16)
                        sp.dma_start(vec[:, :], a["vec"]).then_inc(con_loaded, 16)
                        sp.dma_start(con[:, :], a["con"]).then_inc(con_loaded, 16)
                        sp.dma_start(pos_i[:, :], a["positions"]).then_inc(pos_loaded, 16)
                        for it in items(sp, n_lat, j0):
                            load(sp, it, a["w_lat"][bass.ds(it.t, 1), :, :].rearrange("a p n -> p (a n)"), n)

                    @block.scalar
                    def _(act):
                        act.wait_ge(x_loaded, 16)
                        norm_act(act, s, KD, xk, sq)
                        norm_act_sqrt(act, s, rstd)
                        normed_split_act(act, s, KD, hn, lambda k: hhi[:, k, :])

                        def out(it):
                            act.wait_ge(w_used, it.j + 1)
                            nc.scalar.copy(dyn(lat, it.t), ps[it.slot][:, :]).then_inc(lat_out, 1)
                        for it in items(act, n_lat, j0):
                            split_hi(act, it, n)
                            if not (isinstance(it.t, int) and it.t == 0):
                                out(it.prev)
                        out(Item(n_lat - 1, n_lat - 1, j0, 0))
                        act.wait_ge(lat_out, n_lat)
                        norm_act(act, sq_s, KQ, lambda k: lat[:, k, :], sq)
                        act.wait_ge(sq_s["ss_used"], KQ)
                        norm_act(act, sc_s, KKV, lambda k: lat[:, KQ + k, :], sq)
                        norm_act_sqrt(act, sq_s, rq)
                        norm_act_sqrt(act, sc_s, rc)
                        normed_split_act(act, sq_s, KQ, hn, lambda k: qhi[:, k, :])
                        normed_split_act(act, sc_s, KKV, hn, lambda k: chi[:, k, :])
                        act.wait_ge(angles, 1)
                        nc.scalar.activation(sin[:, :], turns[:, :], ACT.Sin).then_inc(tables, 1)
                        act.wait_ge(angles, 2)
                        nc.scalar.activation(cos[:, :], red[:, :], ACT.Sin).then_inc(tables, 1)

                    @block.gpsimd
                    def _(pool):
                        normed_split_pool(pool, s, KD, hn, lambda k: hhi[:, k, :], lambda k: hlo[:, k, :])
                        for it in items(pool, n_lat, j0):
                            split_lo(pool, it, n)
                        normed_split_pool(pool, sq_s, KQ, hn, lambda k: qhi[:, k, :], lambda k: qlo[:, k, :])
                        normed_split_pool(pool, sc_s, KKV, hn, lambda k: chi[:, k, :], lambda k: clo[:, k, :])

                    @block.vector
                    def _(dve):
                        dve.wait_ge(con_loaded, 32)
                        dve.wait_ge(x_loaded, 16)
                        norm_dve(dve, s, KD, ps_n, rstd)
                        normed_split_dve(dve, s, KD, xk, lambda k: V("norm_mix", k), rstd, hn)
                        chain = Chain(dve, sem("angle_chain"))
                        dve.wait_ge(pos_loaded, 16)
                        chain(nc.vector.tensor_copy(ang[:, :], pos_i[:, :]))
                        chain(nc.vector.tensor_scalar(ang[:, :], ang[:, :], V("inv_freq", 0), None, ALU.mult))
                        magic = float(3 << 22)
                        step1 = 6.28125
                        step2 = float(np.float32(round((2 * np.pi - step1) * 2 ** 20) / 2 ** 20))
                        step3 = float(np.float32(2 * np.pi - step1 - step2))
                        pi_in = float(np.nextafter(np.float32(np.pi), np.float32(0)))
                        for dst, shift, quarter in ((turns, 0.0, 0.0), (red, 0.25, float(np.pi / 2))):
                            chain(nc.vector.tensor_scalar(dst[:, :], ang[:, :], float(1 / (2 * np.pi)), shift, ALU.mult, ALU.add))
                            chain(nc.vector.tensor_scalar(dst[:, :], dst[:, :], magic, None, ALU.add))
                            chain(nc.vector.tensor_scalar(ktmp[:, 0, :], dst[:, :], magic, None, ALU.subtract))
                            chain(nc.vector.scalar_tensor_tensor(out=dst[:, :], in0=ktmp[:, 0, :], scalar=-step1, in1=ang[:, :], op0=ALU.mult, op1=ALU.add))
                            chain(nc.vector.scalar_tensor_tensor(out=dst[:, :], in0=ktmp[:, 0, :], scalar=-step2, in1=dst[:, :], op0=ALU.mult, op1=ALU.add))
                            chain(nc.vector.scalar_tensor_tensor(out=dst[:, :], in0=ktmp[:, 0, :], scalar=-step3, in1=dst[:, :], op0=ALU.mult, op1=ALU.add))
                            chain(nc.vector.tensor_scalar(dst[:, :], dst[:, :], quarter, pi_in, ALU.add, ALU.min))
                            nc.vector.tensor_scalar(dst[:, :], dst[:, :], -pi_in, None, ALU.max).then_inc(angles, 1)
                        norm_dve(dve, sq_s, KQ, ps_q, rq)
                        norm_dve(dve, sc_s, KKV, ps_c, rc)
                        normed_split_dve(dve, sq_s, KQ, lambda k: lat[:, k, :], lambda k: V("q_norm", k), rq, hn)
                        dve.wait_ge(sq_s["lo"], KQ)
                        normed_split_dve(dve, sc_s, KKV, lambda k: lat[:, KQ + k, :], lambda k: V("kv_norm", k), rc, hn)
                        dve.wait_ge(tables, 2)
                        dve.wait_ge(krot, 1)
                        nc.vector.tensor_tensor(ktmp[:, 0, :], lat[:, n_lat - 1, :], cos[:, :], ALU.mult).then_inc(kmul, 1)
                        nc.vector.tensor_tensor(ktmp[:, 1, :], ps_r[:, :], sin[:, :], ALU.mult).then_inc(kmul, 1)
                        dve.wait_ge(kmul, 2)
                        nc.vector.tensor_tensor(krope[:, :], ktmp[:, 0, :], ktmp[:, 1, :], ALU.add).then_inc(kmul, 1)

                    @block.tensor
                    def _(pe):
                        pe.wait_ge(con_loaded, 32)
                        norm_pe(pe, s, KD, sq, ps_n)
                        for it in items(pe, n_lat, j0):
                            pe.wait_ge(w_lo_ready, it.j + 1)
                            wait(pe, lat_out, it.t - 1)
                            for k in range(KD):
                                if isinstance(it.t, int) and it.t == 0:
                                    pe.wait_ge(s["lo"], k + 1)
                                last = three(ps[it.slot][:, :], k * P, P, hhi[:, k, :], hlo[:, k, :], it.slot, k == 0, k == KD - 1)
                            last.then_inc(w_used, 1)
                        pe.wait_ge(lat_out, n_lat)
                        nc.tensor.matmul(ps_r[:, :], C("rot"), lat[:, n_lat - 1, :], start=True, stop=True).then_inc(krot, 1)
                        norm_pe(pe, sq_s, KQ, sq, ps_q)
                        norm_pe(pe, sc_s, KKV, sq, ps_c)

                with phase() as s2:
                    jp = j0 + n_lat
                    ring(s2, "p")
                    qn, kn = sbuf(s2, "q_nope", [P, 2, T]), sbuf(s2, "k_nope", [P, 2, T])
                    qraw, qr = sbuf(s2, "q_rope_raw", [P, T]), sbuf(s2, "q_rope", [P, T])
                    qcos, qsin = sbuf(s2, "q_cos", [P, T]), sbuf(s2, "q_sin", [P, T])
                    v = sbuf(s2, "v", [P, QB, 2 * VDIM])
                    pexp = sbuf(s2, "p_exp", [P, 2, T])
                    pT = sbuf(s2, "p_T", [P, 2, QB, T])
                    mx, nmx, rs, ri = (sbuf(s2, n, [P, 2 * QB]) for n in ("mx", "nmx", "rowsum", "rinv"))
                    pp = [psum(s2, f"proj_ps{b}") for b in range(2)]
                    sc = [psum(s2, f"score_ps{b}") for b in range(2)]
                    tp = [psum(s2, f"pT_ps{b}") for b in range(2)]
                    op = [psum(s2, f"o_ps{b}") for b in range(2)]
                    S = {n: sem(n) for n in ("proj_done", "proj_out", "rot_done", "qrope_mul", "qrope_done", "score_done", "masked",
                                             "max_done", "nmax_done", "exp_done", "rinv_done", "p_norm", "pT_done", "pT_out",
                                             "o_done", "o_hi", "o_lo")}
                    NPR = 7
                    NB = 2 * QB
                    at_qn, at_qr = 0, KQ * 2 * P
                    at_kn = at_qr + KQ * P
                    at_v = at_kn + KKV * 2 * P
                    block = s2.enter_context(nc.Block(no_gpsimd_drain=True))

                    @block.sync
                    def _(sp):
                        for it in items(sp, NP, jp):
                            load(sp, it, a["w_pair"][bass.ds(it.t, 1), :, :].rearrange("a p n -> p (a n)"), SLOT)

                    @block.gpsimd
                    def _(pool):
                        for it in items(pool, NP, jp):
                            split_lo(pool, it, SLOT)

                    @block.tensor
                    def _(pe):
                        def lat_product(it, step, w_at, kk, hi, lo, stride):
                            for k in range(kk):
                                last = three(pp[step % 2][:, :], w_at + k * stride, P, hi[:, k, :], lo[:, k, :], it.slot,
                                             k == 0, k == kk - 1)
                            last.then_inc(S["proj_done"], 1)

                        def value_product(it, g):
                            for tt in range(2):
                                tok = slice((2 * g + tt) * P, (2 * g + tt + 1) * P)
                                out = pp[(5 + g) % 2][:, tt * 2 * VDIM:(tt + 1) * 2 * VDIM]
                                for k in range(KKV):
                                    wv = slice(at_v + k * 2 * VDIM, at_v + (k + 1) * 2 * VDIM)
                                    nc.tensor.matmul(out, chi[:, k, tok], whi[it.slot][:, wv], start=k == 0, stop=False)
                                    nc.tensor.matmul(out, chi[:, k, tok], wlo[it.slot][:, wv], start=False, stop=False)
                                    last = nc.tensor.matmul(out, clo[:, k, tok], whi[it.slot][:, wv], start=False, stop=k == KKV - 1)
                            return last

                        def scores(t, n):
                            h, i = n // QB, n % QB
                            nk, qs, rows = (i + 1) * P, slice(i * P, (i + 1) * P), slice(h * ROPE, (h + 1) * ROPE)
                            wait(pe, S["exp_done"], NB * t + n - 1)
                            nc.tensor.matmul(sc[n % 2][:, 0:nk], qn[:, h, qs], kn[:, h, 0:nk], start=True, stop=False)
                            nc.tensor.matmul(sc[n % 2][:, 0:nk], qr[rows, qs], krope[rows, 0:nk], start=False,
                                             stop=True).then_inc(S["score_done"], 1)

                        def turn_p(t, n):
                            wait(pe, S["pT_out"], NB * t + n - 1)
                            pe.wait_ge(S["p_norm"], NB * t + n + 1)
                            for kb in range(n % QB + 1):
                                ks = slice(kb * P, (kb + 1) * P)
                                last = nc.tensor.transpose(tp[n % 2][:, ks], pexp[:, n % 2, ks], C("ident"))
                            last.then_inc(S["pT_done"], 1)

                        def value_sum(t, h):
                            pe.wait_ge(S["pT_out"], NB * t + QB * (h + 1))
                            wait(pe, S["o_lo"], 2 * t + h - 1)
                            for kb in range(QB):
                                last = nc.tensor.matmul(op[h][:, kb * P:T], v[:, kb, h * VDIM:(h + 1) * VDIM],
                                                        pT[:, h, kb, kb * P:T], start=kb == 0, stop=kb == QB - 1)
                            last.then_inc(S["o_done"], 1)

                        for it in items(pe, NP, jp):
                            t = it.t
                            pe.wait_ge(w_lo_ready, it.j + 1)
                            wait(pe, S["proj_out"], NPR * t)
                            lat_product(it, 0, at_qn, KQ, qhi, qlo, 2 * P)
                            wait(pe, S["qrope_done"], t)
                            lat_product(it, 1, at_qn + P, KQ, qhi, qlo, 2 * P)
                            pe.wait_ge(S["proj_out"], NPR * t + 1)
                            lat_product(it, 2, at_qr, KQ, qhi, qlo, P)
                            pe.wait_ge(S["proj_out"], NPR * t + 2)
                            lat_product(it, 3, at_kn, KKV, chi, clo, 2 * P)
                            pe.wait_ge(S["proj_out"], NPR * t + 3)
                            lat_product(it, 4, at_kn + P, KKV, chi, clo, 2 * P)
                            pe.wait_ge(S["proj_out"], NPR * t + 4)
                            value_product(it, 0).then_inc(S["proj_done"], 1)
                            pe.wait_ge(S["proj_out"], NPR * t + 5)
                            value_product(it, 1).then_inc(w_used, 1)
                            pe.wait_ge(S["proj_out"], NPR * t + 6)
                            nc.tensor.matmul(pp[1][:, :], C("rot"), qraw[:, :], start=True, stop=True).then_inc(S["rot_done"], 1)
                            pe.wait_ge(S["proj_out"], NPR * t + 7)
                            pe.wait_ge(S["qrope_done"], t + 1)
                            for n in range(NB + 1):
                                if n < NB:
                                    scores(t, n)
                                if n > 0:
                                    turn_p(t, n - 1)
                                if n == QB + 2:
                                    value_sum(t, 0)
                            value_sum(t, 1)

                    @block.scalar
                    def _(act):
                        def exps(t, n):
                            act.wait_ge(S["nmax_done"], NB * t + n + 1)
                            wait(act, S["pT_done"], NB * t + n - 1)
                            nk = (n % QB + 1) * P
                            nc.scalar.activation(pexp[:, n % 2, 0:nk], sc[n % 2][:, 0:nk], ACT.Exp, scale=SCALE,
                                                 bias=nmx[:, n:n + 1], accum_out=rs[:, n:n + 1]).then_inc(S["exp_done"], 1)

                        def turned_out(t, n):
                            act.wait_ge(S["pT_done"], NB * t + n + 1)
                            h, i = n // QB, n % QB
                            wait(act, S["o_done"], 2 * t + h - 1)
                            nc.scalar.copy(pT[:, h, 0:i + 1, i * P:(i + 1) * P],
                                           tp[n % 2][:, 0:(i + 1) * P].rearrange("p (k q) -> p k q", q=P)).then_inc(S["pT_out"], 1)

                        def out_hi(t, h):
                            act.wait_ge(S["o_done"], 2 * t + h + 1)
                            nc.scalar.copy(dyn(ohi, 2 * t + h), op[h][:, :]).then_inc(S["o_hi"], 1)

                        for it in items(act, NP, jp):
                            t = it.t
                            split_hi(act, it, SLOT)
                            for step, dst in enumerate((qn[:, 0, :], qn[:, 1, :], qraw[:, :], kn[:, 0, :], kn[:, 1, :])):
                                act.wait_ge(S["proj_done"], (NPR - 1) * t + step + 1)
                                nc.scalar.copy(dst, pp[step % 2][:, :]).then_inc(S["proj_out"], 1)
                            for g in range(2):
                                if g == 0:
                                    act.wait_ge(S["proj_done"], (NPR - 1) * t + 6)
                                else:
                                    act.wait_ge(w_used, it.j + 1)
                                nc.scalar.copy(v[:, 2 * g:2 * g + 2, :], pp[(5 + g) % 2][:, :].rearrange("p (a n) -> p a n", a=2)).then_inc(S["proj_out"], 1)
                            for n in range(NB):
                                exps(t, n)
                                if n >= 2:
                                    turned_out(t, n - 2)
                            turned_out(t, NB - 2)
                            out_hi(t, 0)
                            turned_out(t, NB - 1)
                            out_hi(t, 1)

                    @block.vector
                    def _(dve):
                        def row_max(t, n):
                            i = n % QB
                            nk, diag = (i + 1) * P, slice(i * P, (i + 1) * P)
                            dve.wait_ge(S["score_done"], NB * t + n + 1)
                            nc.vector.tensor_tensor(sc[n % 2][:, diag], sc[n % 2][:, diag], C("causal"), ALU.add).then_inc(S["masked"], 1)
                            dve.wait_ge(S["masked"], NB * t + n + 1)
                            nc.vector.reduce_max(mx[:, n:n + 1], sc[n % 2][:, 0:nk], AX_X).then_inc(S["max_done"], 1)
                            dve.wait_ge(S["max_done"], NB * t + n + 1)
                            nc.vector.tensor_scalar(nmx[:, n:n + 1], mx[:, n:n + 1], -SCALE, None, ALU.mult).then_inc(S["nmax_done"], 1)

                        def normalize(t, n):
                            nk = (n % QB + 1) * P
                            dve.wait_ge(S["exp_done"], NB * t + n + 1)
                            nc.vector.reciprocal(ri[:, n:n + 1], rs[:, n:n + 1]).then_inc(S["rinv_done"], 1)
                            dve.wait_ge(S["rinv_done"], NB * t + n + 1)
                            nc.vector.tensor_scalar(pexp[:, n % 2, 0:nk], pexp[:, n % 2, 0:nk], ri[:, n:n + 1], None,
                                                    ALU.mult).then_inc(S["p_norm"], 1)

                        def out_lo(t, h):
                            dve.wait_ge(S["o_hi"], 2 * t + h + 1)
                            nc.vector.tensor_tensor(dyn(olo, 2 * t + h), op[h][:, :], dyn(ohi, 2 * t + h).bitcast(F32),
                                                    ALU.subtract).then_inc(S["o_lo"], 1)

                        for it in items(dve, NP, jp):
                            t = it.t
                            dve.wait_ge(S["proj_out"], NPR * t + 3)
                            nc.vector.tensor_tensor(qcos[:, :], qraw[:, :], cos[:, :], ALU.mult).then_inc(S["qrope_mul"], 1)
                            dve.wait_ge(S["rot_done"], t + 1)
                            nc.vector.tensor_tensor(qsin[:, :], pp[1][:, :], sin[:, :], ALU.mult).then_inc(S["qrope_mul"], 1)
                            dve.wait_ge(S["qrope_mul"], 2 * t + 2)
                            nc.vector.tensor_tensor(qr[:, :], qcos[:, :], qsin[:, :], ALU.add).then_inc(S["qrope_done"], 1)
                            for n in range(NB):
                                row_max(t, n)
                                if n > 0:
                                    normalize(t, n - 1)
                            normalize(t, NB - 1)
                            out_lo(t, 0)
                            out_lo(t, 1)
                j_used[0] = jp + NP
                project_residual("mo", a["w_attn_out"], ohi, olo)

        def rwkv():
            j0 = j_used[0]
            with phase() as st:
                o_all = sbuf(st, "wkv_out", [P, KD, T])
                kvr = nc.dram_tensor("kvr", (P, KD, 3, T), F32).ap()
                th, la = sbuf(st, "w_lora", [LW, T]), sbuf(st, "a_lora", [LW, T])
                lga, lgb = sbuf(st, "g_lora_a", [P, T]), sbuf(st, "g_lora_b", [LG - P, T])

                with phase() as s1:
                    ring(s1, "r")
                    h = sbuf(s1, "h", [P, KD, T])
                    out_buf = sbuf(s1, "rkv_out", [P, 2, T])
                    xx = sbuf(s1, "shift_diff", [P, KD, T])
                    xm = sbuf(s1, "mixed", [P, 4, T])
                    xhi, xlo = sbuf(s1, "mixed_hi", [P, KD, T], F32R), sbuf(s1, "mixed_lo", [P, KD, T], F32R)
                    l1 = sbuf(s1, "lora_in", [P, KD, 2 * LW + LG])
                    rstd = sbuf(s1, "r_rstd", [P, T])
                    ps = [psum(s1, f"rkv_ps{b}") for b in range(2)]
                    ps_n, ps_w, ps_a, ps_ga, ps_gb = (psum(s1, f"r_{n}") for n in ("ss", "lw", "la", "lga", "lgb"))
                    s = norm_sems("r")
                    lora_loaded, normed, shifted, mixed, m_hi, m_lo, lora_used, rkv_out, lora_out = (
                        sem(f"r_{n}") for n in ("lora_loaded", "normed", "shifted", "mixed", "mix_hi", "mix_lo", "lora_used", "rkv_out", "lora_out"))
                    n = KD * P
                    NL = 3
                    MIXES = (3, 4, 5, 1, 0, 2)
                    stored = [sem("rkv_stored0"), sem("rkv_stored1")]
                    block = s1.enter_context(nc.Block(no_gpsimd_drain=True))

                    @block.sync
                    def _(sp):
                        sp.dma_start(l1[:, :, :], a["lora_in"].rearrange("p (k n) -> p k n", k=KD)).then_inc(lora_loaded, 16)
                        for q in range(3):
                            for it in items(sp, KD, j0 + q * KD):
                                load(sp, it, a["w_rkv"][bass.ds(it.t + q * KD, 1), :, :].rearrange("a p n -> p (a n)"), n)

                    @block.vector
                    def _(dve):
                        norm_dve(dve, s, KD, ps_n, rstd)
                        dve.wait_ge(s["rstd"], 1)
                        for k in range(KD):
                            nc.vector.scalar_tensor_tensor(out=h[:, k, :], in0=xk(k), scalar=V("norm_mix", KD + k), in1=rstd[:, :],
                                                           op0=ALU.mult, op1=ALU.mult).then_inc(normed, 1)
                            dve.wait_ge(normed, k + 1)
                            nc.vector.tensor_tensor(xx[:, k, 1:T], h[:, k, 0:T - 1], h[:, k, 1:T], ALU.subtract).then_inc(shifted, 1)
                            nc.vector.tensor_scalar(xx[:, k, 0:1], h[:, k, 0:1], -1.0, None, ALU.mult).then_inc(shifted, 1)
                        for q, mi in enumerate(MIXES):
                            for k in range(KD):
                                u = q * KD + k
                                dve.wait_ge(shifted, 2 * k + 2)
                                if u - 4 >= NL * KD:
                                    dve.wait_ge(m_lo, u - 4 - NL * KD + 1)
                                elif u >= 4:
                                    dve.wait_ge(lora_used, u - 3)
                                nc.vector.scalar_tensor_tensor(out=xm[:, u % 4, :], in0=xx[:, k, :], scalar=V("mix", mi * KD + k),
                                                               in1=h[:, k, :], op0=ALU.mult, op1=ALU.add).then_inc(mixed, 1)

                    @block.scalar
                    def _(act):
                        norm_act(act, s, KD, xk, xm)
                        norm_act_sqrt(act, s, rstd)
                        act.wait_ge(lora_used, KD)
                        nc.scalar.activation(th[:, :], ps_w[0:LW, :], ACT.Tanh).then_inc(lora_out, 1)
                        act.wait_ge(lora_used, 2 * KD)
                        nc.scalar.copy(la[:, :], ps_a[0:LW, :]).then_inc(lora_out, 1)
                        act.wait_ge(lora_used, 3 * KD)
                        nc.scalar.activation(lga[:, :], ps_ga[:, :], ACT.Sigmoid).then_inc(lora_out, 1)
                        nc.scalar.activation(lgb[:, :], ps_gb[0:LG - P, :], ACT.Sigmoid).then_inc(lora_out, 1)
                        for q in range(3):
                            for k in range(KD):
                                u = (NL + q) * KD + k
                                act.wait_ge(mixed, u + 1)
                                wait(act, w_used, j0 + q * KD if q else 0)
                                nc.scalar.copy(xhi[:, k, :], xm[:, u % 4, :]).then_inc(m_hi, 1)

                            def out(it):
                                b = it.slot
                                before = it.turn - j0 // 2 - (b < j0 % 2)
                                act.wait_ge(w_used, it.j + 1)
                                wait(act, stored[b], 16 * before)
                                nc.scalar.copy(out_buf[:, b, :], ps[b][:, :]).then_inc(rkv_out, 1)
                                act.wait_ge(rkv_out, it.t + q * KD + 1)
                                act.dma_start(kvr[:, bass.ds(it.t, 1), q, :].rearrange("p a t -> p (a t)"), out_buf[:, b, :]).then_inc(stored[b], 16)
                            for it in items(act, KD, j0 + q * KD):
                                split_hi(act, it, n)
                                if not (isinstance(it.t, int) and it.t == 0):
                                    out(it.prev)
                            out(Item(KD - 1, KD - 1, j0 + q * KD, 0))
                        for b in range(2):
                            act.wait_ge(stored[b], 16 * (3 * KD // 2))

                    @block.gpsimd
                    def _(pool):
                        for q in range(3):
                            for k in range(KD):
                                u = (NL + q) * KD + k
                                pool.wait_ge(m_hi, q * KD + k + 1)
                                nc.gpsimd.tensor_tensor(xlo[:, k, :], xm[:, u % 4, :], xhi[:, k, :].bitcast(F32), ALU.subtract).then_inc(m_lo, 1)
                            for it in items(pool, KD, j0 + q * KD):
                                split_lo(pool, it, n)

                    @block.tensor
                    def _(pe):
                        norm_pe(pe, s, KD, xm, ps_n)
                        pe.wait_ge(lora_loaded, 16)
                        for q, (at, m, out) in enumerate(((0, LW, ps_w), (LW, LW, ps_a), (2 * LW, LG, ps_ga))):
                            for k in range(KD):
                                u = q * KD + k
                                pe.wait_ge(mixed, u + 1)
                                last = nc.tensor.matmul(out[0:min(m, P), :], l1[:, k, at:at + min(m, P)], xm[:, u % 4, :],
                                                        start=k == 0, stop=k == KD - 1)
                                if m > P:
                                    last = nc.tensor.matmul(ps_gb[0:m - P, :], l1[:, k, at + P:at + m], xm[:, u % 4, :],
                                                            start=k == 0, stop=k == KD - 1)
                                last.then_inc(lora_used, 1)
                        for q in range(3):
                            for it in items(pe, KD, j0 + q * KD):
                                pe.wait_ge(w_lo_ready, it.j + 1)
                                wait(pe, rkv_out, it.t + q * KD - 1)
                                for k in range(KD):
                                    if isinstance(it.t, int) and it.t == 0:
                                        pe.wait_ge(m_lo, q * KD + k + 1)
                                    last = three(ps[it.slot][:, :], k * P, P, xhi[:, k, :], xlo[:, k, :], it.slot, k == 0, k == KD - 1)
                                last.then_inc(w_used, 1)
                j_used[0] += 3 * KD
                wkv(kvr, th, la, lga, lgb, o_all)
                ohi, olo = sbuf(st, "wkv_ohi", [P, KD, T], F32R), sbuf(st, "wkv_olo", [P, KD, T], F32R)
                project_residual("ro", a["w_rwkv_out"], ohi, olo, o_all)

        def wkv(kvr, th, la, lga, lgb, o_all):
            with phase() as st:
                LANES = 2
                HR = (slice(0, CH), slice(CH, P))
                VR = HR
                UR = (HR[1], HR[0])
                LEVELS = 5
                NT = 13
                work = sbuf(st, "work", [P, LANES * NT - 8, T])

                def tile(i):
                    return raw[i // 4][:, (i % 4) * T:(i % 4 + 1) * T] if i < 8 else work[:, i - 8, :]

                def ch(t2):
                    return t2.rearrange("p (c s) -> p c s", s=CH)

                def flat(t3):
                    return t3.rearrange("p a s -> p (a s)")

                class Lane:

                    def __init__(self, p):
                        def b(name, shape):
                            return sbuf(st, f"{name}{p}", shape)
                        (self.d, self.rate, self.gate, self.D, self.Dc, self.eR, self.eK, self.kk, self.rn,
                         self.kp, self.b1, self.bonus, self.prob) = (tile(p * NT + i) for i in range(NT))
                        self.Dp = self.d
                        self.kk2, self.rk = self.eR, self.eK
                        self.eA = self.d
                        self.inv, self.tt = self.kp, self.b1
                        self.y, self.yc, self.yc2, self.out = self.eR, self.eK, self.d, self.kk
                        self.krv = b("krv", [P, 3, T])
                        self.lw = b("lora_out", [P, 4 * P])
                        self.AR = b("AR", [P, NC, 2, CH])
                        self.KB = b("KB", [P, NC, 2, CH])
                        self.TB = self.KB
                        self.KBT = b("KBT", [P, NC, P])
                        self.VU = b("VU", [P, NC, 2, CH])
                        self.Vs = b("V_stacked", [P, NC, CH])
                        self.AB = b("a_B", [P, NC, 2, CH])
                        self.MB = b("M_B", [P, NC, 2, CH])
                        self.LT = b("LT", [P, NC, CH])
                        self.LB = b("LT_B", [P, NC, 2, CH])
                        self.RKB = b("RKB", [P, NC, 2, CH])
                        self.PB = b("P_B", [P, NC, 2, CH])
                        self.R = b("R", [P, CH])
                        self.Sp, self.Sg = b("S", [P, 2, CH]), b("S_decayed", [P, CH])
                        self.SB = b("S_B", [P, 2, 2, CH])
                        self.gs = b("chunk_decay", [P, NC])
                        self.B = [psum(st, f"wkv_ps{p}_{i}") for i in range(4)]
                        names = ("loaded", "zeroed", "lora_done", "lora_ev", "vb_done", "v_done", "v_out", "dc_done", "dp_done",
                                 "gs_done", "exps", "gs_exp", "kk2_done", "ss_done", "rn_max", "rn_recip", "rn_done", "rk_done",
                                 "bonus_done", "bonus_out", "ar_done", "kb_done", "ab_done", "kbt_done", "kbt_out", "tb_zero", "gram_done", "lt_done",
                                 "gram_out", "p_ready", "pb_done", "lb_done", "x_ready", "tt_done", "tt_out", "tb_done", "pl_done", "p_new",
                                 "rhs_done", "rhs_out", "u_done", "u_out0", "u_out1", "s_done", "s_new", "sb_done", "y_done", "y_out",
                                 "mu_done", "yc_done", "yc2_done", "var_done", "var_recip", "rstd_done", "finished")
                        self.S = {n: sem(f"k{p}_{n}") for n in names}
                        self.chain_sem = sem(f"k{p}_chain")

                lanes = [Lane(p) for p in range(LANES)]

                def turns(eng, steps):
                    each = {}

                    def turn(i):
                        chains = [Chain(eng, ln.chain_sem, i * each[n] if each else 0) for n, ln in enumerate(lanes)]
                        for _ in zip(*(steps(ln, i, LANES * i + p, chains[p]) for p, ln in enumerate(lanes)), strict=True):
                            pass
                        return chains
                    chains = turn(0)
                    each.update({p: c.n for p, c in enumerate(chains)})
                    with eng.Fori(1, KD // LANES) as i:
                        turn(i)

                block = st.enter_context(nc.Block(no_gpsimd_drain=True))

                @block.sync
                def _(sp):
                    def steps(ln, i, c, _):
                        wait(sp, ln.S["gram_done"], i)
                        sp.dma_start(ln.lw[:, :], a["lora_out"][bass.ds(c, 1), :, :].rearrange("a p n -> p (a n)")).then_inc(ln.S["loaded"], 16)
                        sp.dma_start(ln.krv[:, :, :], kvr[:, bass.ds(c, 1), :, :].rearrange("p a k t -> p (a k) t")).then_inc(ln.S["loaded"], 16)
                        yield
                    turns(sp, steps)

                @block.tensor
                def _(pe):
                    mm = nc.tensor.matmul

                    def steps(ln, i, c, _):
                        S, B = ln.S, ln.B
                        pe.wait_ge(S["loaded"], 32 * i + 32)
                        wait(pe, S["finished"], i)
                        mm(B[0][:, :], ln.lw[0:LW, 0:P], th[:, :], start=True, stop=True)
                        mm(B[1][:, :], ln.lw[0:LW, P:2 * P], la[:, :], start=True, stop=True)
                        mm(B[2][:, :], ln.lw[:, 2 * P:3 * P], lga[:, :], start=True, stop=False)
                        mm(B[2][:, :], ln.lw[0:LG - P, 3 * P:4 * P], lgb[:, :], start=False, stop=True).then_inc(S["lora_done"], 1)
                        yield
                        pe.wait_ge(S["vb_done"], 2 * i + 2)
                        for q in range(NC):
                            last = mm(B[3][:, q * CH:(q + 1) * CH], flat(ln.PB[:, q, :, :]), C("ident64", CH), start=True, stop=True)
                        last.then_inc(S["v_done"], 1)
                        yield
                        pe.wait_ge(S["lora_ev"], 3 * i + 3)
                        pe.wait_ge(S["kk2_done"], i + 1)
                        mm(B[0][:, :], C("headsum"), ln.kk2, start=True, stop=True).then_inc(S["ss_done"], 1)
                        pe.wait_ge(S["rk_done"], i + 1)
                        mm(B[1][:, :], C("headsum"), ln.rk, start=True, stop=True).then_inc(S["bonus_done"], 1)
                        yield
                        yield
                        pe.wait_ge(S["v_out"], 3 * i + 3)
                        pe.wait_ge(S["kb_done"], 4 * i + 4)
                        for q in range(NC):
                            last = nc.tensor.transpose(B[2 + q // 4][:, (q % 4) * P:(q % 4 + 1) * P], flat(ln.KB[:, q, :, :]), C("ident"))
                        last.then_inc(S["kbt_done"], 1)
                        yield
                        pe.wait_ge(S["ar_done"], 2 * i + 2)
                        pe.wait_ge(S["rn_max"], i + 1)
                        pe.wait_ge(S["bonus_out"], i + 1)
                        pe.wait_ge(S["kbt_out"], 2 * i + 2)
                        for hh in range(2):
                            for q in range(NC):
                                last = mm(B[2 * hh + q // 4][:, (q % 4) * P:(q % 4 + 1) * P],
                                          flat(ln.KB[HR[hh], q, :, :]), flat(ln.AR[HR[hh], q, :, :]), start=True, stop=True)
                        last.then_inc(S["gram_done"], 1)
                        yield
                        for l in range(LEVELS):
                            pe.wait_ge(S["lb_done"], 2 * (LEVELS * i + l + 1))
                            pe.wait_ge(S["x_ready"], LEVELS * i + l + 1)
                            if l == 0:
                                pe.wait_ge(S["gram_out"], 8 * i + 8)
                            for q in range(NC):
                                last = mm(B[0][:, q * CH:(q + 1) * CH], flat(ln.LB[:, q, :, :]), ch(ln.inv)[:, q, :], start=True, stop=True)
                            last.then_inc(S["tt_done"], 1)
                            yield
                            pe.wait_ge(S["tb_done"], 2 * (LEVELS * i + l + 1))
                            if l > 0:
                                pe.wait_ge(S["p_new"], LEVELS * i + l)
                            for q in range(NC):
                                last = mm(B[1][:, q * CH:(q + 1) * CH], flat(ln.TB[:, q, :, :]), ch(ln.prob)[:, q, :], start=True, stop=True)
                            last.then_inc(S["pl_done"], 1)
                            yield
                        pe.wait_ge(S["pb_done"], 2 * i + 2)
                        pe.wait_ge(S["ab_done"], 2 * i + 2)

                        def outputs(q):
                            out = B[3][:, q * CH:(q + 1) * CH]
                            if q > 0:
                                pe.wait_ge(S["sb_done"], 2 * ((NC - 1) * i + q))
                                mm(out, flat(ln.SB[:, q % 2, :, :]), ln.AR[:, q, 1, :], start=True, stop=False)
                            for hh in range(2):
                                last = mm(B[3][HR[hh], q * CH:(q + 1) * CH], ln.VU[:, q, hh, :], ln.RKB[:, q, hh, :], start=q == 0, stop=True)
                            return last
                        for q in range(NC):
                            out = B[0][:, 0:CH]
                            last = mm(out, flat(ln.MB[:, q, :, :]), ln.Vs[:, q, :], start=True, stop=q == 0)
                            if q > 0:
                                pe.wait_ge(S["s_new"], (NC - 1) * i + q)
                                last = mm(out, flat(ln.AB[:, q, :, :]), ln.Sp[:, q % 2, :], start=False, stop=True)
                            last.then_inc(S["rhs_done"], 1)
                            yield
                            if q > 0:
                                outputs(q - 1)
                            pe.wait_ge(S["rhs_out"], NC * i + q + 1)
                            mm(B[1][:, 0:CH], flat(ln.PB[:, q, :, :]), ln.R[:, :], start=True, stop=True).then_inc(S["u_done"], 1)
                            yield
                            pe.wait_ge(S["u_out0"], NC * i + q + 1)
                            pe.wait_ge(S["u_out1"], NC * i + q + 1)
                            if q < NC - 1:
                                for hh in range(2):
                                    last = mm(B[2][HR[hh], 0:CH], ln.KBT[:, q, hh * CH:(hh + 1) * CH], ln.VU[:, q, hh, :], start=True, stop=True)
                                last.then_inc(S["s_done"], 1)
                            yield
                        outputs(NC - 1).then_inc(S["y_done"], 1)
                        yield
                        pe.wait_ge(S["y_out"], i + 1)
                        mm(B[0][:, :], C("headmean"), ln.y, start=True, stop=True).then_inc(S["mu_done"], 1)
                        yield
                        pe.wait_ge(S["yc2_done"], i + 1)
                        mm(B[1][:, :], C("headmean"), ln.yc2, start=True, stop=True).then_inc(S["var_done"], 1)
                        yield
                        yield
                    turns(pe, steps)

                @block.scalar
                def _(act):
                    A = nc.scalar

                    def steps(ln, i, c, chain):
                        S, B = ln.S, ln.B
                        if isinstance(i, int):
                            act.wait_ge(S["zeroed"], 5)
                        act.wait_ge(S["loaded"], 32 * i + 32)
                        wait(act, S["finished"], i)
                        for hh in range(2):
                            A.copy(ln.PB[HR[hh], :, hh, :], ch(ln.krv[:, 2, :])[HR[hh], :, :]).then_inc(S["vb_done"], 1)
                        act.wait_ge(S["lora_done"], i + 1)
                        A.activation(ln.d, B[0][:, :], ACT.Sigmoid, bias=V("w0", c)).then_inc(S["lora_ev"], 1)
                        A.activation(ln.rate, B[1][:, :], ACT.Sigmoid, bias=V("a0", c)).then_inc(S["lora_ev"], 1)
                        A.copy(ln.gate, B[2][:, :]).then_inc(S["lora_ev"], 1)
                        yield
                        act.wait_ge(S["v_done"], i + 1)
                        A.copy(ln.Vs[:, :, :], ch(B[3][:, :])).then_inc(S["v_out"], 1)
                        for hh in range(2):
                            A.copy(ln.VU[VR[hh], :, hh, :], ch(B[3][VR[hh], :])).then_inc(S["v_out"], 1)
                        yield
                        act.wait_ge(S["rn_recip"], i + 1)
                        A.activation(ln.rn, ln.rn, ACT.Sqrt).then_inc(S["rn_done"], 1)
                        yield
                        act.wait_ge(S["dc_done"], i + 1)
                        act.wait_ge(S["ss_done"], i + 1)
                        A.activation(ln.eR, ln.Dc, ACT.Exp, scale=-KAPPA).then_inc(S["exps"], 1)
                        act.wait_ge(S["bonus_done"], i + 1)
                        A.activation(ln.eK, ln.Dc, ACT.Exp, scale=KAPPA).then_inc(S["exps"], 1)
                        act.wait_ge(S["dp_done"], i + 1)
                        A.activation(ln.eA, ln.Dp, ACT.Exp, scale=-KAPPA).then_inc(S["exps"], 1)
                        act.wait_ge(S["gs_done"], i + 1)
                        A.activation(ln.gs[:, 0:NC - 1], ln.gs[:, 0:NC - 1], ACT.Exp, scale=-KAPPA).then_inc(S["gs_exp"], 1)
                        yield
                        act.wait_ge(S["kbt_done"], i + 1)
                        for b in range(2):
                            A.copy(ln.KBT[:, 4 * b:4 * b + 4, :], B[2 + b][:, :].rearrange("p (c s) -> p c s", s=P)).then_inc(S["kbt_out"], 1)
                        yield
                        yield
                        for l in range(LEVELS):
                            act.wait_ge(S["tt_done"], LEVELS * i + l + 1)
                            A.copy(ln.tt, B[0][:, :]).then_inc(S["tt_out"], 1)
                            if l == 0:
                                act.wait_ge(S["tb_zero"], i + 1)
                            act.wait_ge(S["tt_out"], LEVELS * i + l + 1)
                            A.copy(ln.TB[HR[0], :, 0, :], ch(ln.tt)[HR[0], :, :]).then_inc(S["tb_done"], 1)
                            yield
                            yield
                        act.wait_ge(S["p_new"], LEVELS * i + LEVELS)
                        A.copy(ln.PB[HR[0], :, 0, :], ch(ln.prob)[HR[0], :, :]).then_inc(S["pb_done"], 1)
                        for q in range(NC):
                            act.wait_ge(S["rhs_done"], NC * i + q + 1)
                            A.copy(ln.R[:, :], B[0][:, 0:CH]).then_inc(S["rhs_out"], 1)
                            yield
                            act.wait_ge(S["u_done"], NC * i + q + 1)
                            A.copy(ln.VU[UR[0], q, 0, :], B[1][UR[0], 0:CH]).then_inc(S["u_out0"], 1)
                            yield
                            if q < NC - 1:
                                act.wait_ge(S["s_new"], (NC - 1) * i + q + 1)
                                for hh in range(2):
                                    A.copy(ln.SB[HR[hh], (q + 1) % 2, hh, :], ln.Sp[HR[hh], (q + 1) % 2, :]).then_inc(S["sb_done"], 1)
                            yield
                        act.wait_ge(S["y_done"], i + 1)
                        A.copy(ln.y, B[3][:, :]).then_inc(S["y_out"], 1)
                        yield
                        act.wait_ge(S["yc_done"], i + 1)
                        A.activation(ln.yc2, ln.yc, ACT.Square).then_inc(S["yc2_done"], 1)
                        yield
                        yield
                        act.wait_ge(S["var_recip"], i + 1)
                        A.activation(ln.rn, ln.rn, ACT.Sqrt).then_inc(S["rstd_done"], 1)
                        yield
                    turns(act, steps)

                @block.gpsimd
                def _(pool):
                    G = nc.gpsimd
                    for ln in lanes:
                        for t4 in (ln.PB, ln.AB, ln.MB, ln.SB, ln.LB):
                            G.memset(t4[:, :, :, :], 0.0).then_inc(ln.S["zeroed"], 1)
                    for ln in lanes:
                        pool.wait_ge(ln.S["zeroed"], 5)

                    def steps(ln, i, c, chain):
                        S = ln.S
                        yield
                        pool.wait_ge(S["dc_done"], i + 1)
                        G.tensor_tensor(ln.Dp, ln.Dc, ln.d, ALU.subtract).then_inc(S["dp_done"], 1)
                        yield
                        yield
                        yield
                        yield
                        pool.wait_ge(S["gram_done"], i + 1)
                        for hh in range(2):
                            one = C("incl", CH, HR[hh]).unsqueeze(1).to_broadcast([CH, NC, CH])
                            last = G.tensor_tensor(ln.TB[HR[hh], :, 1 - hh, :], one, one, ALU.subtract)
                        last.then_inc(S["tb_zero"], 1)
                        yield
                        pool.wait_ge(S["lt_done"], 4 * i + 4)
                        for l in range(LEVELS):
                            wait(pool, S["tt_done"], LEVELS * i + l)
                            for hh in range(2):
                                m = con[HR[hh], CON["levels"] + (l + 1) * CH:CON["levels"] + (l + 2) * CH].unsqueeze(1).to_broadcast([CH, NC, CH])
                                G.tensor_tensor(ln.LB[HR[hh], :, hh, :], ln.LT[HR[hh], :, :], m, ALU.mult).then_inc(S["lb_done"], 1)
                            yield
                            yield
                        for q in range(NC):
                            yield
                            yield
                            yield
                        yield
                        yield
                        yield
                        yield
                    turns(pool, steps)

                @block.vector
                def _(dve):
                    X = nc.vector

                    def steps(ln, i, c, chain):
                        S, B = ln.S, ln.B
                        k, r, v = ln.krv[:, 0, :], ln.krv[:, 1, :], ln.krv[:, 2, :]
                        if isinstance(i, int):
                            dve.wait_ge(S["zeroed"], 5)
                        dve.wait_ge(S["loaded"], 32 * i + 32)
                        chain(X.tensor_scalar(ln.kk, k, V("k_k", c), None, ALU.mult))
                        X.tensor_tensor(ln.kk2, ln.kk, ln.kk, ALU.mult).then_inc(S["kk2_done"], 1)
                        yield
                        dve.wait_ge(S["lora_ev"], 3 * i + 2)
                        chain(X.tensor_tensor_scan(ln.D, C("reset", T), ln.d, 0.0, ALU.mult, ALU.add))
                        mid = CH // 2 - 1
                        X.tensor_tensor(ch(ln.Dc), ch(ln.D), ch(ln.D)[:, :, mid:mid + 1].to_broadcast([P, NC, CH]), ALU.subtract).then_inc(S["dc_done"], 1)
                        chain(X.tensor_scalar(ln.kp, ln.rate, -1.0, V("k_a", c), ALU.add, ALU.mult))
                        chain(X.scalar_tensor_tensor(out=ln.kp, in0=ln.kp, scalar=1.0, in1=k, op0=ALU.add, op1=ALU.mult))
                        X.scalar_tensor_tensor(out=ln.rk, in0=r, scalar=V("r_k", c), in1=ln.kp, op0=ALU.mult, op1=ALU.mult).then_inc(S["rk_done"], 1)
                        dve.wait_ge(S["dc_done"], i + 1)
                        X.tensor_tensor(ln.gs[:, 0:NC - 1], ch(ln.Dc)[:, 0:NC - 1, CH - 1], ch(ln.D)[:, 1:NC, mid], ALU.add).then_inc(S["gs_done"], 1)
                        yield
                        dve.wait_ge(S["ss_done"], i + 1)
                        X.tensor_scalar(ln.rn, B[0][:, :], 1e-24, None, ALU.max).then_inc(S["rn_max"], 1)
                        dve.wait_ge(S["rn_max"], i + 1)
                        X.reciprocal(ln.rn, ln.rn).then_inc(S["rn_recip"], 1)
                        dve.wait_ge(S["bonus_done"], i + 1)
                        X.tensor_tensor(ln.bonus, B[1][:, :], v, ALU.mult).then_inc(S["bonus_out"], 1)
                        yield
                        dve.wait_ge(S["rn_done"], i + 1)
                        chain(X.tensor_tensor(ln.kk, ln.kk, ln.rn, ALU.mult))
                        chain(X.tensor_tensor(ln.b1, ln.kk, ln.rate, ALU.mult))
                        yield
                        dve.wait_ge(S["exps"], 3 * i + 2)
                        for hh, slots in enumerate(((ln.kp, ln.b1), (ln.b1, ln.kp))):
                            for slot, src in enumerate(slots):
                                X.tensor_tensor(ln.KB[HR[hh], :, slot, :], ch(src)[HR[hh], :, :], ch(ln.eK)[HR[hh], :, :], ALU.mult).then_inc(S["kb_done"], 1)
                        dve.wait_ge(S["exps"], 3 * i + 3)
                        X.scalar_tensor_tensor(out=ln.AR[:, :, 0, :], in0=ch(ln.kk), scalar=-1.0, in1=ch(ln.eA), op0=ALU.mult, op1=ALU.mult).then_inc(S["ar_done"], 1)
                        X.tensor_tensor(ln.AR[:, :, 1, :], ch(r), ch(ln.eR), ALU.mult).then_inc(S["ar_done"], 1)
                        yield
                        dve.wait_ge(S["ar_done"], 2 * i + 1)
                        for hh in range(2):
                            X.tensor_copy(ln.AB[HR[hh], :, 1 - hh, :], ln.AR[HR[hh], :, 0, :]).then_inc(S["ab_done"], 1)
                        dve.wait_ge(S["gram_done"], i + 1)
                        bank = [B[n][:, :].rearrange("p (c n) -> p c n", n=P) for n in range(4)]

                        def mask(name, rows):
                            return C(name, CH, rows).unsqueeze(1).to_broadcast([rows.stop - rows.start, 4, CH])

                        def part(n):
                            return n // 2, slice(4 * (n % 2), 4 * (n % 2) + 4)
                        for n in range(4):
                            hh, qs = part(n)
                            X.tensor_tensor(ln.LT[UR[hh], qs, :], bank[n][UR[hh], :, 0:CH], mask("strict", UR[hh]), ALU.mult).then_inc(S["lt_done"], 1)
                        dve.wait_ge(S["lt_done"], 4 * i + 4)
                        chain(X.tensor_tensor(ch(ln.prob), ln.LT[:, :, :], con[:, CON["levels"]:CON["levels"] + CH].unsqueeze(1).to_broadcast([P, NC, CH]), ALU.mult))
                        X.tensor_tensor(ch(ln.prob), ch(ln.prob), C("ident64", CH).unsqueeze(1).to_broadcast([P, NC, CH]), ALU.add).then_inc(S["p_ready"], 1)
                        dve.wait_ge(S["p_ready"], i + 1)
                        X.transpose(ln.inv, ln.prob).then_inc(S["x_ready"], 1)
                        for n in range(4):
                            hh, qs = part(n)
                            X.tensor_tensor(ln.MB[VR[hh], qs, 1 - hh, :], bank[n][VR[hh], :, 0:CH], mask("strict", VR[hh]), ALU.mult).then_inc(S["gram_out"], 1)
                            X.tensor_tensor(ln.RKB[:, qs, hh, :], bank[n][:, :, CH:P], mask("incl", slice(0, P)), ALU.mult).then_inc(S["gram_out"], 1)
                        yield
                        for l in range(LEVELS):
                            dve.wait_ge(S["tt_out"], LEVELS * i + l + 1)
                            X.tensor_copy(ln.TB[HR[1], :, 1, :], ch(ln.tt)[HR[1], :, :]).then_inc(S["tb_done"], 1)
                            yield
                            dve.wait_ge(S["pl_done"], LEVELS * i + l + 1)
                            X.tensor_tensor(ln.prob, ln.prob, B[1][:, :], ALU.add).then_inc(S["p_new"], 1)
                            dve.wait_ge(S["p_new"], LEVELS * i + l + 1)
                            if l < LEVELS - 1:
                                X.transpose(ln.inv, ln.prob).then_inc(S["x_ready"], 1)
                            else:
                                X.tensor_copy(ln.PB[HR[1], :, 1, :], ch(ln.prob)[HR[1], :, :]).then_inc(S["pb_done"], 1)
                            yield
                        dve.wait_ge(S["gs_exp"], i + 1)
                        for q in range(NC):
                            if 0 < q < NC - 1:
                                dve.wait_ge(S["s_new"], (NC - 1) * i + q)
                                chain(X.tensor_scalar(ln.Sg[:, :], ln.Sp[:, q % 2, :], ln.gs[:, q:q + 1], None, ALU.mult))
                            yield
                            dve.wait_ge(S["u_done"], NC * i + q + 1)
                            X.tensor_copy(ln.VU[UR[1], q, 1, :], B[1][UR[1], 0:CH]).then_inc(S["u_out1"], 1)
                            yield
                            if q < NC - 1:
                                dve.wait_ge(S["s_done"], (NC - 1) * i + q + 1)
                                if q == 0:
                                    X.tensor_scalar(ln.Sp[:, 1, :], B[2][:, 0:CH], ln.gs[:, 0:1], None, ALU.mult).then_inc(S["s_new"], 1)
                                else:
                                    X.scalar_tensor_tensor(out=ln.Sp[:, (q + 1) % 2, :], in0=B[2][:, 0:CH], scalar=ln.gs[:, q:q + 1],
                                                           in1=ln.Sg[:, :], op0=ALU.mult, op1=ALU.add).then_inc(S["s_new"], 1)
                            yield
                        yield
                        dve.wait_ge(S["mu_done"], i + 1)
                        X.tensor_tensor(ln.yc, ln.y, B[0][:, :], ALU.subtract).then_inc(S["yc_done"], 1)
                        yield
                        dve.wait_ge(S["var_done"], i + 1)
                        chain(X.tensor_scalar(ln.rn, B[1][:, :], GN_EPS, None, ALU.add))
                        X.reciprocal(ln.rn, ln.rn).then_inc(S["var_recip"], 1)
                        yield
                        dve.wait_ge(S["rstd_done"], i + 1)
                        chain(X.tensor_tensor(ln.out, ln.yc, ln.rn, ALU.mult))
                        chain(X.tensor_scalar(ln.out, ln.out, V("ln_w", c), V("ln_b", c), ALU.mult, ALU.add))
                        chain(X.tensor_tensor(ln.out, ln.out, ln.bonus, ALU.add))
                        X.tensor_tensor(dyn(o_all, c), ln.out, ln.gate, ALU.mult).then_inc(S["finished"], 1)
                        yield
                    turns(dve, steps)

        def finish(norm=True):
            with phase() as st:
                sq, rstd = sbuf(st, "f_sq", [P, 2, T]), sbuf(st, "f_rstd", [P, T])
                out = sbuf(st, "f_out", [P, KD, T])
                ps_n = psum(st, "f_ss")
                s = norm_sems("f")
                stored = sem("stored")
                block = st.enter_context(nc.Block(no_gpsimd_drain=True))

                @block.scalar
                def _(act):
                    norm_act(act, s, KD, xk, sq)
                    norm_act_sqrt(act, s, rstd)

                @block.tensor
                def _(pe):
                    norm_pe(pe, s, KD, sq, ps_n)

                @block.vector
                def _(dve):
                    norm_dve(dve, s, KD, ps_n, rstd)
                    dve.wait_ge(s["rstd"], 1)
                    for k in range(KD):
                        if norm:
                            nc.vector.scalar_tensor_tensor(out=out[:, k, :], in0=xk(k), scalar=V("norm_final", k), in1=rstd[:, :],
                                                           op0=ALU.mult, op1=ALU.mult).then_inc(s["hn"], 1)
                        else:
                            nc.vector.tensor_copy(out[:, k, :], xk(k)).then_inc(s["hn"], 1)

                @block.sync
                def _(sp):
                    for k in range(KD):
                        sp.wait_ge(s["hn"], k + 1)
                        sp.dma_start(a["out"][:, k, :], out[:, k, :]).then_inc(stored, 16)
                    sp.wait_ge(stored, 16 * KD)

        attention()
        if stop != "attn":
            conv_glu("f0", 0, a["ffn_in0"], a["ffn_out0"])
            if stop != "ffn0":
                rwkv()
                if stop != "rwkv":
                    conv_glu("f1", 1, a["ffn_in1"], a["ffn_out1"])
        finish(stop == "all")


def constant_matrices():
    c = np.zeros((P, NCON), np.float32)

    def put(name, m):
        c[:, CON[name]:CON[name] + m.shape[1]] = m
    i, j = np.arange(P)[:, None], np.arange(P)[None, :]
    put("ones", np.ones((P, P)))
    half = ROPE // 2
    first = j % ROPE < half
    put("rot", np.where(first & (i == j + half), -1.0, 0.0) + np.where(~first & (i == j - half), 1.0, 0.0))
    put("ident", np.eye(P))
    put("causal", np.where(j > i, NEG, 0.0))
    put("headsum", (i // RN == j // RN) * 1.0)
    put("headmean", (i // RN == j // RN) / RN)
    s, t = np.arange(P)[:, None] % CH, np.arange(CH)[None, :]
    put("incl", (s <= t) * 1.0)
    put("strict", (s < t) * 1.0)
    put("ident64", (s == t) * 1.0)
    put("levels", np.concatenate([(s // (2 * m) == t // (2 * m)) & (s // m % 2 == 0) & (t // m % 2 == 1)
                                  for m in (1, 2, 4, 8, 16, 32)], axis=1) * 1.0)
    put("reset", np.broadcast_to(np.arange(T)[None, :] % CH != 0, (P, T)) * 1.0)
    return c


def kernel(**inputs):
    import numpy as _np
    import concourse.bacc as _bacc
    from concourse import mybir as _mybir
    from concourse.bass_utils import run_bass_kernel_spmd as _run

    g = {k: _np.asarray(v) for k, v in inputs.items()}

    def tiles(w, m=P):
        k, n = w.shape
        return w.reshape(k // P, P, n // m, m).transpose(2, 1, 0, 3).reshape(n // m, P, k // P * m)

    def chan(v):
        return v.reshape(-1, P).T

    half = ROPE // 2
    inv_freq = (_np.float32(10000.0) ** (-_np.arange(half, dtype=_np.float32) / _np.float32(half))).astype(_np.float32)
    vec = _np.concatenate([chan(g["norm_mix"]), chan(g["norm_ffn"]), chan(g["norm_final"]), chan(g["mla_q_norm"]), chan(g["mla_kv_norm"]),
                           chan(g["rwkv_mix"]), chan(g["rwkv_w0"]), chan(g["rwkv_a0"]), chan(g["rwkv_k_k"]), chan(g["rwkv_k_a"]),
                           chan(g["rwkv_r_k"]), chan(g["rwkv_ln_w"]), chan(g["rwkv_ln_b"]), chan(g["ffn_conv_w"]), chan(g["ffn_conv_b"]),
                           _np.tile(inv_freq, P // half)[:, None]], axis=1)
    w_in = g["mla_w_in"][0]
    rope_cols = w_in[:, QL + KVL:]
    w_lat = tiles(_np.concatenate([w_in[:, :QL + KVL], rope_cols, rope_cols], axis=1))
    uq = g["mla_w_uq"][0].reshape(QL, HEADS, NOPE + ROPE)
    ukv = g["mla_w_ukv"][0].reshape(KVL, HEADS, NOPE + VDIM)
    w_pair = _np.concatenate([tiles(uq[:, :, :NOPE].reshape(QL, -1), 2 * NOPE), tiles(uq[:, :, NOPE:].reshape(QL, -1), 2 * ROPE),
                              tiles(ukv[:, :, :NOPE].reshape(KVL, -1), 2 * NOPE), tiles(ukv[:, :, NOPE:].reshape(KVL, -1), 2 * VDIM)], axis=2)
    lora_out = _np.zeros((KD, P, 4 * P), _np.float32)
    lora_out[:, :LW, 0:P] = g["rwkv_w2"][0].reshape(LW, KD, P).transpose(1, 0, 2)
    lora_out[:, :LW, P:2 * P] = g["rwkv_a2"][0].reshape(LW, KD, P).transpose(1, 0, 2)
    g2 = g["rwkv_g2"][0].reshape(LG, KD, P).transpose(1, 0, 2)
    lora_out[:, :, 2 * P:3 * P] = g2[:, :P]
    lora_out[:, :LG - P, 3 * P:4 * P] = g2[:, P:]
    arrays = {
        "x": g["x"][0].T.reshape(KD, P, T).transpose(1, 0, 2),
        "positions": _np.broadcast_to(g["positions"][0][None, :], (P, T)),
        "vec": vec, "con": constant_matrices(),
        "w_lat": w_lat, "w_pair": w_pair, "w_attn_out": tiles(g["mla_w_o"][0]),
        "lora_in": tiles(_np.concatenate([g["rwkv_w1"][0], g["rwkv_a1"][0], g["rwkv_g1"][0]], axis=1), 2 * LW + LG)[0],
        "w_rkv": _np.concatenate([tiles(g["rwkv_w_rkv"][0, n]) for n in (1, 0, 2)]),
        "lora_out": lora_out, "w_rwkv_out": tiles(g["rwkv_w_o"][0]),
    }
    for layer in range(2):
        w = g["ffn_w_in"][layer]
        arrays[f"ffn_in{layer}"] = _np.concatenate([tiles(w[:, :DFF]), tiles(w[:, DFF:])], axis=2)
        wo = g["ffn_w_out"][layer]
        arrays[f"ffn_out{layer}"] = _np.concatenate([tiles(wo[:DFF // 2]), tiles(wo[DFF // 2:])])
    arrays = {k: _np.ascontiguousarray(v) for k, v in arrays.items()}
    nc = _bacc.Bacc("TRN2", target_bir_lowering=False, num_devices=1)
    aps = {k: nc.dram_tensor(f"in_{k}", v.shape, _mybir.dt.from_np(v.dtype), kind="ExternalInput").ap() for k, v in arrays.items()}
    aps["out"] = nc.dram_tensor("out", (P, KD, T), _mybir.dt.float32, kind="ExternalOutput").ap()
    trunk(nc, aps)
    r = _run(nc, [{f"in_{k}": v for k, v in arrays.items()}], core_ids=[0])
    out = r.results[0]["out"]
    return _np.ascontiguousarray(out.transpose(2, 1, 0).reshape(1, T, D))
```

```python
from contextlib import ExitStack, contextmanager

import numpy as np

import concourse.bass as bass
from concourse import mybir

F32 = mybir.dt.float32
F32R = mybir.dt.float32r
I32 = mybir.dt.int32
ALU = mybir.AluOpType
ACT = mybir.ActivationFunctionType
AX_X = mybir.AxisListType.X

P = 128
T = 512
D = 1024
KD = D // P
NORM_EPS = 1e-6
HEADS, NOPE, ROPE, VDIM = 8, 128, 64, 128
QL, KVL = 384, 256
KQ, KKV = QL // P, KVL // P
QB = T // P
SCALE = float(NOPE + ROPE) ** -0.5
NEG = -1.0e30
RH, RN = 16, 64
GN_EPS = 64e-5
CH = 64
NC = T // CH
LW, LG = 64, 160
DFF = 2816
HALF = DFF // P // 2
KAPPA = float(np.exp(-0.5))
SLOT = 3 * 2 * P + 3 * P + 2 * 2 * P + 2 * 2 * P

VEC = {}
_at = 0
for _name, _n in (("norm_mix", 2 * KD), ("norm_ffn", 2 * KD), ("norm_final", KD), ("q_norm", KQ), ("kv_norm", KKV),
                  ("mix", 6 * KD), ("w0", KD), ("a0", KD), ("k_k", KD), ("k_a", KD), ("r_k", KD), ("ln_w", KD),
                  ("ln_b", KD), ("conv_w", 2 * 3 * 2 * HALF), ("conv_b", 2 * 2 * HALF), ("inv_freq", 1),
                  ("norm_eps", 1), ("gn_eps", 1)):
    VEC[_name] = _at
    _at += _n
NVEC = _at
CON = {}
_at = 0
for _name, _n in (("ones", P), ("rot", P), ("ident", P), ("causal", P), ("headsum", P), ("headmean", P),
                  ("strict", CH), ("incl", CH), ("ident64", CH), ("levels", 6 * CH), ("reset", T)):
    CON[_name] = _at
    _at += _n
NCON = _at


class Item:

    def __init__(self, t, tpar, j0, thalf):
        self.t, self.j = t, j0 + t
        self.slot = (j0 + tpar) % 2
        self.turn = thalf + (j0 + tpar) // 2
        self.args = (t, tpar, j0, thalf)

    @property
    def prev(self):
        t, tpar, j0, thalf = self.args
        return Item(t - 1, tpar - 1, j0, thalf)


def items(eng, n, j0):
    lead = 2 + n % 2
    for t in range(lead):
        yield Item(t, t, j0, 0)
    if n > lead:
        with eng.Fori(0, (n - lead) // 2) as i:
            for b in range(2):
                yield Item(lead + b + 2 * i, lead + b, j0, i)


def early_items(j0):
    return [Item(t, t, j0, 0) for t in range(2)]


def is_early(it):
    return isinstance(it.t, int) and it.t < 2


def wait(eng, sem, value):
    if isinstance(value, int) and value <= 0:
        return
    eng.wait_ge(sem, value)


class Chain:

    def __init__(self, eng, sem, base=0):
        self.eng, self.sem, self.base, self.n = eng, sem, base, 0

    def __call__(self, ins):
        ins.then_inc(self.sem, 1)
        self.n += 1
        self.eng.wait_ge(self.sem, self.base + self.n)


def trunk(nc, a):
    with ExitStack() as outer:
        scopes = [[]]

        @contextmanager
        def phase():
            scopes.append([])
            with ExitStack() as stack:
                yield stack
            used = scopes.pop()
            if used:
                nc.clear_and_free_semaphores(used)
                nc.all_engine_barrier()

        def sem(name):
            s = nc.alloc_semaphore(name=name)
            scopes[-1].append(s)
            return s

        def sbuf(stack, name, shape, dt=F32):
            return stack.enter_context(nc.sbuf_tensor(name, shape, dt))

        def psum(stack, name, shape=(P, 512)):
            return stack.enter_context(nc.psum_tensor(name, list(shape), F32))

        x = sbuf(outer, "x_resid", [P, KD, T])
        vec = sbuf(outer, "vec", [P, NVEC])
        con = sbuf(outer, "con", [P, NCON])
        raw = [sbuf(outer, f"w_raw{b}", [P, SLOT]) for b in range(2)]
        square = sbuf(outer, "square", [P, 2, T])
        square_sum = sbuf(outer, "square_sum", [P, T])
        whi, wlo = [None, None], [None, None]

        def ring(stack, tag):
            for b in range(2):
                whi[b] = sbuf(stack, f"{tag}_w_hi{b}", [P, SLOT], F32R)
                wlo[b] = sbuf(stack, f"{tag}_w_lo{b}", [P, SLOT], F32R)

        w_loaded = [sem("w_loaded0"), sem("w_loaded1")]
        w_hi_ready, w_lo_ready, w_used = sem("w_hi_ready"), sem("w_lo_ready"), sem("w_used")
        x_loaded, con_loaded = sem("x_loaded"), sem("con_loaded")

        def C(name, n=P, rows=slice(0, P)):
            return con[rows, CON[name]:CON[name] + n]

        def V(name, k):
            if isinstance(k, int):
                return vec[:, VEC[name] + k:VEC[name] + k + 1]
            return vec[:, bass.ds(k + VEC[name], 1)]

        def load(sp, it, src, n):
            wait(sp, w_lo_ready, it.j - 1)
            sp.dma_start(raw[it.slot][:, 0:n], src).then_inc(w_loaded[it.slot], 16)

        FIRST = {"p": ("w_pair", SLOT), "mo": ("w_attn_out", KD * P), "f0": ("ffn_in0", 2 * KD * P),
                 "r": ("w_rkv", KD * P), "f1": ("ffn_in1", 2 * KD * P)}

        def load_ahead(sp, tag, j0):
            if tag in FIRST:
                name, n = FIRST[tag]
                for it in early_items(j0):
                    load(sp, it, a[name][it.t, :, :], n)

        def split_hi(act, it, n):
            act.wait_ge(w_loaded[it.slot], 16 * it.turn + 16)
            wait(act, w_used, it.j - 1)
            nc.scalar.copy(whi[it.slot][:, 0:n], raw[it.slot][:, 0:n]).then_inc(w_hi_ready, 1)

        def split_lo(pool, it, n):
            pool.wait_ge(w_loaded[it.slot], 16 * it.turn + 16)
            pool.wait_ge(w_hi_ready, it.j + 1)
            nc.gpsimd.tensor_tensor(wlo[it.slot][:, 0:n], raw[it.slot][:, 0:n],
                                    whi[it.slot][:, 0:n].bitcast(F32), ALU.subtract).then_inc(w_lo_ready, 1)

        def three(out, w_at, m, rhs_hi, rhs_lo, slot, start, stop):
            wh, wl = whi[slot][:, w_at:w_at + m], wlo[slot][:, w_at:w_at + m]
            nc.tensor.matmul(out, wh, rhs_hi, start=start, stop=False)
            nc.tensor.matmul(out, wh, rhs_lo, start=False, stop=False)
            return nc.tensor.matmul(out, wl, rhs_hi, start=False, stop=stop)

        def norm_sems(tag):
            given = ahead.get(tag, {})
            return given | {n: sem(f"{tag}_{n}") for n in ("sq", "ss_added", "ss_done", "ln", "rstd", "hn", "hi", "lo") if n not in given}

        ahead = {tag: {n: sem(f"{tag}_{n}") for n in ("sq", "ss_added")} for tag in ("f0", "r", "f1", "f")}

        def square_act(act, s, it, x_done, before=0):
            act.wait_ge(x_done, it.t + before + 1)
            dst = square_sum[:, :] if isinstance(it.t, int) and it.t == 0 else square[:, it.slot, :]
            nc.scalar.activation(dst, xk(it.t), ACT.Square).then_inc(s["sq"], 1)

        def square_dve(dve, s, it):
            if isinstance(it.t, int) and it.t == 0:
                return
            dve.wait_ge(s["sq"], it.t + 1)
            wait(dve, s["ss_added"], it.t - 1)
            nc.vector.tensor_tensor(square_sum[:, :], square_sum[:, :], square[:, it.slot, :], ALU.add).then_inc(s["ss_added"], 1)

        def norm_act(act, s, n, src, sq, acc):
            for k in range(n):
                wait(act, s["ss_added"], k - 2)
                nc.scalar.activation(acc[:, :] if k == 0 else sq[:, k % 2, :], src(k), ACT.Square).then_inc(s["sq"], 1)

        def norm_dve(dve, s, n, sq, acc):
            for k in range(1, n):
                dve.wait_ge(s["sq"], k + 1)
                wait(dve, s["ss_added"], k - 1)
                nc.vector.tensor_tensor(acc[:, :], acc[:, :], sq[:, k % 2, :], ALU.add).then_inc(s["ss_added"], 1)

        def norm_act_rstd(act, s, n, ps, rstd):
            act.wait_ge(s["ss_done"], 1)
            nc.scalar.activation(rstd[:, :], ps[:, :], ACT.Ln, bias=V("norm_eps", 0), scale=1.0 / (n * P)).then_inc(s["ln"], 1)
            act.wait_ge(s["ln"], 1)
            nc.scalar.activation(rstd[:, :], rstd[:, :], ACT.Exp, scale=-0.5).then_inc(s["rstd"], 1)

        def norm_pe(pe, s, n, acc, ps):
            pe.wait_ge(s["ss_added"], n - 1)
            nc.tensor.matmul(ps[:, :], C("ones"), acc[:, :], start=True, stop=True).then_inc(s["ss_done"], 1)

        def normed_split_dve(dve, s, n, src, gain, rstd, hn):
            dve.wait_ge(s["rstd"], 1)
            for k in range(n):
                wait(dve, s["lo"], k - 1)
                nc.vector.scalar_tensor_tensor(out=hn[:, k % 2, :], in0=src(k), scalar=gain(k), in1=rstd[:, :],
                                               op0=ALU.mult, op1=ALU.mult).then_inc(s["hn"], 1)

        def normed_split_act(act, s, n, hn, hi):
            for k in range(n):
                act.wait_ge(s["hn"], k + 1)
                nc.scalar.copy(hi(k), hn[:, k % 2, :]).then_inc(s["hi"], 1)

        def normed_split_pool(pool, s, n, hn, hi, lo):
            for k in range(n):
                pool.wait_ge(s["hi"], k + 1)
                pool.wait_ge(s["hn"], k + 1)
                nc.gpsimd.tensor_tensor(lo(k), hn[:, k % 2, :], hi(k).bitcast(F32), ALU.subtract).then_inc(s["lo"], 1)

        def xk(k):
            return x[:, k, :] if isinstance(k, int) else x[:, bass.ds(k, 1), :].rearrange("p a t -> p (a t)")

        def dyn(t3, k):
            return t3[:, k, :] if isinstance(k, int) else t3[:, bass.ds(k, 1), :].rearrange("p a t -> p (a t)")

        j_used = [0]

        def project_residual(tag, w, ohi, olo, next_phase, o=None):
            j0 = j_used[0]
            n = KD * P
            next_norm = ahead[next_phase]
            with phase() as st:
                ring(st, tag)
                ps = [psum(st, f"{tag}_ps{b}") for b in range(2)]
                free, o_hi, o_lo = sem(f"{tag}_added"), sem(f"{tag}_o_hi"), sem(f"{tag}_o_lo")
                block = st.enter_context(nc.Block(no_gpsimd_drain=True))

                @block.sync
                def _(sp):
                    for it in items(sp, KD, j0):
                        if not (is_early(it) if tag in FIRST else isinstance(it.t, int) and it.t == 0):
                            load(sp, it, w[bass.ds(it.t, 1), :, :].rearrange("a p n -> p (a n)"), n)
                    load_ahead(sp, next_phase, j0 + KD)

                @block.scalar
                def _(act):
                    split_hi(act, Item(0, 0, j0, 0), n)
                    if o is not None:
                        for k in range(KD):
                            nc.scalar.copy(ohi[:, k, :], o[:, k, :]).then_inc(o_hi, 1)
                    for it in items(act, KD, j0):
                        if not (isinstance(it.t, int) and it.t == 0):
                            split_hi(act, it, n)
                        if not (isinstance(it.t, int) and it.t == 0):
                            square_act(act, next_norm, it.prev, free)
                    square_act(act, next_norm, Item(KD - 1, KD - 1, j0, 0), free)

                @block.gpsimd
                def _(pool):
                    for it in items(pool, KD, j0):
                        split_lo(pool, it, n)

                @block.tensor
                def _(pe):
                    for it in items(pe, KD, j0):
                        pe.wait_ge(w_lo_ready, it.j + 1)
                        wait(pe, free, it.t - 1)
                        for k in range(KD):
                            if o is not None and isinstance(it.t, int) and it.t == 0:
                                pe.wait_ge(o_lo, k + 1)
                            last = three(ps[it.slot][:, :], k * P, P, ohi[:, k, :], olo[:, k, :], it.slot, k == 0, k == KD - 1)
                        last.then_inc(w_used, 1)

                @block.vector
                def _(dve):
                    if o is not None:
                        for k in range(KD):
                            dve.wait_ge(o_hi, k + 1)
                            nc.vector.tensor_tensor(olo[:, k, :], o[:, k, :], ohi[:, k, :].bitcast(F32), ALU.subtract).then_inc(o_lo, 1)
                    for it in items(dve, KD, j0):
                        dve.wait_ge(w_used, it.j + 1)
                        nc.vector.tensor_tensor(xk(it.t), ps[it.slot][:, :], xk(it.t), ALU.add).then_inc(free, 1)
                        square_dve(dve, next_norm, it)
            j_used[0] += KD

        def conv_glu(tag, layer, w_in, w_out, next_phase):
            jb = j_used[0]
            n_in, n_out = 2 * KD * P, HALF * P
            next_norm = ahead[next_phase]
            with phase() as st:
                ring(st, tag)
                rstd = sbuf(st, f"{tag}_rstd", [P, T])
                hn = sbuf(st, f"{tag}_hn", [P, 2, T])
                hhi, hlo = sbuf(st, f"{tag}_hhi", [P, KD, T], F32R), sbuf(st, f"{tag}_hlo", [P, KD, T], F32R)
                ahi, alo = sbuf(st, f"{tag}_ahi", [P, HALF, T], F32R), sbuf(st, f"{tag}_alo", [P, HALF, T], F32R)
                cv, sl = sbuf(st, f"{tag}_conv", [P, 2, T]), sbuf(st, f"{tag}_silu", [P, 2, T])
                ga = sbuf(st, f"{tag}_act", [P, 2, T])
                ps_g = [psum(st, f"{tag}_gate{b}") for b in range(2)]
                ps_u = [psum(st, f"{tag}_up{b}") for b in range(2)]
                ps_y = [psum(st, f"{tag}_y{b}") for b in range(2)]
                ps_n = psum(st, f"{tag}_ss")
                s = norm_sems(tag)
                tap2, tap1, conv_done, silu_done, gated, act_hi, act_lo, added = (
                    sem(f"{tag}_{n}") for n in ("tap2", "tap1", "conv_done", "silu_done", "gated", "act_hi", "act_lo", "added"))
                block = st.enter_context(nc.Block(no_gpsimd_drain=True))
                per_half = HALF + KD

                def halves():
                    for hf in range(2):
                        j0 = jb + hf * per_half
                        yield hf, j0, j0 + HALF, hf * HALF, hf * KD

                @block.sync
                def _(sp):
                    for hf, ji, jo, tb, ob in halves():
                        for it in items(sp, HALF, ji):
                            if not (hf == 0 and is_early(it)):
                                load(sp, it, w_in[bass.ds(it.t + tb, 1), :, :].rearrange("a p n -> p (a n)"), n_in)
                        for it in items(sp, KD, jo):
                            load(sp, it, w_out[bass.ds(it.t + ob, 1), :, :].rearrange("a p n -> p (a n)"), n_out)
                    load_ahead(sp, next_phase, jb + 2 * per_half)

                @block.gpsimd
                def _(pool):
                    split_lo(pool, Item(0, 0, jb, 0), n_in)
                    normed_split_pool(pool, s, KD, hn, lambda k: hhi[:, k, :], lambda k: hlo[:, k, :])
                    for hf, ji, jo, tb, ob in halves():
                        for it in items(pool, HALF, ji):
                            if not (hf == 0 and isinstance(it.t, int) and it.t == 0):
                                split_lo(pool, it, n_in)
                        for it in items(pool, KD, jo):
                            split_lo(pool, it, n_out)

                def conv_act(act, it, tb):
                    u = it.t + tb
                    act.wait_ge(w_used, it.j + 1)
                    wait(act, silu_done, u - 1)
                    nc.scalar.activation(cv[:, it.slot, :], ps_g[it.slot][:, :], ACT.Identity,
                                         scale=V("conv_w", u + (layer * 3 + 2) * 2 * HALF),
                                         bias=V("conv_b", u + layer * 2 * HALF)).then_inc(tap2, 1)
                    act.wait_ge(conv_done, u + 1)
                    wait(act, gated, u - 1)
                    nc.scalar.activation(sl[:, it.slot, :], cv[:, it.slot, :], ACT.Silu).then_inc(silu_done, 1)

                @block.scalar
                def _(act):
                    split_hi(act, Item(0, 0, jb, 0), n_in)
                    norm_act_rstd(act, s, KD, ps_n, rstd)
                    normed_split_act(act, s, KD, hn, lambda k: hhi[:, k, :])
                    for hf, ji, jo, tb, ob in halves():
                        for it in items(act, HALF, ji):
                            if not (hf == 0 and isinstance(it.t, int) and it.t == 0):
                                split_hi(act, it, n_in)
                            if not (isinstance(it.t, int) and it.t == 0):
                                conv_act(act, it.prev, tb)
                        split_hi(act, Item(0, 0, jo, 0), n_out)
                        conv_act(act, Item(HALF - 1, HALF - 1, ji, 0), tb)
                        for it in items(act, KD, jo):
                            if not (isinstance(it.t, int) and it.t == 0):
                                split_hi(act, it, n_out)
                                if hf == 1:
                                    square_act(act, next_norm, it.prev, added, KD)
                    square_act(act, next_norm, Item(KD - 1, KD - 1, jo, 0), added, KD)

                @block.vector
                def _(dve):
                    normed_split_dve(dve, s, KD, xk, lambda k: V("norm_ffn", layer * KD + k), rstd, hn)
                    for hf, ji, jo, tb, ob in halves():
                        for it in items(dve, HALF, ji):
                            u, b = it.t + tb, it.slot
                            dve.wait_ge(tap2, u + 1)
                            nc.vector.scalar_tensor_tensor(
                                out=cv[:, b, 1:T], in0=ps_g[b][:, 0:T - 1], scalar=V("conv_w", u + (layer * 3 + 1) * 2 * HALF),
                                in1=cv[:, b, 1:T], op0=ALU.mult, op1=ALU.add).then_inc(tap1, 1)
                            dve.wait_ge(tap1, u + 1)
                            nc.vector.scalar_tensor_tensor(
                                out=cv[:, b, 2:T], in0=ps_g[b][:, 0:T - 2], scalar=V("conv_w", u + (layer * 3) * 2 * HALF),
                                in1=cv[:, b, 2:T], op0=ALU.mult, op1=ALU.add).then_inc(conv_done, 1)
                            dve.wait_ge(silu_done, u + 1)
                            wait(dve, act_lo, u - 1)
                            nc.vector.tensor_tensor(ga[:, b, :], ps_u[b][:, :], sl[:, b, :], ALU.mult).then_inc(gated, 1)
                            dve.wait_ge(gated, u + 1)
                            nc.vector.tensor_copy(dyn(ahi, it.t), ga[:, b, :]).then_inc(act_hi, 1)
                            dve.wait_ge(act_hi, u + 1)
                            nc.vector.tensor_tensor(dyn(alo, it.t), ga[:, b, :], dyn(ahi, it.t).bitcast(F32),
                                                    ALU.subtract).then_inc(act_lo, 1)
                        for it in items(dve, KD, jo):
                            dve.wait_ge(w_used, it.j + 1)
                            nc.vector.tensor_tensor(xk(it.t), ps_y[it.slot][:, :], xk(it.t), ALU.add).then_inc(added, 1)
                            if hf == 1:
                                square_dve(dve, next_norm, it)

                @block.tensor
                def _(pe):
                    norm_pe(pe, s, KD, square_sum, ps_n)
                    for hf, ji, jo, tb, ob in halves():
                        for it in items(pe, HALF, ji):
                            b = it.slot
                            pe.wait_ge(w_lo_ready, it.j + 1)
                            wait(pe, gated, it.t + tb - 1)
                            for k in range(KD):
                                if hf == 0 and isinstance(it.t, int) and it.t == 0:
                                    pe.wait_ge(s["lo"], k + 1)
                                three(ps_g[b][:, :], k * P, P, hhi[:, k, :], hlo[:, k, :], b, k == 0, k == KD - 1)
                            for k in range(KD):
                                last = three(ps_u[b][:, :], (KD + k) * P, P, hhi[:, k, :], hlo[:, k, :], b, k == 0, k == KD - 1)
                            last.then_inc(w_used, 1)
                        for it in items(pe, KD, jo):
                            b = it.slot
                            pe.wait_ge(w_lo_ready, it.j + 1)
                            wait(pe, added, it.t + ob - 1)
                            for f in range(HALF):
                                if isinstance(it.t, int) and it.t == 0:
                                    pe.wait_ge(act_lo, tb + f + 1)
                                last = three(ps_y[b][:, :], f * P, P, ahi[:, f, :], alo[:, f, :], b, f == 0, f == HALF - 1)
                            last.then_inc(w_used, 1)
            j_used[0] += 2 * per_half

        def attention():
            j0 = j_used[0]
            n_lat = KQ + KKV + 1
            NP = HEADS // 2
            with phase() as st:
                cos, sin = sbuf(st, "cos", [P, T]), sbuf(st, "sin", [P, T])
                qhi, qlo = sbuf(st, "qlat_hi", [P, KQ, T], F32R), sbuf(st, "qlat_lo", [P, KQ, T], F32R)
                chi, clo = sbuf(st, "clat_hi", [P, KKV, T], F32R), sbuf(st, "clat_lo", [P, KKV, T], F32R)
                krope = sbuf(st, "krope", [P, T])
                ohi, olo = sbuf(st, "attn_ohi", [P, HEADS, T], F32R), sbuf(st, "attn_olo", [P, HEADS, T], F32R)

                with phase() as s1:
                    ring(s1, "m")
                    sq, rstd = square, sbuf(s1, "m_rstd", [P, T])
                    hn = sbuf(s1, "m_hn", [P, 2, T])
                    hhi, hlo = sbuf(s1, "m_hhi", [P, KD, T], F32R), sbuf(s1, "m_hlo", [P, KD, T], F32R)
                    lat = sbuf(s1, "lat", [P, n_lat, T])
                    pos_i, ang, turns, red = sbuf(s1, "pos_i", [P, T], I32), sbuf(s1, "ang", [P, T]), sbuf(s1, "turns", [P, T]), sbuf(s1, "red", [P, T])
                    rq, rc = sbuf(s1, "rstd_q", [P, T]), sbuf(s1, "rstd_c", [P, T])
                    ktmp = sbuf(s1, "ktmp", [P, 2, T])
                    ps = [psum(s1, f"lat_ps{b}") for b in range(2)]
                    ps_n, ps_q, ps_c, ps_r = (psum(s1, f"m_{n}") for n in ("ss", "ssq", "ssc", "krot"))
                    s, sq_s, sc_s = norm_sems("m"), norm_sems("mq"), norm_sems("mc")
                    lat_out, angles, tables, krot, kmul = (sem(n) for n in ("lat_out", "angles", "tables", "krot", "kmul"))
                    pos_loaded = sem("pos_loaded")
                    n = KD * P
                    block = s1.enter_context(nc.Block(no_gpsimd_drain=True))

                    @block.sync
                    def _(sp):
                        sp.dma_start(pos_i[:, :], a["positions"]).then_inc(pos_loaded, 16)
                        sp.dma_start(vec[:, :], a["vec"]).then_inc(con_loaded, 16)
                        sp.dma_start(x[:, :, :], a["x"]).then_inc(x_loaded, 16)
                        sp.dma_start(con[:, :], a["con"]).then_inc(con_loaded, 16)
                        for it in items(sp, n_lat, j0):
                            load(sp, it, a["w_lat"][bass.ds(it.t, 1), :, :].rearrange("a p n -> p (a n)"), n)
                        load_ahead(sp, "p", j0 + n_lat)

                    @block.scalar
                    def _(act):
                        act.wait_ge(x_loaded, 16)
                        act.wait_ge(con_loaded, 32)
                        norm_act(act, s, KD, xk, sq, rstd)
                        for it in early_items(j0):
                            split_hi(act, it, n)
                        norm_act_rstd(act, s, KD, ps_n, rstd)
                        normed_split_act(act, s, KD, hn, lambda k: hhi[:, k, :])

                        def out(it):
                            act.wait_ge(w_used, it.j + 1)
                            nc.scalar.copy(dyn(lat, it.t), ps[it.slot][:, :]).then_inc(lat_out, 1)
                        for it in items(act, n_lat, j0):
                            if not is_early(it):
                                split_hi(act, it, n)
                            if not (isinstance(it.t, int) and it.t == 0):
                                out(it.prev)
                        out(Item(n_lat - 1, n_lat - 1, j0, 0))
                        act.wait_ge(lat_out, n_lat)
                        norm_act(act, sq_s, KQ, lambda k: lat[:, k, :], sq, rq)
                        act.wait_ge(sq_s["ss_added"], KQ - 1)
                        norm_act(act, sc_s, KKV, lambda k: lat[:, KQ + k, :], sq, rc)
                        norm_act_rstd(act, sq_s, KQ, ps_q, rq)
                        norm_act_rstd(act, sc_s, KKV, ps_c, rc)
                        normed_split_act(act, sq_s, KQ, hn, lambda k: qhi[:, k, :])
                        normed_split_act(act, sc_s, KKV, hn, lambda k: chi[:, k, :])
                        act.wait_ge(angles, 1)
                        nc.scalar.activation(sin[:, :], turns[:, :], ACT.Sin).then_inc(tables, 1)
                        act.wait_ge(angles, 2)
                        nc.scalar.activation(cos[:, :], red[:, :], ACT.Sin).then_inc(tables, 1)

                    @block.gpsimd
                    def _(pool):
                        for it in early_items(j0):
                            split_lo(pool, it, n)
                        normed_split_pool(pool, s, KD, hn, lambda k: hhi[:, k, :], lambda k: hlo[:, k, :])
                        for it in items(pool, n_lat, j0):
                            if not is_early(it):
                                split_lo(pool, it, n)
                        normed_split_pool(pool, sq_s, KQ, hn, lambda k: qhi[:, k, :], lambda k: qlo[:, k, :])
                        normed_split_pool(pool, sc_s, KKV, hn, lambda k: chi[:, k, :], lambda k: clo[:, k, :])

                    @block.vector
                    def _(dve):
                        chain = Chain(dve, sem("angle_chain"))
                        dve.wait_ge(pos_loaded, 16)
                        dve.wait_ge(con_loaded, 32)
                        chain(nc.vector.tensor_copy(ang[:, :], pos_i[:, :]))
                        chain(nc.vector.tensor_scalar(ang[:, :], ang[:, :], V("inv_freq", 0), None, ALU.mult))
                        magic = float(3 << 22)
                        step1 = 6.28125
                        step2 = float(np.float32(round((2 * np.pi - step1) * 2 ** 20) / 2 ** 20))
                        step3 = float(np.float32(2 * np.pi - step1 - step2))
                        pi_in = float(np.nextafter(np.float32(np.pi), np.float32(0)))
                        for dst, shift, quarter in ((turns, 0.0, 0.0), (red, 0.25, float(np.pi / 2))):
                            chain(nc.vector.tensor_scalar(dst[:, :], ang[:, :], float(1 / (2 * np.pi)), shift, ALU.mult, ALU.add))
                            chain(nc.vector.tensor_scalar(dst[:, :], dst[:, :], magic, None, ALU.add))
                            chain(nc.vector.tensor_scalar(ktmp[:, 0, :], dst[:, :], magic, None, ALU.subtract))
                            chain(nc.vector.scalar_tensor_tensor(out=dst[:, :], in0=ktmp[:, 0, :], scalar=-step1, in1=ang[:, :], op0=ALU.mult, op1=ALU.add))
                            chain(nc.vector.scalar_tensor_tensor(out=dst[:, :], in0=ktmp[:, 0, :], scalar=-step2, in1=dst[:, :], op0=ALU.mult, op1=ALU.add))
                            chain(nc.vector.scalar_tensor_tensor(out=dst[:, :], in0=ktmp[:, 0, :], scalar=-step3, in1=dst[:, :], op0=ALU.mult, op1=ALU.add))
                            chain(nc.vector.tensor_scalar(dst[:, :], dst[:, :], quarter, pi_in, ALU.add, ALU.min))
                            nc.vector.tensor_scalar(dst[:, :], dst[:, :], -pi_in, None, ALU.max).then_inc(angles, 1)
                        dve.wait_ge(x_loaded, 16)
                        norm_dve(dve, s, KD, sq, rstd)
                        normed_split_dve(dve, s, KD, xk, lambda k: V("norm_mix", k), rstd, hn)
                        norm_dve(dve, sq_s, KQ, sq, rq)
                        norm_dve(dve, sc_s, KKV, sq, rc)
                        normed_split_dve(dve, sq_s, KQ, lambda k: lat[:, k, :], lambda k: V("q_norm", k), rq, hn)
                        dve.wait_ge(sq_s["lo"], KQ)
                        normed_split_dve(dve, sc_s, KKV, lambda k: lat[:, KQ + k, :], lambda k: V("kv_norm", k), rc, hn)
                        dve.wait_ge(tables, 2)
                        dve.wait_ge(krot, 1)
                        nc.vector.tensor_tensor(ktmp[:, 0, :], lat[:, n_lat - 1, :], cos[:, :], ALU.mult).then_inc(kmul, 1)
                        nc.vector.tensor_tensor(ktmp[:, 1, :], ps_r[:, :], sin[:, :], ALU.mult).then_inc(kmul, 1)
                        dve.wait_ge(kmul, 2)
                        nc.vector.tensor_tensor(krope[:, :], ktmp[:, 0, :], ktmp[:, 1, :], ALU.add).then_inc(kmul, 1)

                    @block.tensor
                    def _(pe):
                        pe.wait_ge(con_loaded, 32)
                        norm_pe(pe, s, KD, rstd, ps_n)
                        for it in items(pe, n_lat, j0):
                            pe.wait_ge(w_lo_ready, it.j + 1)
                            wait(pe, lat_out, it.t - 1)
                            for k in range(KD):
                                if isinstance(it.t, int) and it.t == 0:
                                    pe.wait_ge(s["lo"], k + 1)
                                last = three(ps[it.slot][:, :], k * P, P, hhi[:, k, :], hlo[:, k, :], it.slot, k == 0, k == KD - 1)
                            last.then_inc(w_used, 1)
                        pe.wait_ge(lat_out, n_lat)
                        nc.tensor.matmul(ps_r[:, :], C("rot"), lat[:, n_lat - 1, :], start=True, stop=True).then_inc(krot, 1)
                        norm_pe(pe, sq_s, KQ, rq, ps_q)
                        norm_pe(pe, sc_s, KKV, rc, ps_c)

                with phase() as s2:
                    jp = j0 + n_lat
                    ring(s2, "p")
                    qn, kn = sbuf(s2, "q_nope", [P, 2, T]), sbuf(s2, "k_nope", [P, 2, T])
                    qraw, qr = sbuf(s2, "q_rope_raw", [P, T]), sbuf(s2, "q_rope", [P, T])
                    qcos, qsin = sbuf(s2, "q_cos", [P, T]), sbuf(s2, "q_sin", [P, T])
                    v = sbuf(s2, "v", [P, QB, 2 * VDIM])
                    pexp = sbuf(s2, "p_exp", [P, 2, T])
                    pT = sbuf(s2, "p_T", [P, 2, QB, T])
                    mx, nmx, rs, ri = (sbuf(s2, n, [P, 2 * QB]) for n in ("mx", "nmx", "rowsum", "rinv"))
                    pp = [psum(s2, f"proj_ps{b}") for b in range(2)]
                    sc = [psum(s2, f"score_ps{b}") for b in range(2)]
                    tp = [psum(s2, f"pT_ps{b}") for b in range(2)]
                    op = [psum(s2, f"o_ps{b}") for b in range(2)]
                    S = {n: sem(n) for n in ("proj_done", "proj_out", "rot_done", "qrope_mul", "qrope_done", "score_done", "masked",
                                             "max_done", "nmax_done", "exp_done", "rinv_done", "p_norm", "pT_done", "pT_out",
                                             "o_done", "o_hi", "o_lo")}
                    NPR = 7
                    NB = 2 * QB
                    at_qn, at_qr = 0, KQ * 2 * P
                    at_kn = at_qr + KQ * P
                    at_v = at_kn + KKV * 2 * P
                    pairs = [Item(t, t, jp, 0) for t in range(NP)]
                    block = s2.enter_context(nc.Block(no_gpsimd_drain=True))

                    @block.sync
                    def _(sp):
                        for it in pairs:
                            if not is_early(it):
                                load(sp, it, a["w_pair"][bass.ds(it.t, 1), :, :].rearrange("a p n -> p (a n)"), SLOT)
                        load_ahead(sp, "mo", jp + NP)

                    @block.gpsimd
                    def _(pool):
                        for it in pairs:
                            split_lo(pool, it, SLOT)

                    @block.tensor
                    def _(pe):
                        def lat_product(it, step, w_at, kk, hi, lo, stride):
                            for k in range(kk):
                                last = three(pp[step % 2][:, :], w_at + k * stride, P, hi[:, k, :], lo[:, k, :], it.slot,
                                             k == 0, k == kk - 1)
                            last.then_inc(S["proj_done"], 1)

                        def value_product(it, g):
                            for tt in range(2):
                                tok = slice((2 * g + tt) * P, (2 * g + tt + 1) * P)
                                out = pp[(5 + g) % 2][:, tt * 2 * VDIM:(tt + 1) * 2 * VDIM]
                                for k in range(KKV):
                                    wv = slice(at_v + k * 2 * VDIM, at_v + (k + 1) * 2 * VDIM)
                                    nc.tensor.matmul(out, chi[:, k, tok], whi[it.slot][:, wv], start=k == 0, stop=False)
                                    nc.tensor.matmul(out, chi[:, k, tok], wlo[it.slot][:, wv], start=False, stop=False)
                                    last = nc.tensor.matmul(out, clo[:, k, tok], whi[it.slot][:, wv], start=False, stop=k == KKV - 1)
                            return last

                        def scores(t, n):
                            h, i = n // QB, n % QB
                            nk, qs, rows = (i + 1) * P, slice(i * P, (i + 1) * P), slice(h * ROPE, (h + 1) * ROPE)
                            wait(pe, S["exp_done"], NB * t + n - 1)
                            nc.tensor.matmul(sc[n % 2][:, 0:nk], qn[:, h, qs], kn[:, h, 0:nk], start=True, stop=False)
                            nc.tensor.matmul(sc[n % 2][:, 0:nk], qr[rows, qs], krope[rows, 0:nk], start=False,
                                             stop=True).then_inc(S["score_done"], 1)

                        def turn_p(t, n):
                            wait(pe, S["pT_out"], NB * t + n - 1)
                            pe.wait_ge(S["p_norm"], NB * t + n + 1)
                            for kb in range(n % QB + 1):
                                ks = slice(kb * P, (kb + 1) * P)
                                last = nc.tensor.transpose(tp[n % 2][:, ks], pexp[:, n % 2, ks], C("ident"))
                            last.then_inc(S["pT_done"], 1)

                        def value_sum(t, h):
                            pe.wait_ge(S["pT_out"], NB * t + QB * (h + 1))
                            wait(pe, S["o_lo"], 2 * t + h - 1)
                            for kb in range(QB):
                                last = nc.tensor.matmul(op[h][:, kb * P:T], v[:, kb, h * VDIM:(h + 1) * VDIM],
                                                        pT[:, h, kb, kb * P:T], start=kb == 0, stop=kb == QB - 1)
                            last.then_inc(S["o_done"], 1)

                        for it in pairs:
                            t = it.t
                            pe.wait_ge(w_lo_ready, it.j + 1)
                            wait(pe, S["proj_out"], NPR * t)
                            lat_product(it, 0, at_qn, KQ, qhi, qlo, 2 * P)
                            wait(pe, S["qrope_done"], t)
                            lat_product(it, 1, at_qn + P, KQ, qhi, qlo, 2 * P)
                            pe.wait_ge(S["proj_out"], NPR * t + 1)
                            lat_product(it, 2, at_qr, KQ, qhi, qlo, P)
                            pe.wait_ge(S["proj_out"], NPR * t + 2)
                            lat_product(it, 3, at_kn, KKV, chi, clo, 2 * P)
                            pe.wait_ge(S["proj_out"], NPR * t + 3)
                            lat_product(it, 4, at_kn + P, KKV, chi, clo, 2 * P)
                            pe.wait_ge(S["proj_out"], NPR * t + 4)
                            value_product(it, 0).then_inc(S["proj_done"], 1)
                            pe.wait_ge(S["proj_out"], NPR * t + 5)
                            value_product(it, 1).then_inc(w_used, 1)
                            pe.wait_ge(S["proj_out"], NPR * t + 6)
                            nc.tensor.matmul(pp[1][:, :], C("rot"), qraw[:, :], start=True, stop=True).then_inc(S["rot_done"], 1)
                            pe.wait_ge(S["proj_out"], NPR * t + 7)
                            pe.wait_ge(S["qrope_done"], t + 1)
                            for n in range(NB + 1):
                                if n < NB:
                                    scores(t, n)
                                if n > 0:
                                    turn_p(t, n - 1)
                                if n == QB + 2:
                                    value_sum(t, 0)
                            value_sum(t, 1)

                    @block.scalar
                    def _(act):
                        def exps(t, n):
                            act.wait_ge(S["nmax_done"], NB * t + n + 1)
                            wait(act, S["pT_done"], NB * t + n - 1)
                            nk = (n % QB + 1) * P
                            nc.scalar.activation(pexp[:, n % 2, 0:nk], sc[n % 2][:, 0:nk], ACT.Exp, scale=SCALE,
                                                 bias=nmx[:, n:n + 1], accum_out=rs[:, n:n + 1]).then_inc(S["exp_done"], 1)

                        def turned_out(t, n):
                            act.wait_ge(S["pT_done"], NB * t + n + 1)
                            h, i = n // QB, n % QB
                            wait(act, S["o_done"], 2 * t + h - 1)
                            nc.scalar.copy(pT[:, h, 0:i + 1, i * P:(i + 1) * P],
                                           tp[n % 2][:, 0:(i + 1) * P].rearrange("p (k q) -> p k q", q=P)).then_inc(S["pT_out"], 1)

                        def out_hi(t, h):
                            act.wait_ge(S["o_done"], 2 * t + h + 1)
                            nc.scalar.copy(dyn(ohi, 2 * t + h), op[h][:, :]).then_inc(S["o_hi"], 1)

                        for it in pairs:
                            t = it.t
                            if t == 0:
                                split_hi(act, it, SLOT)
                            for step, dst in enumerate((qn[:, 0, :], qn[:, 1, :], qraw[:, :], kn[:, 0, :], kn[:, 1, :])):
                                act.wait_ge(S["proj_done"], (NPR - 1) * t + step + 1)
                                nc.scalar.copy(dst, pp[step % 2][:, :]).then_inc(S["proj_out"], 1)
                            for g in range(2):
                                if g == 0:
                                    act.wait_ge(S["proj_done"], (NPR - 1) * t + 6)
                                else:
                                    act.wait_ge(w_used, it.j + 1)
                                nc.scalar.copy(v[:, 2 * g:2 * g + 2, :], pp[(5 + g) % 2][:, :].rearrange("p (a n) -> p a n", a=2)).then_inc(S["proj_out"], 1)
                            for n in range(NB):
                                if n == 3 and t + 1 < NP:
                                    split_hi(act, pairs[t + 1], SLOT)
                                exps(t, n)
                                if n >= 2:
                                    turned_out(t, n - 2)
                            turned_out(t, NB - 2)
                            out_hi(t, 0)
                            turned_out(t, NB - 1)
                            out_hi(t, 1)

                    @block.vector
                    def _(dve):
                        def row_max(t, n):
                            i = n % QB
                            nk, diag = (i + 1) * P, slice(i * P, (i + 1) * P)
                            dve.wait_ge(S["score_done"], NB * t + n + 1)
                            nc.vector.tensor_tensor(sc[n % 2][:, diag], sc[n % 2][:, diag], C("causal"), ALU.add).then_inc(S["masked"], 1)
                            dve.wait_ge(S["masked"], NB * t + n + 1)
                            nc.vector.reduce_max(mx[:, n:n + 1], sc[n % 2][:, 0:nk], AX_X).then_inc(S["max_done"], 1)
                            dve.wait_ge(S["max_done"], NB * t + n + 1)
                            nc.vector.tensor_scalar(nmx[:, n:n + 1], mx[:, n:n + 1], -SCALE, None, ALU.mult).then_inc(S["nmax_done"], 1)

                        def normalize(t, n):
                            nk = (n % QB + 1) * P
                            dve.wait_ge(S["exp_done"], NB * t + n + 1)
                            nc.vector.reciprocal(ri[:, n:n + 1], rs[:, n:n + 1]).then_inc(S["rinv_done"], 1)
                            dve.wait_ge(S["rinv_done"], NB * t + n + 1)
                            nc.vector.tensor_scalar(pexp[:, n % 2, 0:nk], pexp[:, n % 2, 0:nk], ri[:, n:n + 1], None,
                                                    ALU.mult).then_inc(S["p_norm"], 1)

                        def out_lo(t, h):
                            dve.wait_ge(S["o_hi"], 2 * t + h + 1)
                            nc.vector.tensor_tensor(dyn(olo, 2 * t + h), op[h][:, :], dyn(ohi, 2 * t + h).bitcast(F32),
                                                    ALU.subtract).then_inc(S["o_lo"], 1)

                        for it in pairs:
                            t = it.t
                            dve.wait_ge(S["proj_out"], NPR * t + 3)
                            nc.vector.tensor_tensor(qcos[:, :], qraw[:, :], cos[:, :], ALU.mult).then_inc(S["qrope_mul"], 1)
                            dve.wait_ge(S["rot_done"], t + 1)
                            nc.vector.tensor_tensor(qsin[:, :], pp[1][:, :], sin[:, :], ALU.mult).then_inc(S["qrope_mul"], 1)
                            dve.wait_ge(S["qrope_mul"], 2 * t + 2)
                            nc.vector.tensor_tensor(qr[:, :], qcos[:, :], qsin[:, :], ALU.add).then_inc(S["qrope_done"], 1)
                            for n in range(NB):
                                row_max(t, n)
                                if n > 0:
                                    normalize(t, n - 1)
                            normalize(t, NB - 1)
                            out_lo(t, 0)
                            out_lo(t, 1)
                j_used[0] = jp + NP
                project_residual("mo", a["w_attn_out"], ohi, olo, "f0")

        def rwkv():
            j0 = j_used[0]
            with phase() as st:
                kvr = nc.dram_tensor("kvr", (P, KD, 3, T), F32).ap()
                th, la = sbuf(st, "w_lora", [LW, T]), sbuf(st, "a_lora", [LW, T])
                lga, lgb = sbuf(st, "g_lora_a", [P, T]), sbuf(st, "g_lora_b", [LG - P, T])

                with phase() as s1:
                    ring(s1, "r")
                    h = sbuf(s1, "h", [P, KD, T])
                    out_buf = sbuf(s1, "rkv_out", [P, 2, T])
                    xx = sbuf(s1, "shift_diff", [P, KD, T])
                    xm = sbuf(s1, "mixed", [P, 4, T])
                    xhi, xlo = sbuf(s1, "mixed_hi", [P, 2, KD, T], F32R), sbuf(s1, "mixed_lo", [P, 2, KD, T], F32R)
                    l1 = sbuf(s1, "lora_in", [P, KD, 2 * LW + LG])
                    rstd = out_buf[:, 0, :]
                    ps = [psum(s1, f"rkv_ps{b}") for b in range(2)]
                    ps_n, ps_w, ps_a, ps_ga, ps_gb = (psum(s1, f"r_{n}") for n in ("ss", "lw", "la", "lga", "lgb"))
                    s = norm_sems("r")
                    lora_loaded, normed, shifted, mixed, m_hi, m_lo, lora_used, rkv_out, lora_out = (
                        sem(f"r_{n}") for n in ("lora_loaded", "normed", "shifted", "mixed", "mix_hi", "mix_lo", "lora_used", "rkv_out", "lora_out"))
                    n = KD * P
                    NL = 3
                    MIXES = (3, 4, 5, 1, 0, 2)
                    stored = [sem("rkv_stored0"), sem("rkv_stored1")]
                    block = s1.enter_context(nc.Block(no_gpsimd_drain=True))

                    @block.sync
                    def _(sp):
                        sp.dma_start(l1[:, :, :], a["lora_in"].rearrange("p (k n) -> p k n", k=KD)).then_inc(lora_loaded, 16)
                        for q in range(3):
                            for it in items(sp, KD, j0 + q * KD):
                                if not (q == 0 and is_early(it)):
                                    load(sp, it, a["w_rkv"][bass.ds(it.t + q * KD, 1), :, :].rearrange("a p n -> p (a n)"), n)

                    @block.vector
                    def _(dve):
                        def mix(q, k):
                            u = q * KD + k
                            slot = u % 4 if q <= NL else k % 2
                            dve.wait_ge(shifted, 2 * k + 2)
                            if q > NL:
                                dve.wait_ge(m_lo, (q - NL) * KD + k - 1)
                            elif u - 4 >= NL * KD:
                                dve.wait_ge(m_lo, u - 4 - NL * KD + 1)
                            elif u >= 4:
                                dve.wait_ge(lora_used, u - 3)
                            nc.vector.scalar_tensor_tensor(out=xm[:, slot, :], in0=xx[:, k, :], scalar=V("mix", MIXES[q] * KD + k),
                                                           in1=h[:, k, :], op0=ALU.mult, op1=ALU.add).then_inc(mixed, 1)
                        dve.wait_ge(s["rstd"], 1)
                        for k in range(KD):
                            nc.vector.scalar_tensor_tensor(out=h[:, k, :], in0=xk(k), scalar=V("norm_mix", KD + k), in1=rstd[:, :],
                                                           op0=ALU.mult, op1=ALU.mult).then_inc(normed, 1)
                        for q in range(len(MIXES)):
                            for k in range(KD):
                                mix(q, k)

                    @block.scalar
                    def _(act):
                        norm_act_rstd(act, s, KD, ps_n, rstd)
                        for it in early_items(j0):
                            split_hi(act, it, n)
                        act.wait_ge(lora_used, KD)
                        nc.scalar.activation(th[:, :], ps_w[0:LW, :], ACT.Tanh).then_inc(lora_out, 1)
                        act.wait_ge(lora_used, 2 * KD)
                        nc.scalar.copy(la[:, :], ps_a[0:LW, :]).then_inc(lora_out, 1)
                        act.wait_ge(lora_used, 3 * KD)
                        nc.scalar.activation(lga[:, :], ps_ga[:, :], ACT.Sigmoid).then_inc(lora_out, 1)
                        nc.scalar.activation(lgb[:, :], ps_gb[0:LG - P, :], ACT.Sigmoid).then_inc(lora_out, 1)
                        def mix_hi(q, k, slot):
                            act.wait_ge(mixed, (NL + q) * KD + k + 1)
                            nc.scalar.copy(dyn(xhi[:, q % 2, :, :], k), xm[:, slot, :]).then_inc(m_hi, 1)
                        for k in range(KD):
                            mix_hi(0, k, k % 4)
                        for q in range(3):
                            def out(it):
                                b = it.slot
                                before = it.turn - j0 // 2 - (b < j0 % 2)
                                act.wait_ge(w_used, it.j + 1)
                                wait(act, stored[b], 16 * before)
                                nc.scalar.copy(out_buf[:, b, :], ps[b][:, :]).then_inc(rkv_out, 1)
                                act.wait_ge(rkv_out, it.t + q * KD + 1)
                                act.dma_start(kvr[:, bass.ds(it.t, 1), q, :].rearrange("p a t -> p (a t)"), out_buf[:, b, :]).then_inc(stored[b], 16)
                            for it in items(act, KD, j0 + q * KD):
                                if not (is_early(it) if q == 0 else isinstance(it.t, int) and it.t == 0):
                                    split_hi(act, it, n)
                                if not (isinstance(it.t, int) and it.t == 0):
                                    out(it.prev)
                                if q < 2:
                                    mix_hi(q + 1, it.t, (it.slot + j0) % 2)
                            if q < 2:
                                split_hi(act, Item(0, 0, j0 + (q + 1) * KD, 0), n)
                            out(Item(KD - 1, KD - 1, j0 + q * KD, 0))
                        for b in range(2):
                            act.wait_ge(stored[b], 16 * (3 * KD // 2))

                    @block.gpsimd
                    def _(pool):
                        def mix_lo(q, k, slot):
                            pool.wait_ge(m_hi, q * KD + k + 1)
                            nc.gpsimd.tensor_tensor(dyn(xlo[:, q % 2, :, :], k), xm[:, slot, :],
                                                    dyn(xhi[:, q % 2, :, :], k).bitcast(F32), ALU.subtract).then_inc(m_lo, 1)
                        for k in range(KD):
                            pool.wait_ge(normed, k + 1)
                            nc.gpsimd.tensor_tensor(xx[:, k, 1:T], h[:, k, 0:T - 1], h[:, k, 1:T], ALU.subtract).then_inc(shifted, 1)
                            nc.gpsimd.tensor_scalar(xx[:, k, 0:1], h[:, k, 0:1], -1.0, None, ALU.mult).then_inc(shifted, 1)
                        for it in early_items(j0):
                            split_lo(pool, it, n)
                        for k in range(KD):
                            mix_lo(0, k, k % 4)
                        for q in range(3):
                            for it in items(pool, KD, j0 + q * KD):
                                if not (q == 0 and is_early(it)):
                                    split_lo(pool, it, n)
                                if q < 2:
                                    mix_lo(q + 1, it.t, (it.slot + j0) % 2)

                    @block.tensor
                    def _(pe):
                        norm_pe(pe, s, KD, square_sum, ps_n)
                        pe.wait_ge(lora_loaded, 16)
                        for q, (at, m, out) in enumerate(((0, LW, ps_w), (LW, LW, ps_a), (2 * LW, LG, ps_ga))):
                            for k in range(KD):
                                u = q * KD + k
                                pe.wait_ge(mixed, u + 1)
                                last = nc.tensor.matmul(out[0:min(m, P), :], l1[:, k, at:at + min(m, P)], xm[:, u % 4, :],
                                                        start=k == 0, stop=k == KD - 1)
                                if m > P:
                                    last = nc.tensor.matmul(ps_gb[0:m - P, :], l1[:, k, at + P:at + m], xm[:, u % 4, :],
                                                            start=k == 0, stop=k == KD - 1)
                                last.then_inc(lora_used, 1)
                        for q in range(3):
                            for it in items(pe, KD, j0 + q * KD):
                                pe.wait_ge(w_lo_ready, it.j + 1)
                                wait(pe, rkv_out, it.t + q * KD - 1)
                                for k in range(KD):
                                    if isinstance(it.t, int) and it.t == 0:
                                        pe.wait_ge(m_lo, q * KD + k + 1)
                                    last = three(ps[it.slot][:, :], k * P, P, xhi[:, q % 2, k, :], xlo[:, q % 2, k, :], it.slot, k == 0, k == KD - 1)
                                last.then_inc(w_used, 1)
                j_used[0] += 3 * KD
                o_all = sbuf(st, "wkv_out", [P, KD, T])
                wkv(kvr, th, la, lga, lgb, o_all)
                ohi, olo = sbuf(st, "wkv_ohi", [P, KD, T], F32R), sbuf(st, "wkv_olo", [P, KD, T], F32R)
                project_residual("ro", a["w_rwkv_out"], ohi, olo, "f1", o_all)

        def wkv(kvr, th, la, lga, lgb, o_all):
            with phase() as st:
                LANES = 2
                HR = (slice(0, CH), slice(CH, P))
                VR = HR
                UR = (HR[1], HR[0])
                LEVELS = 5
                NT = 15
                work = sbuf(st, "work", [P, LANES * NT - 8, T])

                def tile(i):
                    return raw[i // 4][:, (i % 4) * T:(i % 4 + 1) * T] if i < 8 else work[:, i - 8, :]

                def ch(t2):
                    return t2.rearrange("p (c s) -> p c s", s=CH)

                def flat(t3):
                    return t3.rearrange("p a s -> p (a s)")

                class Lane:

                    def __init__(self, p):
                        def b(name, shape):
                            return sbuf(st, f"{name}{p}", shape)
                        (self.d, self.rate, self.D, self.Dc, self.gate, self.eR, self.eK, self.kk, self.rn,
                         self.kp, self.b1, self.bonus, self.prob, self.kk2, self.rk) = (tile(p * NT + i) for i in range(NT))
                        self.Dp = self.d
                        self.eA = self.d
                        self.inv, self.tt = self.kp, self.b1
                        self.y, self.yc, self.yc2, self.out = self.eR, self.eK, self.prob, self.prob
                        self.krv = b("krv", [P, 3, T])
                        self.lw = b("lora_out", [P, 4 * P])
                        self.AR = b("AR", [P, NC, 2, 2, CH])
                        self.KB = b("KB", [P, NC, 2, CH])
                        self.KBT = b("KBT", [P, NC, P])
                        self.VU = b("VU", [P, NC, 2, CH])
                        self.G = b("G", [P, NC, 2, 2, CH])
                        self.Lm = b("L_masked", [P, 2, NC, CH])
                        self.R = b("R", [P, CH])
                        self.Sp, self.Sg = b("S", [P, 2, CH]), b("S_decayed", [P, CH])
                        self.gs = b("chunk_decay", [P, NC])
                        self.B = [psum(st, f"wkv_ps{p}_{i}") for i in range(4)]
                        names = ("loaded", "zeroed", "lora_done", "gate_done", "lora_ev", "v_done", "v_out", "dc_done", "dp_done",
                                 "gs_done", "exps", "gs_exp", "kk2_done", "ss_done", "rn_max", "rn_ln", "rn_done", "rk_done",
                                 "bonus_done", "bonus_out", "ar_done", "kb_done", "b1_done", "kk_done", "kbt_done", "kbt_out", "gram_done",
                                 "gram_out", "lm_done", "x_ready", "tt_done", "tt_out", "pl_done", "p_new",
                                 "rhs_done", "rhs_out", "u_done", "u_out0", "u_out1", "s_done", "s_new", "y_done", "y_out",
                                 "mu_done", "yc_done", "yc2_done", "var_done", "var_ln", "rstd_done", "finished")
                        self.S = {n: sem(f"k{p}_{n}") for n in names}
                        self.chain_sem, self.out_sem = sem(f"k{p}_chain"), sem(f"k{p}_out_chain")

                lanes = [Lane(p) for p in range(LANES)]

                def turns(eng, steps, mean, variance, output):
                    each = {}

                    def turn(i, behind):
                        chains = [Chain(eng, ln.chain_sem, i * each[n] if each else 0) for n, ln in enumerate(lanes)]
                        for _ in zip(*(steps(ln, i, LANES * i + p, chains[p], behind) for p, ln in enumerate(lanes)), strict=True):
                            pass
                        return chains
                    chains = turn(0, False)
                    each.update({p: c.n for p, c in enumerate(chains)})
                    with eng.Fori(1, KD // LANES) as i:
                        turn(i, True)
                    for part in (mean, variance, output):
                        for p, ln in enumerate(lanes):
                            part(ln, KD // LANES - 1, KD - LANES + p)

                block = st.enter_context(nc.Block(no_gpsimd_drain=True))

                @block.sync
                def _(sp):
                    def loads(ln, i, c):
                        wait(sp, ln.S["gram_done"], i)
                        sp.dma_start(ln.lw[:, :], a["lora_out"][bass.ds(c, 1), :, :].rearrange("a p n -> p (a n)")).then_inc(ln.S["loaded"], 16)
                        sp.dma_start(ln.krv[:, :, :], kvr[:, bass.ds(c, 1), :, :].rearrange("p a k t -> p (a k) t")).then_inc(ln.S["loaded"], 16)
                    for p, ln in enumerate(lanes):
                        loads(ln, 0, p)
                    with sp.Fori(1, KD // LANES) as i:
                        for p, ln in enumerate(lanes):
                            loads(ln, i, LANES * i + p)
                    first = Item(0, 0, j_used[0], 0)
                    assert first.slot == 0
                    sp.wait_ge(lanes[0].S["gram_done"], KD // LANES)
                    load(sp, first, a["w_rwkv_out"][0, :, :], KD * P)

                @block.tensor
                def _(pe):
                    mm = nc.tensor.matmul

                    regs = [pe.alloc_register(f"pe_count{n}") for n in range(2)]

                    def small(*counts):
                        if not all(isinstance(n, int) for n in counts):
                            for r, n in zip(regs, counts):
                                pe.reg_mov(r, n)
                            counts = regs
                        pe.wait_ge(con_loaded, 32)
                        return counts

                    def mean(ln, i, c):
                        pe.wait_ge(ln.S["y_out"], i + 1)
                        mm(ln.B[3][:, :], C("headmean"), ln.y, start=True, stop=True).then_inc(ln.S["mu_done"], 1)

                    def variance(ln, i, c):
                        pe.wait_ge(ln.S["yc2_done"], i + 1)
                        mm(ln.B[3][:, :], C("headmean"), ln.yc2, start=True, stop=True).then_inc(ln.S["var_done"], 1)

                    def output(ln, i, c):
                        pass

                    def steps(ln, i, c, _, behind):
                        S, B = ln.S, ln.B
                        pe.wait_ge(S["loaded"], 32 * i + 32)
                        mm(B[0][:, :], ln.lw[0:LW, 0:P], th[:, :], start=True, stop=True)
                        mm(B[1][:, :], ln.lw[0:LW, P:2 * P], la[:, :], start=True, stop=True).then_inc(S["lora_done"], 1)
                        yield
                        if behind:
                            mean(ln, i - 1, None)
                        mm(B[2][:, :], ln.lw[:, 2 * P:3 * P], lga[:, :], start=True, stop=False)
                        mm(B[2][:, :], ln.lw[0:LG - P, 3 * P:4 * P], lgb[:, :], start=False, stop=True).then_inc(S["gate_done"], 1)
                        yield
                        if behind:
                            variance(ln, i - 1, None)
                        yield
                        if behind:
                            counts = small(i)
                            pe.wait_ge(S["var_ln"], counts[0])
                        for q in range(NC):
                            for hh in range(2):
                                last = mm(B[3][VR[hh], q * CH:(q + 1) * CH], ln.krv[HR[hh], 2, q * CH:(q + 1) * CH], C("ident64", CH, HR[hh]), start=True, stop=True)
                        last.then_inc(S["v_done"], 1)
                        yield
                        pe.wait_ge(S["lora_ev"], 3 * i + 3)
                        pe.wait_ge(S["kk2_done"], i + 1)
                        mm(B[0][:, :], C("headsum"), ln.kk2, start=True, stop=True).then_inc(S["ss_done"], 1)
                        pe.wait_ge(S["rk_done"], i + 1)
                        mm(B[1][:, :], C("headsum"), ln.rk, start=True, stop=True).then_inc(S["bonus_done"], 1)
                        yield
                        yield
                        pe.wait_ge(S["v_out"], 2 * i + 2)
                        pe.wait_ge(S["kb_done"], 4 * i + 4)
                        for q in range(NC):
                            last = nc.tensor.transpose(B[2 + q // 4][:, (q % 4) * P:(q % 4 + 1) * P], flat(ln.KB[:, q, :, :]), C("ident"))
                        last.then_inc(S["kbt_done"], 1)
                        yield
                        pe.wait_ge(S["ar_done"], 4 * i + 4)
                        pe.wait_ge(S["rn_max"], i + 1)
                        pe.wait_ge(S["bonus_out"], i + 1)
                        pe.wait_ge(S["kbt_out"], 2 * i + 2)
                        if isinstance(i, int):
                            pe.wait_ge(S["zeroed"], 1)
                        for q in range(NC):
                            last = mm(B[q // 2][:, (q % 2) * 2 * P:(q % 2 + 1) * 2 * P], flat(ln.KB[:, q, :, :]),
                                      ln.AR[:, q, :, :, :].rearrange("p h a s -> p (h a s)"), start=True, stop=True)
                        last.then_inc(S["gram_done"], 1)
                        yield
                        for l in range(LEVELS):
                            counts = small(2 * (LEVELS * i + l + 1), LEVELS * i + l + 1)
                            pe.wait_ge(S["lm_done"], counts[0])
                            pe.wait_ge(S["x_ready"], counts[1])
                            for q in range(NC):
                                for rows in HR:
                                    last = mm(B[0][rows, q * CH:(q + 1) * CH], ln.Lm[rows, l % 2, q, :], ch(ln.inv)[rows, q, :], start=True, stop=True)
                            last.then_inc(S["tt_done"], 1)
                            yield
                            counts = small(LEVELS * i + l + 1)
                            pe.wait_ge(S["tt_out"], counts[0])
                            for q in range(NC):
                                for rows in HR:
                                    last = mm(B[1][rows, q * CH:(q + 1) * CH], ch(ln.tt)[rows, q, :], ch(ln.prob)[rows, q, :], start=True, stop=True)
                            last.then_inc(S["pl_done"], 1)
                            yield
                        def outputs(q):
                            at = slice(q * CH, (q + 1) * CH)
                            for hh in range(2):
                                last = mm(B[3][HR[hh], at], ln.VU[:, q, hh, :], ln.G[:, q, hh, 1, :], start=True, stop=q == 0)
                                if q > 0:
                                    last = mm(B[3][HR[hh], at], ln.Sp[HR[hh], q % 2, :], ln.AR[HR[hh], q, hh, 1, :], start=False, stop=True)
                            return last
                        for q in range(NC):
                            if q == 0:
                                counts = small(LEVELS * i + LEVELS)
                                pe.wait_ge(S["p_new"], counts[0])
                            for hh in range(2):
                                last = mm(B[0][UR[hh], 0:CH], ln.G[VR[hh], q, hh, 0, :], ln.VU[VR[hh], q, hh, :], start=True, stop=q == 0)
                            if q > 0:
                                counts = small((NC - 1) * i + q)
                                pe.wait_ge(S["s_new"], counts[0])
                                for hh in range(2):
                                    last = mm(B[0][UR[hh], 0:CH], ln.AR[HR[hh], q, hh, 0, :], ln.Sp[HR[hh], q % 2, :], start=False, stop=True)
                            last.then_inc(S["rhs_done"], 1)
                            yield
                            if q > 0:
                                outputs(q - 1)
                            counts = small(NC * i + q + 1)
                            pe.wait_ge(S["rhs_out"], counts[0])
                            for rows in HR:
                                last = mm(B[1][rows, 0:CH], ch(ln.prob)[rows, q, :], ln.R[rows, :], start=True, stop=True)
                            last.then_inc(S["u_done"], 1)
                            yield
                            pe.wait_ge(S["u_out0"], NC * i + q + 1)
                            pe.wait_ge(S["u_out1"], NC * i + q + 1)
                            if q < NC - 1:
                                for hh in range(2):
                                    last = mm(B[2][HR[hh], 0:CH], ln.KBT[:, q, hh * CH:(hh + 1) * CH], ln.VU[:, q, hh, :], start=True, stop=True)
                                last.then_inc(S["s_done"], 1)
                            yield
                        outputs(NC - 1).then_inc(S["y_done"], 1)
                        yield

                    turns(pe, steps, mean, variance, output)

                @block.scalar
                def _(act):
                    A = nc.scalar

                    def mean(ln, i, c):
                        act.wait_ge(ln.S["y_done"], i + 1)
                        A.copy(ln.y, ln.B[3][:, :]).then_inc(ln.S["y_out"], 1)

                    def variance(ln, i, c):
                        act.wait_ge(ln.S["yc_done"], i + 1)
                        A.activation(ln.yc2, ln.yc, ACT.Square).then_inc(ln.S["yc2_done"], 1)

                    def output(ln, i, c):
                        act.wait_ge(ln.S["var_done"], i + 1)
                        A.activation(ln.rn, ln.B[3][:, :], ACT.Ln, bias=V("gn_eps", 0)).then_inc(ln.S["var_ln"], 1)
                        act.wait_ge(ln.S["var_ln"], i + 1)
                        A.activation(ln.rn, ln.rn, ACT.Exp, scale=-0.5).then_inc(ln.S["rstd_done"], 1)

                    def steps(ln, i, c, chain, behind):
                        S, B = ln.S, ln.B
                        if behind:
                            mean(ln, i - 1, None)
                        yield
                        act.wait_ge(S["lora_done"], i + 1)
                        A.activation(ln.d, B[0][:, :], ACT.Sigmoid, bias=V("w0", c)).then_inc(S["lora_ev"], 1)
                        A.activation(ln.rate, B[1][:, :], ACT.Sigmoid, bias=V("a0", c)).then_inc(S["lora_ev"], 1)
                        if behind:
                            variance(ln, i - 1, None)
                        yield
                        if behind:
                            act.wait_ge(S["var_done"], i)
                            A.activation(ln.rn, B[3][:, :], ACT.Ln, bias=V("gn_eps", 0)).then_inc(S["var_ln"], 1)
                        yield
                        if behind:
                            act.wait_ge(S["var_ln"], i)
                            A.activation(ln.rn, ln.rn, ACT.Exp, scale=-0.5).then_inc(S["rstd_done"], 1)
                        act.wait_ge(S["v_done"], i + 1)
                        for hh in range(2):
                            A.copy(ln.VU[VR[hh], :, hh, :], ch(B[3][VR[hh], :])).then_inc(S["v_out"], 1)
                        yield
                        wait(act, S["finished"], i)
                        act.wait_ge(S["gate_done"], i + 1)
                        A.copy(ln.gate, B[2][:, :]).then_inc(S["lora_ev"], 1)
                        act.wait_ge(S["dc_done"], i + 1)
                        A.activation(ln.eR, ln.Dc, ACT.Exp, scale=-KAPPA).then_inc(S["exps"], 1)
                        A.activation(ln.eK, ln.Dc, ACT.Exp, scale=KAPPA).then_inc(S["exps"], 1)
                        act.wait_ge(S["dp_done"], i + 1)
                        A.activation(ln.eA, ln.Dp, ACT.Exp, scale=-KAPPA).then_inc(S["exps"], 1)
                        act.wait_ge(S["gs_done"], i + 1)
                        A.activation(ln.gs[:, 0:NC - 1], ln.gs[:, 0:NC - 1], ACT.Exp, scale=-KAPPA).then_inc(S["gs_exp"], 1)
                        yield
                        act.wait_ge(S["rn_max"], i + 1)
                        A.activation(ln.rn, ln.rn, ACT.Ln).then_inc(S["rn_ln"], 1)
                        yield
                        act.wait_ge(S["rn_ln"], i + 1)
                        A.activation(ln.rn, ln.rn, ACT.Exp, scale=-0.5).then_inc(S["rn_done"], 1)
                        act.wait_ge(S["kbt_done"], i + 1)
                        for b in range(2):
                            A.copy(ln.KBT[:, 4 * b:4 * b + 4, :], B[2 + b][:, :].rearrange("p (c s) -> p c s", s=P)).then_inc(S["kbt_out"], 1)
                        yield
                        yield
                        for l in range(LEVELS):
                            act.wait_ge(S["tt_done"], LEVELS * i + l + 1)
                            A.copy(ln.tt, B[0][:, :]).then_inc(S["tt_out"], 1)
                            yield
                            yield
                        for q in range(NC):
                            act.wait_ge(S["rhs_done"], NC * i + q + 1)
                            A.copy(ln.R[:, :], B[0][:, 0:CH]).then_inc(S["rhs_out"], 1)
                            yield
                            act.wait_ge(S["u_done"], NC * i + q + 1)
                            A.copy(ln.VU[UR[0], q, 0, :], B[1][UR[0], 0:CH]).then_inc(S["u_out0"], 1)
                            yield
                            yield
                        yield

                    turns(act, steps, mean, variance, output)

                @block.gpsimd
                def _(pool):
                    G = nc.gpsimd
                    for ln in lanes:
                        G.memset(ln.AR[:, :, :, :, :], 0.0).then_inc(ln.S["zeroed"], 1)

                    def none(ln, i, c):
                        pass

                    def steps(ln, i, c, chain, behind):
                        S = ln.S
                        yield
                        yield
                        yield
                        yield
                        yield
                        yield
                        yield
                        yield
                        pool.wait_ge(S["gram_out"], 4 * i + 4)
                        for l in range(LEVELS):
                            if l > 1:
                                pool.wait_ge(S["tt_done"], LEVELS * i + l - 1)
                            for hh in range(2):
                                m = con[UR[hh], CON["levels"] + (l + 1) * CH:CON["levels"] + (l + 2) * CH].unsqueeze(1).to_broadcast([CH, NC, CH])
                                G.tensor_tensor(ln.Lm[UR[hh], l % 2, :, :], ln.G[UR[hh], :, hh, 0, :], m, ALU.mult).then_inc(S["lm_done"], 1)
                            yield
                            yield
                        for q in range(NC):
                            yield
                            yield
                            yield
                        yield
                    turns(pool, steps, none, none, none)

                @block.vector
                def _(dve):
                    X = nc.vector

                    def mean(ln, i, c):
                        pass

                    def variance(ln, i, c):
                        dve.wait_ge(ln.S["mu_done"], i + 1)
                        X.tensor_tensor(ln.yc, ln.y, ln.B[3][:, :], ALU.subtract).then_inc(ln.S["yc_done"], 1)

                    def output(ln, i, c):
                        chain = Chain(dve, ln.out_sem, 3 * i)
                        dve.wait_ge(ln.S["rstd_done"], i + 1)
                        chain(X.tensor_tensor(ln.out, ln.yc, ln.rn, ALU.mult))
                        chain(X.tensor_scalar(ln.out, ln.out, V("ln_w", c), V("ln_b", c), ALU.mult, ALU.add))
                        chain(X.tensor_tensor(ln.out, ln.out, ln.bonus, ALU.add))
                        X.tensor_tensor(dyn(o_all, c), ln.out, ln.gate, ALU.mult).then_inc(ln.S["finished"], 1)

                    def steps(ln, i, c, chain, behind):
                        S, B = ln.S, ln.B
                        k, r, v = ln.krv[:, 0, :], ln.krv[:, 1, :], ln.krv[:, 2, :]
                        if isinstance(i, int):
                            dve.wait_ge(S["zeroed"], 1)
                        dve.wait_ge(S["loaded"], 32 * i + 32)
                        chain(X.tensor_scalar(ln.kk, k, V("k_k", c), None, ALU.mult))
                        X.tensor_tensor(ln.kk2, ln.kk, ln.kk, ALU.mult).then_inc(S["kk2_done"], 1)
                        yield
                        dve.wait_ge(S["lora_ev"], 3 * i + 2)
                        chain(X.tensor_tensor_scan(ln.D, C("reset", T), ln.d, 0.0, ALU.mult, ALU.add))
                        mid = CH // 2 - 1
                        X.tensor_tensor(ch(ln.Dc), ch(ln.D), ch(ln.D)[:, :, mid:mid + 1].to_broadcast([P, NC, CH]), ALU.subtract).then_inc(S["dc_done"], 1)
                        chain(X.tensor_scalar(ln.kp, ln.rate, -1.0, V("k_a", c), ALU.add, ALU.mult))
                        chain(X.scalar_tensor_tensor(out=ln.kp, in0=ln.kp, scalar=1.0, in1=k, op0=ALU.add, op1=ALU.mult))
                        chain(X.tensor_tensor(ln.b1, ln.kk, ln.rate, ALU.mult))
                        X.scalar_tensor_tensor(out=ln.rk, in0=r, scalar=V("r_k", c), in1=ln.kp, op0=ALU.mult, op1=ALU.mult).then_inc(S["rk_done"], 1)
                        dve.wait_ge(S["dc_done"], i + 1)
                        X.tensor_tensor(ln.Dp, ln.Dc, ln.d, ALU.subtract).then_inc(S["dp_done"], 1)
                        X.tensor_tensor(ln.gs[:, 0:NC - 1], ch(ln.Dc)[:, 0:NC - 1, CH - 1], ch(ln.D)[:, 1:NC, mid], ALU.add).then_inc(S["gs_done"], 1)
                        if behind:
                            variance(ln, i - 1, None)
                        yield
                        yield
                        if behind:
                            output(ln, i - 1, c - LANES)
                            dve.wait_ge(S["finished"], i)
                        yield
                        dve.wait_ge(S["ss_done"], i + 1)
                        X.tensor_scalar(ln.rn, B[0][:, :], 1e-24, None, ALU.max).then_inc(S["rn_max"], 1)
                        dve.wait_ge(S["bonus_done"], i + 1)
                        X.tensor_tensor(ln.bonus, B[1][:, :], v, ALU.mult).then_inc(S["bonus_out"], 1)
                        yield
                        dve.wait_ge(S["exps"], 3 * i + 3)
                        for hh in range(2):
                            X.tensor_tensor(ln.KB[HR[hh], :, hh, :], ch(ln.kp)[HR[hh], :, :], ch(ln.eK)[HR[hh], :, :], ALU.mult).then_inc(S["kb_done"], 1)
                            X.tensor_tensor(ln.AR[HR[hh], :, hh, 1, :], ch(r)[HR[hh], :, :], ch(ln.eR)[HR[hh], :, :], ALU.mult).then_inc(S["ar_done"], 1)
                        X.tensor_tensor(ln.b1, ln.b1, ln.eK, ALU.mult).then_inc(S["b1_done"], 1)
                        X.tensor_tensor(ln.kk, ln.kk, ln.eA, ALU.mult).then_inc(S["kk_done"], 1)
                        yield
                        dve.wait_ge(S["rn_done"], i + 1)
                        dve.wait_ge(S["b1_done"], i + 1)
                        dve.wait_ge(S["kk_done"], i + 1)
                        for hh in range(2):
                            X.tensor_tensor(ln.KB[HR[hh], :, 1 - hh, :], ch(ln.b1)[HR[hh], :, :], ch(ln.rn)[HR[hh], :, :], ALU.mult).then_inc(S["kb_done"], 1)
                        for hh in range(2):
                            X.scalar_tensor_tensor(out=ln.AR[HR[hh], :, hh, 0, :], in0=ch(ln.kk)[HR[hh], :, :], scalar=-1.0,
                                                   in1=ch(ln.rn)[HR[hh], :, :], op0=ALU.mult, op1=ALU.mult).then_inc(S["ar_done"], 1)
                        yield
                        dve.wait_ge(S["gram_done"], i + 1)
                        masks = con[:, CON["strict"]:CON["strict"] + P].unsqueeze(1).to_broadcast([P, 4, P])
                        for n in range(4):
                            X.tensor_tensor(ln.G[:, 2 * n:2 * n + 2, :, :, :].rearrange("p c h a s -> p (c h) (a s)"),
                                            B[n][:, :].rearrange("p (n s) -> p n s", s=P), masks, ALU.mult).then_inc(S["gram_out"], 1)
                        dve.wait_ge(S["gram_out"], 4 * i + 4)
                        for hh in range(2):
                            m = con[UR[hh], CON["levels"]:CON["levels"] + CH].unsqueeze(1).to_broadcast([CH, NC, CH])
                            chain(X.tensor_tensor(ch(ln.prob)[UR[hh], :, :], ln.G[UR[hh], :, hh, 0, :], m, ALU.mult))
                        chain(X.tensor_tensor(ch(ln.prob), ch(ln.prob), C("ident64", CH).unsqueeze(1).to_broadcast([P, NC, CH]), ALU.add))
                        X.transpose(ln.inv, ln.prob).then_inc(S["x_ready"], 1)
                        yield
                        for l in range(LEVELS):
                            yield
                            dve.wait_ge(S["pl_done"], LEVELS * i + l + 1)
                            X.tensor_tensor(ln.prob, ln.prob, B[1][:, :], ALU.add).then_inc(S["p_new"], 1)
                            if l < LEVELS - 1:
                                dve.wait_ge(S["p_new"], LEVELS * i + l + 1)
                                X.transpose(ln.inv, ln.prob).then_inc(S["x_ready"], 1)
                            yield
                        dve.wait_ge(S["gs_exp"], i + 1)
                        for q in range(NC):
                            if 0 < q < NC - 1:
                                dve.wait_ge(S["s_new"], (NC - 1) * i + q)
                                chain(X.tensor_scalar(ln.Sg[:, :], ln.Sp[:, q % 2, :], ln.gs[:, q:q + 1], None, ALU.mult))
                            yield
                            dve.wait_ge(S["u_done"], NC * i + q + 1)
                            X.tensor_copy(ln.VU[UR[1], q, 1, :], B[1][UR[1], 0:CH]).then_inc(S["u_out1"], 1)
                            yield
                            if q < NC - 1:
                                dve.wait_ge(S["s_done"], (NC - 1) * i + q + 1)
                                if q == 0:
                                    X.tensor_scalar(ln.Sp[:, 1, :], B[2][:, 0:CH], ln.gs[:, 0:1], None, ALU.mult).then_inc(S["s_new"], 1)
                                else:
                                    X.scalar_tensor_tensor(out=ln.Sp[:, (q + 1) % 2, :], in0=B[2][:, 0:CH], scalar=ln.gs[:, q:q + 1],
                                                           in1=ln.Sg[:, :], op0=ALU.mult, op1=ALU.add).then_inc(S["s_new"], 1)
                            yield
                        yield

                    turns(dve, steps, mean, variance, output)

        def finish():
            with phase() as st:
                rstd = sbuf(st, "f_rstd", [P, T])
                out = sbuf(st, "f_out", [P, KD, T])
                ps_n = psum(st, "f_ss")
                s = norm_sems("f")
                stored = sem("stored")
                block = st.enter_context(nc.Block(no_gpsimd_drain=True))

                @block.scalar
                def _(act):
                    norm_act_rstd(act, s, KD, ps_n, rstd)

                @block.tensor
                def _(pe):
                    norm_pe(pe, s, KD, square_sum, ps_n)

                @block.vector
                def _(dve):
                    dve.wait_ge(s["rstd"], 1)
                    for k in range(KD):
                        nc.vector.scalar_tensor_tensor(out=out[:, k, :], in0=xk(k), scalar=V("norm_final", k), in1=rstd[:, :],
                                                       op0=ALU.mult, op1=ALU.mult).then_inc(s["hn"], 1)

                @block.sync
                def _(sp):
                    for k in range(KD):
                        sp.wait_ge(s["hn"], k + 1)
                        sp.dma_start(a["out"][:, k, :], out[:, k, :]).then_inc(stored, 16)
                    sp.wait_ge(stored, 16 * KD)

        attention()
        conv_glu("f0", 0, a["ffn_in0"], a["ffn_out0"], "r")
        rwkv()
        conv_glu("f1", 1, a["ffn_in1"], a["ffn_out1"], "f")
        finish()


def constant_matrices():
    c = np.zeros((P, NCON), np.float32)

    def put(name, m):
        c[:, CON[name]:CON[name] + m.shape[1]] = m
    i, j = np.arange(P)[:, None], np.arange(P)[None, :]
    put("ones", np.ones((P, P)))
    half = ROPE // 2
    first = j % ROPE < half
    put("rot", np.where(first & (i == j + half), -1.0, 0.0) + np.where(~first & (i == j - half), 1.0, 0.0))
    put("ident", np.eye(P))
    put("causal", np.where(j > i, NEG, 0.0))
    put("headsum", (i // RN == j // RN) * 1.0)
    put("headmean", (i // RN == j // RN) / RN)
    s, t = np.arange(P)[:, None] % CH, np.arange(CH)[None, :]
    put("incl", (s <= t) * 1.0)
    put("strict", (s < t) * 1.0)
    put("ident64", (s == t) * 1.0)
    put("levels", np.concatenate([(s // (2 * m) == t // (2 * m)) & (s // m % 2 == 0) & (t // m % 2 == 1)
                                  for m in (1, 2, 4, 8, 16, 32)], axis=1) * 1.0)
    put("reset", np.broadcast_to(np.arange(T)[None, :] % CH != 0, (P, T)) * 1.0)
    return c


def kernel(**inputs):
    import numpy as _np
    import concourse.bacc as _bacc
    from concourse import mybir as _mybir
    from concourse.bass_utils import run_bass_kernel_spmd as _run

    g = {k: _np.asarray(v) for k, v in inputs.items()}

    def tiles(w, m=P):
        k, n = w.shape
        return w.reshape(k // P, P, n // m, m).transpose(2, 1, 0, 3).reshape(n // m, P, k // P * m)

    def chan(v):
        return v.reshape(-1, P).T

    half = ROPE // 2
    inv_freq = (_np.float32(10000.0) ** (-_np.arange(half, dtype=_np.float32) / _np.float32(half))).astype(_np.float32)
    vec = _np.concatenate([chan(g["norm_mix"]), chan(g["norm_ffn"]), chan(g["norm_final"]), chan(g["mla_q_norm"]), chan(g["mla_kv_norm"]),
                           chan(g["rwkv_mix"]), chan(g["rwkv_w0"]), chan(g["rwkv_a0"]), chan(g["rwkv_k_k"]), chan(g["rwkv_k_a"]),
                           chan(g["rwkv_r_k"]), chan(g["rwkv_ln_w"]), chan(g["rwkv_ln_b"]), chan(g["ffn_conv_w"]), chan(g["ffn_conv_b"]),
                           _np.tile(inv_freq, P // half)[:, None], _np.full((P, 1), NORM_EPS, _np.float32),
                           _np.full((P, 1), GN_EPS, _np.float32)], axis=1)
    w_in = g["mla_w_in"][0]
    rope_cols = w_in[:, QL + KVL:]
    w_lat = tiles(_np.concatenate([w_in[:, :QL + KVL], rope_cols, rope_cols], axis=1))
    uq = g["mla_w_uq"][0].reshape(QL, HEADS, NOPE + ROPE)
    ukv = g["mla_w_ukv"][0].reshape(KVL, HEADS, NOPE + VDIM)
    w_pair = _np.concatenate([tiles(uq[:, :, :NOPE].reshape(QL, -1), 2 * NOPE), tiles(uq[:, :, NOPE:].reshape(QL, -1), 2 * ROPE),
                              tiles(ukv[:, :, :NOPE].reshape(KVL, -1), 2 * NOPE), tiles(ukv[:, :, NOPE:].reshape(KVL, -1), 2 * VDIM)], axis=2)
    lora_out = _np.zeros((KD, P, 4 * P), _np.float32)
    lora_out[:, :LW, 0:P] = g["rwkv_w2"][0].reshape(LW, KD, P).transpose(1, 0, 2)
    lora_out[:, :LW, P:2 * P] = g["rwkv_a2"][0].reshape(LW, KD, P).transpose(1, 0, 2)
    g2 = g["rwkv_g2"][0].reshape(LG, KD, P).transpose(1, 0, 2)
    lora_out[:, :, 2 * P:3 * P] = g2[:, :P]
    lora_out[:, :LG - P, 3 * P:4 * P] = g2[:, P:]
    arrays = {
        "x": g["x"][0].T.reshape(KD, P, T).transpose(1, 0, 2),
        "positions": _np.broadcast_to(g["positions"][0][None, :], (P, T)),
        "vec": vec, "con": constant_matrices(),
        "w_lat": w_lat, "w_pair": w_pair, "w_attn_out": tiles(g["mla_w_o"][0]),
        "lora_in": tiles(_np.concatenate([g["rwkv_w1"][0], g["rwkv_a1"][0], g["rwkv_g1"][0]], axis=1), 2 * LW + LG)[0],
        "w_rkv": _np.concatenate([tiles(g["rwkv_w_rkv"][0, n]) for n in (1, 0, 2)]),
        "lora_out": lora_out, "w_rwkv_out": tiles(g["rwkv_w_o"][0]),
    }
    for layer in range(2):
        w = g["ffn_w_in"][layer]
        arrays[f"ffn_in{layer}"] = _np.concatenate([tiles(w[:, :DFF]), tiles(w[:, DFF:])], axis=2)
        wo = g["ffn_w_out"][layer]
        arrays[f"ffn_out{layer}"] = _np.concatenate([tiles(wo[:DFF // 2]), tiles(wo[DFF // 2:])])
    arrays = {k: _np.ascontiguousarray(v) for k, v in arrays.items()}
    nc = _bacc.Bacc("TRN2", target_bir_lowering=False, num_devices=1)
    aps = {k: nc.dram_tensor(f"in_{k}", v.shape, _mybir.dt.from_np(v.dtype), kind="ExternalInput").ap() for k, v in arrays.items()}
    aps["out"] = nc.dram_tensor("out", (P, KD, T), _mybir.dt.float32, kind="ExternalOutput").ap()
    trunk(nc, aps)
    r = _run(nc, [{f"in_{k}": v for k, v in arrays.items()}], core_ids=[0])
    out = r.results[0]["out"]
    return _np.ascontiguousarray(out.transpose(2, 1, 0).reshape(1, T, D))
```
